# Optimizing a Trainium2 kernel written in Bass

```python
import math
import jax, jax.numpy as jnp
from jax import lax
import numpy as np

D_MODEL = 2048
BATCH = 1
SEQ = 256
DEPTH = 1
DEC_BATCH = 8
DEC_SEQ = 1
PAST_LEN = 2048
PAGE_SIZE = 128

RET_HEADS = 8
RET_DK = 128
RET_DV = 256
RET_QK = RET_HEADS * RET_DK
RET_V = RET_HEADS * RET_DV
RET_CHUNK = 128
ROPE_BASE = 10000.0
HG_HEADS = 8
HG_DK = 128
HG_DV = 128
HG_K = HG_HEADS * HG_DK
HG_V = HG_HEADS * HG_DV
HG_CHUNK = 16
D_FF = -(-8 * D_MODEL // (3 * 256)) * 256
EPS = 1e-6

IN_SIZES = [RET_QK, RET_QK, RET_V, RET_V, HG_K, HG_K, HG_V, HG_V, D_MODEL, D_MODEL]
IN_TOTAL = int(sum(IN_SIZES))
IN_OFFSETS = [int(o) for o in np.cumsum(IN_SIZES)[:-1]]

kernel_name = 'hybrid_retnet_hgrn2_step'

def rms_norm(x, g):
    xf = x.astype(jnp.float32)
    y = xf * lax.rsqrt(jnp.mean(xf * xf, axis=-1, keepdims=True) + EPS)
    return (y * g.astype(jnp.float32)).astype(x.dtype)

def head_rms(o):
    return o * lax.rsqrt(jnp.mean(o * o, axis=-1, keepdims=True) + EPS)

def to_heads(a, n_heads):
    B, T, _ = a.shape
    return a.reshape(B, T, n_heads, -1).transpose(0, 2, 1, 3).astype(jnp.float32)

def from_heads(a):
    B, H, T, d = a.shape
    return a.transpose(0, 2, 1, 3).reshape(B, T, H * d)

def rotary(x, pos):
    half = x.shape[-1] // 2
    inv_freq = ROPE_BASE ** (-jnp.arange(half, dtype=jnp.float32) / half)
    ang = pos.astype(jnp.float32)[:, None] * inv_freq[None, :]
    cos, sin = jnp.cos(ang), jnp.sin(ang)
    x1, x2 = x[..., :half], x[..., half:]
    return jnp.concatenate([x1 * cos - x2 * sin, x2 * cos + x1 * sin], axis=-1)

def split_chunks(a, n_chunks, c):
    B, H, T, d = a.shape
    return a.reshape(B, H, n_chunks, c, d).transpose(2, 0, 1, 3, 4)

def merge_chunks(a):
    N, B, H, C, d = a.shape
    return a.transpose(1, 2, 0, 3, 4).reshape(B, H, N * C, d)

def retention_chunkwise(q, k, v, s0, log_gamma):
    B, H, T, _ = q.shape
    C = math.gcd(T, RET_CHUNK)
    N = T // C
    idx = jnp.arange(C, dtype=jnp.float32)
    diff = idx[:, None] - idx[None, :]
    lg = log_gamma[:, None, None]
    decay_mask = jnp.where(diff >= 0, jnp.exp(jnp.maximum(diff, 0.0) * lg), 0.0)
    q_decay = jnp.exp((idx + 1.0)[None, :] * log_gamma[:, None])[..., None]
    k_decay = jnp.exp((C - 1.0 - idx)[None, :] * log_gamma[:, None])[..., None]
    chunk_decay = jnp.exp(C * log_gamma)[:, None, None]

    def step(S, blk):
        qc, kc, vc = blk
        scores = jnp.einsum('bhnd,bhmd->bhnm', qc, kc) * decay_mask
        o = (jnp.einsum('bhnm,bhme->bhne', scores, vc)
             + jnp.einsum('bhnd,bhde->bhne', qc * q_decay, S))
        S = chunk_decay * S + jnp.einsum('bhmd,bhme->bhde', kc * k_decay, vc)
        return S, o

    S, o = lax.scan(step, s0, (split_chunks(q, N, C), split_chunks(k, N, C), split_chunks(v, N, C)))
    return merge_chunks(o), S

def hgrn2_chunkwise(q, k, logf, v, s0):
    B, H, T, _ = q.shape
    C = math.gcd(T, HG_CHUNK)
    N = T // C
    pos = jnp.arange(C)
    causal = (pos[:, None] >= pos[None, :])[:, :, None]

    def step(S, blk):
        qc, kc, lfc, vc = blk
        b = jnp.cumsum(lfc, axis=-2)
        rel = jnp.where(causal, b[:, :, :, None, :] - b[:, :, None, :, :], -jnp.inf)
        A = jnp.einsum('bhnd,bhmd,bhnmd->bhnm', qc, kc, jnp.exp(rel))
        o = (jnp.einsum('bhnm,bhme->bhne', A, vc)
             + jnp.einsum('bhnd,bhde->bhne', qc * jnp.exp(b), S))
        b_last = b[:, :, -1:, :]
        S = (jnp.exp(b_last[:, :, 0, :])[..., None] * S
             + jnp.einsum('bhmd,bhme->bhde', kc * jnp.exp(b_last - b), vc))
        return S, o

    blocks = (split_chunks(q, N, C), split_chunks(k, N, C), split_chunks(logf, N, C), split_chunks(v, N, C))
    S, o = lax.scan(step, s0, blocks)
    return merge_chunks(o), S

def decoder_layer(x, pos, s_ret, s_hg, lb, w_in, w_ret_out, w_hgrn_out, w_out,
                  norm_mix, norm_ffn, hgrn_norm, w_ffn_in, w_ffn_out):
    h = rms_norm(x, norm_mix)
    proj = h @ w_in
    rq, rk, rv, rg, hq, hf, hi, hg, ga, gb = jnp.split(proj, IN_OFFSETS, axis=-1)

    log_gamma = jnp.log(1.0 - 2.0 ** (-5.0 - jnp.arange(RET_HEADS, dtype=jnp.float32)))
    q = rotary(to_heads(rq, RET_HEADS), pos)
    k = rotary(to_heads(rk, RET_HEADS), pos) * (RET_DK ** -0.5)
    v = to_heads(rv, RET_HEADS)
    o_r, s_ret_new = retention_chunkwise(q, k, v, s_ret.astype(jnp.float32), log_gamma)
    o_r = from_heads(head_rms(o_r)) * jax.nn.silu(rg.astype(jnp.float32))
    y_a = o_r.astype(x.dtype) @ w_ret_out

    lbh = lb.reshape(HG_HEADS, 1, HG_DK)
    z = to_heads(hf, HG_HEADS)
    logf = jnp.logaddexp(jnp.log(lbh), jnp.log1p(-lbh) + jax.nn.log_sigmoid(z))
    k_in = (1.0 - lbh) * jax.nn.sigmoid(-z)
    qh = jax.nn.silu(to_heads(hq, HG_HEADS))
    o_h, s_hg_new = hgrn2_chunkwise(qh, k_in, logf, to_heads(hi, HG_HEADS), s_hg.astype(jnp.float32))
    o_h = head_rms(o_h) * hgrn_norm.astype(jnp.float32)
    o_h = from_heads(o_h) * jax.nn.silu(hg.astype(jnp.float32))
    y_b = o_h.astype(x.dtype) @ w_hgrn_out

    merged = jax.nn.sigmoid(ga) * y_a + jax.nn.sigmoid(gb) * y_b
    x = x + merged @ w_out

    h2 = rms_norm(x, norm_ffn)
    g, u = jnp.split(h2 @ w_ffn_in, [D_FF], axis=-1)
    x = x + (jax.nn.silu(g) * u) @ w_ffn_out
    return x, s_ret_new, s_hg_new

def setup_inputs(seed: int = 0) -> dict:
    key = jax.random.key(seed)
    ks = jax.random.split(key, 16)
    f32 = jnp.float32
    nrm = lambda k, shape, s: (jax.random.normal(k, shape, f32) * s)
    return {
        'x_prompt': nrm(ks[0], (BATCH, SEQ, D_MODEL), 1.0),
        'x_sample': nrm(ks[1], (DEC_BATCH, DEC_SEQ, D_MODEL), 1.0),
        'state_ret': nrm(ks[2], (DEPTH, DEC_BATCH, RET_HEADS, RET_DK, RET_DV), 0.5),
        'state_hgrn': nrm(ks[3], (DEPTH, DEC_BATCH, HG_HEADS, HG_DK, HG_DV), 0.5),
        'w_in': nrm(ks[4], (DEPTH, D_MODEL, IN_TOTAL), D_MODEL ** -0.5),
        'w_ret_out': nrm(ks[5], (DEPTH, RET_V, D_MODEL), RET_V ** -0.5),
        'w_hgrn_out': nrm(ks[6], (DEPTH, HG_V, D_MODEL), HG_V ** -0.5),
        'w_out': nrm(ks[7], (DEPTH, D_MODEL, D_MODEL), D_MODEL ** -0.5),
        'norm_mix': 1.0 + nrm(ks[8], (DEPTH, D_MODEL), 0.02),
        'norm_ffn': 1.0 + nrm(ks[9], (DEPTH, D_MODEL), 0.02),
        'hgrn_norm': 1.0 + nrm(ks[10], (DEPTH, HG_DV), 0.02),
        'hgrn_lb_logits': nrm(ks[11], (DEPTH + 1, HG_K), 0.5),
        'w_ffn_in': nrm(ks[12], (DEPTH, D_MODEL, 2 * D_FF), D_MODEL ** -0.5),
        'w_ffn_out': nrm(ks[13], (DEPTH, D_FF, D_MODEL), D_FF ** -0.5),
        'norm_final': 1.0 + nrm(ks[14], (D_MODEL,), 0.02),
    }

def reference(x_prompt, x_sample, state_ret, state_hgrn, w_in, w_ret_out, w_hgrn_out, w_out,
              norm_mix, norm_ffn, hgrn_norm, hgrn_lb_logits, w_ffn_in, w_ffn_out, norm_final):
    lower_bounds = jnp.cumsum(jax.nn.softmax(hgrn_lb_logits.astype(jnp.float32), axis=0), axis=0)

    pos_prompt = jnp.arange(x_prompt.shape[1])
    pos_sample = PAST_LEN + jnp.arange(x_sample.shape[1])
    b_prompt = x_prompt.shape[0]

    xp, xs = x_prompt, x_sample
    ret_p, hg_p, ret_s, hg_s = [], [], [], []
    for l in range(DEPTH):
        lw = (w_in[l], w_ret_out[l], w_hgrn_out[l], w_out[l], norm_mix[l], norm_ffn[l],
              hgrn_norm[l], w_ffn_in[l], w_ffn_out[l])
        zr = jnp.zeros((b_prompt, RET_HEADS, RET_DK, RET_DV), jnp.float32)
        zh = jnp.zeros((b_prompt, HG_HEADS, HG_DK, HG_DV), jnp.float32)
        xp, sr, sh = decoder_layer(xp, pos_prompt, zr, zh, lower_bounds[l], *lw)
        ret_p.append(sr.astype(state_ret.dtype))
        hg_p.append(sh.astype(state_hgrn.dtype))
        xs, sr, sh = decoder_layer(xs, pos_sample, state_ret[l], state_hgrn[l], lower_bounds[l], *lw)
        ret_s.append(sr.astype(state_ret.dtype))
        hg_s.append(sh.astype(state_hgrn.dtype))

    y_prompt = rms_norm(xp, norm_final)
    y_sample = rms_norm(xs, norm_final)
    return (y_prompt, y_sample, jnp.stack(ret_p), jnp.stack(hg_p), jnp.stack(ret_s), jnp.stack(hg_s))


_drawn_inputs = setup_inputs


def setup_inputs(seed=0):
    import zlib

    import numpy as np

    out = dict(_drawn_inputs(seed))
    spreads = {}
    factors = {'norm_ffn': 4.061, 'hgrn_norm': 7.63, 'norm_final': 2.783}
    for name, (base, spread) in spreads.items():
        noise = np.random.default_rng([zlib.crc32(name.encode()), seed]).standard_normal(out[name].shape)
        drawn = base * np.exp(spread * noise) if base else spread * noise
        out[name] = __import__('jax').numpy.asarray(drawn.astype(out[name].dtype))
    for name, factor in factors.items():
        out[name] = (out[name] * factor).astype(out[name].dtype)
    return out
```

```python
from contextlib import ExitStack

import concourse.bass as bass
from concourse import mybir

ALU = mybir.AluOpType
ACT = mybir.ActivationFunctionType
F32 = mybir.dt.float32
F32R = mybir.dt.float32r
I32 = mybir.dt.int32

P = 128
D = 2048
KT = D // P
NP = 256
NS = 8
T = NP + NS
H = 8
DK = 128
RV = 256
HV = 128
FF = 5632
FT = FF // P
EPS = 1e-6
NLEV = 7

RQ, RK, RVO, RG = 0, 1024, 2048, 4096
HQ, HF, HI, HG = 6144, 7168, 8192, 9216
GA, GB = 10240, 12288

RING = 4
CK = 4
CHUNK = CK * 256

HEAD_CHUNKS, MERGE_CHUNKS, PAIR_CHUNKS, IN_CHUNKS, OUT_CHUNKS = 20, 14, 4, 8, 11
C_MERGE = H * HEAD_CHUNKS
C_WOUT = C_MERGE + 8 * MERGE_CHUNKS
C_FIN = C_WOUT + 8 * PAIR_CHUNKS
C_FOUT = C_FIN + (FT // 2) * IN_CHUNKS
C_END = C_FOUT + 8 * OUT_CHUNKS
U_MERGE = 2 * H
U_WOUT = U_MERGE + 8
U_FIN = U_WOUT + 4
U_FOUT = U_FIN + FT // 2
U_END = U_FOUT + 4

K_ROPE = 0
K_MASK = K_ROPE + 4 * T
K_LEVEL = K_MASK + H * NP
K_IDENT = K_LEVEL + NLEV * 64
K_ONES = K_IDENT + P
K_KDEC = K_ONES + P
K_GAMMA = K_KDEC + 2 * H
K_EYE8 = K_GAMMA + H
K_SIZE = K_EYE8 + 8
V_MIX, V_FFN, V_FINAL, V_HG, V_LB = 0, KT, 2 * KT, 3 * KT, 3 * KT + 1
V_SIZE = V_LB + 2 * H


def halves(ap, s):
    v = ap.rearrange("p (b two s) -> p b two s", two=2, s=s)
    return v[:, :, 0, :], v[:, :, 1, :]


def build(nc, consts, vectors, xT, w_in, w_ret, w_hg, w_out, w_fin, w_fout, s_ret, s_hg,
          yT, ret_p, hg_p, ret_s, hg_s):
    with ExitStack() as ctx:
        def sem(name):
            return ctx.enter_context(nc.semaphore(name))

        def alloc(stack, name, shape, dt=F32):
            return stack.enter_context(nc.sbuf_tensor(name, shape, dt))

        raw = [alloc(ctx, f"raw{i}", [P, CHUNK]) for i in range(RING)]
        hi = [alloc(ctx, f"hi{i}", [P, CHUNK], F32R) for i in range(RING)]
        lo = [alloc(ctx, f"lo{i}", [P, CHUNK], F32R) for i in range(RING)]
        ones = alloc(ctx, "ones", [P, P])
        vec = alloc(ctx, "vec", [P, V_SIZE])
        rms_std = alloc(ctx, "rms_std", [P, T])
        rms_inv = alloc(ctx, "rms_inv", [P, T])
        epsilon = alloc(ctx, "epsilon", [P, 1])

        early = ExitStack()
        h_hi = alloc(early, "h_hi", [P, KT, T], F32R)
        h_lo = alloc(early, "h_lo", [P, KT, T], F32R)
        ret_o = alloc(early, "ret_o", [P, 2 * H, T])
        hg_o = alloc(early, "hg_o", [P, H, T])

        heads = ExitStack()
        cst = alloc(heads, "cst", [P, K_SIZE])
        lb = alloc(heads, "lb", [P, H])
        omlb = alloc(heads, "omlb", [P, H])
        lb_tmp = alloc(heads, "lb_tmp", [P, 4, H])
        norm_tmp = ExitStack()
        x_in = alloc(norm_tmp, "x_in", [P, KT, T])
        x_sq = alloc(norm_tmp, "x_sq", [P, KT, T])
        norm_tmp.close()
        hq_sig = alloc(heads, "hq_sig", [P, T])
        z_sig = alloc(heads, "z_sig", [P, T])
        z_nsig = alloc(heads, "z_nsig", [P, T])
        forget = alloc(heads, "forget", [P, T])
        hkey = alloc(heads, "hkey", [P, T])
        hquery = alloc(heads, "hquery", [P, T])
        hval = alloc(heads, "hval", [P, T])
        hg_sig = alloc(heads, "hg_sig", [P, T])
        hg_gate = alloc(heads, "hg_gate", [P, T])
        qk_raw = alloc(heads, "qk_raw", [P, 2, T])
        qk_swap = alloc(heads, "qk_swap", [P, 2, T])
        qk = alloc(heads, "qk", [P, 2, T])
        vT = alloc(heads, "vT", [P, 2, T])
        rg_sig = alloc(heads, "rg_sig", [P, 2, T])
        rg_gate = alloc(heads, "rg_gate", [P, 2, T])
        hval_nat = alloc(heads, "hval_nat", [P, 2, HV])
        hval8 = alloc(heads, "hval8", [NS, HV])
        kbar_nat = alloc(heads, "kbar_nat", [P, 2, DK])
        hkey8 = alloc(heads, "hkey8", [NS, DK])
        v_nat = alloc(heads, "v_nat", [P, 2, RV])
        v8 = alloc(heads, "v8", [NS, RV])
        kd_nat = alloc(heads, "kd_nat", [P, 2, DK])
        k8 = alloc(heads, "k8", [NS, DK])
        hkey_masked = alloc(heads, "hkey_masked", [NS, NS, DK])
        k_masked = alloc(heads, "k_masked", [NS, NS, DK])
        hg_scores = alloc(heads, "hg_scores", [P, 3, P])
        ret_scores = alloc(heads, "ret_scores", [P, 384])
        oT = alloc(heads, "oT", [P, 2, T])
        ohT = alloc(heads, "ohT", [P, T])
        o_sq = alloc(heads, "o_sq", [P, 3, T])
        o_std = alloc(heads, "o_std", [P, 2, T])
        o_inv = alloc(heads, "o_inv", [P, 2, T])
        ret_stage = alloc(heads, "ret_stage", [P, RV])
        hg_stage = alloc(heads, "hg_stage", [P, HV])
        S_ret = alloc(heads, "S_ret", [P, NS, RV])
        S_hg = alloc(heads, "S_hg", [P, NS, HV])
        run_f = alloc(heads, "run_f", [P, NP])
        run_g = alloc(heads, "run_g", [P, NP])
        q_lev = [alloc(heads, f"q_lev{i}", [P, P]) for i in range(NLEV + 1)]
        k_lev = [alloc(heads, f"k_lev{i}", [P, NP]) for i in range(NLEV)]
        k_top = alloc(heads, "k_top", [P, P])
        kbar = alloc(heads, "kbar", [P, NP])
        qk_prod = alloc(heads, "qk_prod", [P, NP])
        heads.close()

        merge = ExitStack()
        ro_hi = alloc(merge, "ro_hi", [P, 2 * H, T], F32R)
        ro_lo = alloc(merge, "ro_lo", [P, 2 * H, T], F32R)
        ho_hi = alloc(merge, "ho_hi", [P, H, T], F32R)
        ho_lo = alloc(merge, "ho_lo", [P, H, T], F32R)
        m_hi = alloc(merge, "m_hi", [P, KT, T], F32R)
        m_lo = alloc(merge, "m_lo", [P, KT, T], F32R)
        ga_sig = alloc(merge, "ga_sig", [P, 2, T])
        gb_sig = alloc(merge, "gb_sig", [P, 2, T])
        m_a = alloc(merge, "m_a", [P, 2, T])
        m_b = alloc(merge, "m_b", [P, 2, T])
        merge.close()
        early.close()

        late = ExitStack()
        x2 = alloc(late, "x2", [P, KT, T])
        sq = alloc(late, "sq", [P, 2, T])
        sq_sum = alloc(late, "sq_sum", [P, 2, T])
        gate_sig = alloc(late, "gate_sig", [P, 2, T])
        gate_up = alloc(late, "gate_up", [P, 2, T])
        h2_f = alloc(late, "h2_f", [P, 4, T])
        h2_hi = alloc(late, "h2_hi", [P, KT, T], F32R)
        h2_lo = alloc(late, "h2_lo", [P, KT, T], F32R)
        hid_hi = alloc(late, "hid_hi", [P, FT, T], F32R)
        hid_lo = alloc(late, "hid_lo", [P, FT, T], F32R)
        late.close()

        c_rope = cst[:, K_ROPE:K_ROPE + 4 * T].rearrange("p (a c t) -> p a c t", a=2, c=2)
        c_ident = cst[:, K_IDENT:K_IDENT + P]
        c_level = cst[:, K_LEVEL:K_LEVEL + NLEV * 64].bitcast(I32).rearrange("p (l j) -> p l j", l=NLEV)
        c_kdec = cst[:, K_KDEC:K_KDEC + 2 * H].rearrange("p (b h) -> p b h", b=2)
        c_eye8 = cst[0:NS, K_EYE8:K_EYE8 + 8]

        def psum(name, banks):
            return ctx.enter_context(nc.psum_tensor(name, [P, banks, 512], F32))

        pA = psum("pA", 2)
        pB = psum("pB", 2)
        p4 = psum("p4", 1)
        p56 = psum("p56", 2)
        p7 = psum("p7", 1)
        pC = [p56[:, 0, 0:T], p56[:, 1, 0:T]]
        pD = [p4[:, 0, 0:T], p7[:, 0, 0:T]]
        pair_a = [pA[:, 0, 0:T], pA[:, 1, 0:T]]
        pair_b = [pB[:, 0, 0:T], pB[:, 1, 0:T]]

        raw_full = [sem(f"raw_full{i}") for i in range(RING)]
        hi_done = sem("hi_done")
        split_done = sem("split_done")
        chunk_used = sem("chunk_used")
        a_free, b_free = sem("a_free"), sem("b_free")
        p4_full, p4_free = sem("p4_full"), sem("p4_free")
        p56_full, p56_free = sem("p56_full"), sem("p56_free")
        p7_full, p7_free = sem("p7_full"), sem("p7_free")
        vec_in, x_in_full, cst_in = sem("vec_in"), [sem(f"x_in_full{i}") for i in range(4)], sem("cst_in")
        setup_done = sem("setup_done")
        x_squared = sem("x_squared")
        sumsq_done = sem("sumsq_done")
        std_done = sem("std_done")
        inv_done = sem("inv_done")
        h_scaled, h_hi_done, h_done = sem("h_scaled"), sem("h_hi_done"), sem("h_done")
        lb_max, lb_exp, lb_step = sem("lb_max"), sem("lb_exp"), sem("lb_step")
        hqf_sig = sem("hqf_sig")
        forget_done = sem("forget_done")
        hig_copied = sem("hig_copied")
        qk_copied = sem("qk_copied")
        products = sem("products")
        rotated = sem("rotated")
        score_step = sem("score_step")
        masked = sem("masked")
        rg_sig_done = sem("rg_sig_done")
        outputs_squared = sem("outputs_squared")
        o_inv_done = sem("o_inv_done")
        normed = sem("normed")
        state_in_ret, state_in_hg = sem("state_in_ret"), sem("state_in_hg")
        state_out = sem("state_out")
        prompt_out_ret, prompt_out_hg = sem("prompt_out_ret"), sem("prompt_out_hg")
        o_hi_done, o_split = sem("o_hi_done"), sem("o_split")
        ga_done, gb_done = sem("ga_done"), sem("gb_done")
        m_step = sem("m_step")
        m_hi_done, m_done = sem("m_hi_done"), sem("m_done")
        c_free, d_free = sem("c_free"), sem("d_free")
        x_again = sem("x_again")
        res_step = sem("res_step")
        h2_scaled, h2_hi_done, h2_done = sem("h2_scaled"), sem("h2_hi_done"), sem("h2_done")
        gate_sig_done = sem("gate_sig_done")
        hid_hi_done, hid_done = sem("hid_hi_done"), sem("hid_done")
        y_scaled, y_out = sem("y_scaled"), sem("y_out")

        def rows(w):
            return w.rearrange("(c k p) n -> c p k n", k=CK, p=P)

        v_in, v_ret, v_hg, v_out = rows(w_in), rows(w_ret), rows(w_hg), rows(w_out)
        v_fin, v_fout = rows(w_fin), rows(w_fout)

        v_tall = w_in.rearrange("(c k p) n -> c p k n", k=2 * CK, p=P)

        def tall(i, first, col):
            return v_tall[i // 2][:, :, first + 1024 * (i % 2):][:, :, bass.ds(col, 128)]

        block = ctx.enter_context(nc.Block())

        @block.sync
        def _(sp):
            sp.sem_inc(prompt_out_ret, 16)
            sp.sem_inc(prompt_out_hg, 16)
            sp.sem_inc(state_out, 32)
            sp.dma_start(vec[:], vectors).then_inc(vec_in, 16)
            for i in range(4):
                sp.dma_start(x_in[:, 4 * i:4 * i + 4, :], xT[:, 4 * i:4 * i + 4, :]).then_inc(x_in_full[i], 16)
            sp.dma_start(cst[:], consts).then_inc(cst_in, 16)

            def load(k, c, src):
                sp.wait_ge(split_done, c + 1)
                dst = raw[k % RING][:].rearrange("p (k n) -> p k n", n=src.shape[-1])
                sp.dma_start(dst, src).then_inc(raw_full[k % RING], 16)

            def columns(k, c, view, n, col, first=0):
                for i in range(n):
                    load(k + i, c + i, view[i][:, :, first:][:, :, bass.ds(col, 256)])

            with sp.Fori(0, H) as h:
                c = h * HEAD_CHUNKS
                for i in range(4):
                    load(i, c + i, tall(i, HQ, h * 128))
                for i in range(4):
                    load(4 + i, c + 4 + i, tall(i, HI, h * 128))
                sp.wait_ge(state_out, h * 32 + 32)
                sp.dma_start(S_hg[:], s_hg[:, bass.ds(h, 1), :, :].rearrange("b h d e -> d (b h) e")
                             ).then_inc(state_in_hg, 16)
                sp.dma_start(S_ret[:], s_ret[:, bass.ds(h, 1), :, :].rearrange("b h d e -> d (b h) e")
                             ).then_inc(state_in_ret, 16)
                for i in range(4):
                    load(8 + i, c + 8 + i, tall(i, RQ, sp.snap(h + 1) * 128 - 128))
                columns(12, c + 12, v_in, 4, h * 256, RVO)
                columns(16, c + 16, v_in, 4, h * 256, RG)
            with sp.Fori(0, 4) as it:
                for u in range(2):
                    c = it * (2 * MERGE_CHUNKS) + (C_MERGE + u * MERGE_CHUNKS)
                    k, col, first = u * MERGE_CHUNKS, sp.snap(it + 1) * 512 - 512, u * 256
                    columns(k, c, v_in, 4, col, first + GA)
                    columns(k + 4, c + 4, v_in, 4, col, first + GB)
                    columns(k + 8, c + 8, v_ret, 4, col, first)
                    columns(k + 12, c + 12, v_hg, 2, col, first)
            with sp.Fori(0, 4) as it:
                for u in range(2):
                    columns(4 * u, it * 8 + (C_WOUT + 4 * u), v_out, 4, it * 512, 256 * u)
                    if u == 0:
                        sp.wait_ge(chunk_used, C_WOUT + RING)
                        sp.dma_start(x2[:, bass.ds(it * 4, 4), :], xT[:, bass.ds(it * 4, 4), :]).then_inc(x_again, 16)
            with sp.Fori(0, FT // 2) as j:
                columns(0, j * 8 + C_FIN, v_fin, 4, j * 256)
                columns(4, j * 8 + (C_FIN + 4), v_fin, 4, j * 256, FF)
            with sp.Fori(0, 2) as it:
                for g in range(4):
                    columns(g * OUT_CHUNKS, it * (4 * OUT_CHUNKS) + (C_FOUT + g * OUT_CHUNKS), v_fout,
                            OUT_CHUNKS, it * 1024, g * 256)
            for i in range(4):
                sp.wait_ge(y_scaled, 4 * i + 4)
                sp.dma_start(yT[:, 4 * i:4 * i + 4, :], x2[:, 4 * i:4 * i + 4, :]).then_inc(y_out, 16)
            sp.wait_ge(y_out, 64)

        @block.scalar
        def _(act):
            copy = nc.scalar.copy
            fn = nc.scalar.activation

            def split_hi(k, c, n):
                for i in range(n):
                    s = (k + i) % RING
                    act.wait_ge(raw_full[s], 16 * ((c + i) // RING + 1) if isinstance(c, int)
                                else (c + i - s) * 4 + 16)
                    act.wait_ge(chunk_used, c + (i + 1))
                    copy(hi[s][:], raw[s][:]).then_inc(hi_done, 1)

            for i in range(4):
                act.wait_ge(x_in_full[i], 16)
                fn(x_sq[:, 4 * i:4 * i + 4, :], x_in[:, 4 * i:4 * i + 4, :], ACT.Square).then_inc(x_squared, 1)
            act.wait_ge(lb_max, 3)
            fn(lb_tmp[:, 1:3, :], lb_tmp[:, 1:3, :], ACT.Exp).then_inc(lb_exp, 1)
            split_hi(0, 0, RING)
            act.wait_ge(setup_done, 2)
            act.wait_ge(sumsq_done, 1)
            fn(rms_std[:], pA[:, 0, 0:T], ACT.Sqrt, bias=epsilon[:], scale=1.0 / D).then_inc(std_done, 1)
            for k in range(KT):
                act.wait_ge(h_scaled, k + 1)
                copy(h_hi[:, k, :], x_in[:, k, :]).then_inc(h_hi_done, 1)

            with act.Fori(0, H) as h:
                c = h * HEAD_CHUNKS
                split_hi(4, c + 4, 4)
                act.wait_ge(chunk_used, c + 8)
                fn(hq_sig[:], pair_a[0], ACT.Sigmoid).then_inc(hqf_sig, 1)
                fn(z_sig[:], pair_a[1], ACT.Sigmoid).then_inc(hqf_sig, 1)
                fn(z_nsig[:], pair_a[1], ACT.Sigmoid, scale=-1.0).then_inc(hqf_sig, 1)
                split_hi(8, c + 8, 4)
                act.wait_ge(chunk_used, c + 12)
                copy(hval[:], pair_b[0]).then_inc(hig_copied, 1)
                fn(hg_sig[:], pair_b[1], ACT.Sigmoid).then_inc(hig_copied, 1)
                split_hi(12, c + 12, 4)
                act.wait_ge(chunk_used, c + 16)
                copy(qk_raw[:], pA[:, :, 0:T]).then_inc(qk_copied, 1)
                copy(qk_swap[0:64], pA[64:128, :, 0:T]).then_inc(qk_copied, 1)
                copy(qk_swap[64:128], pA[0:64, :, 0:T]).then_inc(a_free, 1)
                act.wait_ge(p7_full, h * 5 + 1)
                copy(hval_nat[:], p7[:, 0, 0:256].rearrange("p (b e) -> p b e", b=2))
                copy(hval8[:], p7[0:NS, 0, 256:384]).then_inc(p7_free, 1)
                act.wait_ge(p4_full, h * 4 + 2)
                copy(kbar_nat[:], p4[:, 0, 0:256].rearrange("p (b e) -> p b e", b=2))
                copy(hkey8[:], p4[0:NS, 0, 256:384]).then_inc(p4_free, 1)
                split_hi(16, c + 16, 4)
                act.wait_ge(chunk_used, c + 20)
                copy(vT[:], pB[:, :, 0:T]).then_inc(b_free, 1)
                act.wait_ge(p56_full, h * 6 + 2)
                copy(v_nat[:], p56[:, 0, :].rearrange("p (b e) -> p b e", b=2))
                for b in range(2):
                    fn(kd_nat[:, b, :], p56[:, 1, b * 128:b * 128 + 128], ACT.Copy,
                       scale=c_kdec[:, b, bass.ds(h, 1)])
                copy(k8[:], p56[0:NS, 1, 256:384]).then_inc(p56_free, 1)
                act.wait_ge(p7_full, h * 5 + 2)
                copy(v8[:], p7[0:NS, 0, 0:RV]).then_inc(p7_free, 1)
                act.wait_ge(p7_full, h * 5 + 3)
                act.wait_ge(prompt_out_hg, h * 16 + 16)
                copy(ohT[:, 0:NP], p7[:, 0, 0:NP])
                copy(hg_stage[:], p7[:, 0, 256:384]).then_inc(p7_free, 1)
                act.wait_ge(p7_free, h * 5 + 4)
                act.dma_start(hg_p[bass.ds(h, 1)].rearrange("h d e -> (h d) e"), hg_stage[:]).then_inc(prompt_out_hg, 16)
                split_hi(20, c + 20, 4)
                act.wait_ge(chunk_used, c + 24)
                fn(rg_sig[:], p56[:, :, 0:T], ACT.Sigmoid).then_inc(rg_sig_done, 1)
                act.wait_ge(p4_full, h * 4 + 4)
                copy(oT[:, :, 0:NP], p4[:, 0, :].rearrange("p (e n) -> p e n", e=2)).then_inc(p4_free, 1)
                act.wait_ge(p7_full, h * 5 + 4)
                act.wait_ge(prompt_out_ret, h * 16 + 16)
                copy(ret_stage[:], p7[:, 0, 0:RV]).then_inc(p7_free, 1)
                act.wait_ge(p7_free, h * 5 + 5)
                act.dma_start(ret_p[bass.ds(h, 1)].rearrange("h d e -> (h d) e"), ret_stage[:]).then_inc(prompt_out_ret, 16)
                act.wait_ge(p7_full, h * 5 + 5)
                copy(oT[:, :, NP:T], p7[:, 0, 0:16].rearrange("p (e b) -> p e b", e=2))
                copy(ohT[:, NP:T], p7[:, 0, 16:24]).then_inc(p7_free, 1)
                act.wait_ge(p7_free, h * 5 + 6)
                act.dma_start(hg_s[:, bass.ds(h, 1), :, :].rearrange("b h d e -> d (b h) e"), S_hg[:]).then_inc(state_out, 16)
                act.dma_start(ret_s[:, bass.ds(h, 1), :, :].rearrange("b h d e -> d (b h) e"), S_ret[:]).then_inc(state_out, 16)
                fn(o_sq[:, 0:2, :], oT[:], ACT.Square).then_inc(outputs_squared, 1)
                fn(o_sq[:, 2, :], ohT[:], ACT.Square).then_inc(outputs_squared, 1)
                act.wait_ge(p56_full, h * 6 + 6)
                fn(o_std[:, 0, :], p56[:, 0, 0:T], ACT.Sqrt, bias=epsilon[:], scale=1.0 / RV)
                fn(o_std[:, 1, :], p56[:, 1, 0:T], ACT.Sqrt, bias=epsilon[:], scale=1.0 / HV).then_inc(p56_free, 1)

            act.wait_ge(state_out, 32 * (H + 1))
            act.wait_ge(prompt_out_ret, 16 * (H + 1))
            act.wait_ge(prompt_out_hg, 16 * (H + 1))
            act.wait_ge(normed, 4 * H + 4)
            for i in range(2):
                copy(ro_hi[:, 8 * i:8 * i + 8, :], ret_o[:, 8 * i:8 * i + 8, :]).then_inc(o_hi_done, 1)
            copy(ho_hi[:], hg_o[:]).then_inc(o_hi_done, 1)

            with act.Fori(0, 4) as it:
                for u in range(2):
                    c = it * (2 * MERGE_CHUNKS) + (C_MERGE + u * MERGE_CHUNKS + 4)
                    k = u * MERGE_CHUNKS + 4
                    split_hi(k, c, 4)
                    act.wait_ge(chunk_used, c + RING)
                    fn(ga_sig[:], pA[:, :, 0:T], ACT.Sigmoid).then_inc(a_free, 1)
                    split_hi(k + 4, c + 4, 4)
                    act.wait_ge(chunk_used, c + (4 + RING))
                    fn(gb_sig[:], pB[:, :, 0:T], ACT.Sigmoid).then_inc(b_free, 1)
                    split_hi(k + 8, c + 8, 4)
                    split_hi(k + 12, c + 12, 2)
                    act.wait_ge(m_step, it * 4 + (2 * u + 2))
                    copy(m_hi[:, bass.ds(it * 4 + 2 * u, 2), :], m_a[:]).then_inc(m_hi_done, 1)

            with act.Fori(0, 4) as it:
                split_hi(4, it * 8 + (C_WOUT + 4), 8)

            def rms_root(n):
                act.wait_ge(sumsq_done, n)
                fn(rms_std[:], p4[:, 0, 0:T], ACT.Sqrt, bias=epsilon[:], scale=1.0 / D).then_inc(std_done, 1)

            rms_root(2)
            for k in range(KT):
                act.wait_ge(h2_scaled, k + 1)
                copy(h2_hi[:, k, :], h2_f[:, k % 4, :]).then_inc(h2_hi_done, 1)

            with act.Fori(0, FT // 2) as j:
                split_hi(4, j * 8 + (C_FIN + 4), 4)
                act.wait_ge(chunk_used, j * 8 + (C_FIN + 4 + RING))
                fn(gate_sig[:], pA[:, :, 0:T], ACT.Sigmoid).then_inc(gate_sig_done, 1)
                split_hi(8, j * 8 + (C_FIN + 8), 4)
                act.wait_ge(b_free, j + (U_FIN + 2))
                copy(hid_hi[:, bass.ds(j * 2, 2), :], gate_up[:]).then_inc(hid_hi_done, 1)

            for c in range(C_FOUT + RING, C_END):
                split_hi(c, c, 1)
            rms_root(3)

        @block.gpsimd
        def _(pool):
            tt = nc.gpsimd.tensor_tensor
            pool.sem_inc(normed, 4)
            pool.wait_ge(h_done, KT)
            for i in range(NLEV):
                nc.gpsimd.memset(k_lev[i][:], 0.0).then_inc(products, 1)

            steps = 2 + 4 * NLEV + 5
            with pool.Fori(0, H) as h:
                count = [NLEV]

                def step(ins):
                    count[0] += 1
                    ins.then_inc(products, 1)
                    pool.wait_ge(products, h * steps + count[0])

                pool.wait_ge(forget_done, h * 2 + 2)
                pool.wait_ge(a_free, h * 2 + 2)
                tt(qk_prod[:], hquery[:, 0:NP], hkey[:, 0:NP], ALU.mult).then_inc(products, 1)
                nc.gpsimd.memset(run_g[:], 1.0).then_inc(products, 1)
                count[0] += 2
                step(nc.gpsimd.tensor_copy(run_f[:], forget[:, 0:NP]))
                for i in range(NLEV):
                    s = 1 << i
                    f0, f1 = halves(run_f[:], s)
                    g0, g1 = halves(run_g[:], s)
                    k0, _ = halves(hkey[:, 0:NP], s)
                    _, q1 = halves(hquery[:, 0:NP], s)
                    kl0, _ = halves(k_lev[i][:], s)
                    shape = [P, NP // (2 * s), s]
                    tt(q_lev[i][:].rearrange("p (b s) -> p b s", s=s), q1, f1, ALU.mult).then_inc(products, 1)
                    count[0] += 1
                    step(tt(kl0, k0, g0, ALU.mult))
                    step(tt(g0, g0, f1[:, :, s - 1:s].broadcast_to(shape), ALU.mult))
                    step(tt(f1, f1, f0[:, :, s - 1:s].broadcast_to(shape), ALU.mult))
                tt(q_lev[NLEV][:], hquery[:, P:NP], run_f[:, P:NP], ALU.mult).then_inc(products, 1)
                tt(k_top[:], hkey[:, 0:P], run_g[:, 0:P], ALU.mult).then_inc(products, 1)
                count[0] += 2
                step(tt(run_g[:, 0:P], run_g[:, 0:P], run_f[:, NP - 1:NP].broadcast_to([P, P]), ALU.mult))
                step(tt(kbar[:], hkey[:, 0:NP], run_g[:], ALU.mult))
                assert count[0] == NLEV + steps
                pool.wait_ge(qk_copied, h * 2 + 2)
                pool.wait_ge(a_free, h * 2 + 3)
                tt(qk[:], qk_raw[:], c_rope[:, :, 0, :], ALU.mult).then_inc(rotated, 1)
                tt(qk_swap[:], qk_swap[:], c_rope[:, :, 1, :], ALU.mult).then_inc(rotated, 1)
                pool.wait_ge(rotated, h * 3 + 2)
                tt(qk[:], qk[:], qk_swap[:], ALU.add).then_inc(rotated, 1)
                pool.wait_ge(o_inv_done, h + 1)
                pool.wait_ge(p56_free, h * 7 + 5)
                tt(oT[:], oT[:], o_inv[:, 0:1, :].broadcast_to([P, 2, T]), ALU.mult).then_inc(normed, 1)
                tt(ohT[:], ohT[:], o_inv[:, 1, :], ALU.mult).then_inc(normed, 1)
                pool.wait_ge(normed, h * 4 + 6)
                tt(ret_o[:, bass.ds(h * 2, 2), :], oT[:], rg_gate[:], ALU.mult).then_inc(normed, 1)
                tt(hg_o[:, bass.ds(h, 1), :].rearrange("p h t -> p (h t)"), ohT[:], hg_gate[:], ALU.mult).then_inc(normed, 1)

        @block.vector
        def _(dve):
            tt, ts = nc.vector.tensor_tensor, nc.vector.tensor_scalar
            stt = nc.vector.scalar_tensor_tensor

            def split_lo(k, c, n):
                for i in range(n):
                    s = (k + i) % RING
                    dve.wait_ge(hi_done, c + (i + 1))
                    tt(lo[s][:], raw[s][:], hi[s][:].bitcast(F32), ALU.subtract).then_inc(split_done, 1)

            dve.sem_inc(split_done, RING)
            nc.vector.memset(epsilon[:], EPS).then_inc(setup_done, 1)
            nc.vector.memset(ones[:], 1.0).then_inc(setup_done, 1)
            dve.wait_ge(vec_in, 16)
            logits = vec[:, V_LB:V_LB + 2 * H].rearrange("p (r h) -> p r h", r=2)
            tt(lb_tmp[:, 0, :], logits[:, 0, :], logits[:, 1, :], ALU.max).then_inc(lb_max, 1)
            dve.wait_ge(lb_max, 1)
            for r in range(2):
                tt(lb_tmp[:, 1 + r, :], logits[:, r, :], lb_tmp[:, 0, :], ALU.subtract).then_inc(lb_max, 1)
            split_lo(0, 0, RING)
            dve.wait_ge(lb_exp, 1)
            tt(lb_tmp[:, 3, :], lb_tmp[:, 1, :], lb_tmp[:, 2, :], ALU.add).then_inc(lb_step, 1)
            dve.wait_ge(lb_step, 1)
            nc.vector.reciprocal(lb_tmp[:, 0, :], lb_tmp[:, 3, :]).then_inc(lb_step, 1)
            dve.wait_ge(lb_step, 2)
            tt(lb[:], lb_tmp[:, 1, :], lb_tmp[:, 0, :], ALU.mult).then_inc(lb_step, 1)
            dve.wait_ge(lb_step, 3)
            ts(omlb[:], lb[:], -1.0, 1.0, ALU.mult, ALU.add).then_inc(lb_step, 1)
            dve.wait_ge(std_done, 1)
            nc.vector.reciprocal(rms_inv[:], rms_std[:]).then_inc(inv_done, 1)
            dve.wait_ge(inv_done, 1)
            for k in range(KT + 1):
                if k < KT:
                    stt(x_in[:, k, :], x_in[:, k, :], vec[:, V_MIX + k:V_MIX + k + 1], rms_inv[:],
                        ALU.mult, ALU.mult).then_inc(h_scaled, 1)
                if k:
                    dve.wait_ge(h_hi_done, k)
                    tt(h_lo[:, k - 1, :], x_in[:, k - 1, :], h_hi[:, k - 1, :].bitcast(F32),
                       ALU.subtract).then_inc(h_done, 1)
            dve.wait_ge(cst_in, 16)
            dve.wait_ge(lb_step, 4)

            def masked_keys(out, key):
                tt(out, key.rearrange("p (a d) -> p a d", a=1).broadcast_to([NS, NS, DK]),
                   c_eye8.rearrange("p (b a) -> p b a", a=1).broadcast_to([NS, NS, DK]),
                   ALU.mult).then_inc(masked, 1)

            with dve.Fori(0, H) as h:
                c = h * HEAD_CHUNKS
                split_lo(4, c + 4, 4)
                dve.wait_ge(hqf_sig, h * 3 + 3)
                ts(forget[:], z_sig[:], omlb[:, bass.ds(h, 1)], lb[:, bass.ds(h, 1)], ALU.mult, ALU.add
                   ).then_inc(forget_done, 1)
                ts(hkey[:], z_nsig[:], omlb[:, bass.ds(h, 1)], None, ALU.mult).then_inc(forget_done, 1)
                tt(hquery[:], pair_a[0], hq_sig[:], ALU.mult).then_inc(a_free, 1)
                split_lo(8, c + 8, 4)
                dve.wait_ge(normed, h * 4 + 4)
                dve.wait_ge(hig_copied, h * 2 + 2)
                stt(hg_gate[:], pair_b[1], vec[:, V_HG:V_HG + 1], hg_sig[:], ALU.mult, ALU.mult
                    ).then_inc(b_free, 1)
                split_lo(12, c + 12, 4)
                dve.wait_ge(p4_full, h * 4 + 1)
                tt(hg_scores[:, 0:3:2, :], p4[:, 0, 0:256].rearrange("p (b n) -> p b n", b=2),
                   c_ident.rearrange("p (a n) -> p a n", a=1).broadcast_to([P, 2, P]), ALU.mult
                   ).then_inc(score_step, 1)
                dve.wait_ge(p56_full, h * 6 + 1)
                dve.wait_ge(score_step, h + 1)
                nc.vector.tensor_copy(hg_scores[:, 1, :], p4[:, 0, 256:384]).then_inc(p4_free, 1)
                for i in range(NLEV):
                    s = 1 << i
                    dst = hg_scores[:, 0:3:2, :].rearrange("p k (b two s) -> p k b two s", two=2, s=s)[:, :, :, 1, :]
                    src = p56[:, :, 64 * i:64 * i + 64].rearrange("p k (b s) -> p k b s", s=s)
                    msk = c_level[:, i:i + 1, :].rearrange("p a (b s) -> p a b s", s=s).broadcast_to([P, 2, 64 // s, s])
                    if i:
                        nc.vector.drain()
                    last = nc.vector.copy_predicated(dst, msk, src)
                last.then_inc(p56_free, 1)
                dve.wait_ge(p4_free, h * 4 + 3)
                masked_keys(hkey_masked[:], hkey8[:])
                split_lo(16, c + 16, 4)
                dve.wait_ge(p4_full, h * 4 + 3)
                tt(ret_scores[:, 0:NP], p4[:, 0, 0:NP], cst[:, bass.ds(h * NP + K_MASK, NP)], ALU.mult)
                tt(ret_scores[:, NP:384], p4[:, 0, NP:384], cst[:, bass.ds(h * NP + K_MASK, P)], ALU.mult
                   ).then_inc(p4_free, 1)
                dve.wait_ge(p56_free, h * 7 + 3)
                masked_keys(k_masked[:], k8[:])
                dve.wait_ge(p56_full, h * 6 + 3)
                dve.wait_ge(state_in_hg, h * 16 + 16)
                for b in range(NS):
                    last = stt(S_hg[:, b, :], S_hg[:, b, :], forget[:, NP + b:NP + b + 1],
                               p56[:, b // 4, (b % 4) * 128:(b % 4) * 128 + 128], ALU.mult, ALU.add)
                last.then_inc(p56_free, 1)
                split_lo(20, c + 20, 4)
                dve.wait_ge(rg_sig_done, h + 1)
                tt(rg_gate[:], p56[:, :, 0:T], rg_sig[:], ALU.mult).then_inc(p56_free, 1)
                dve.wait_ge(state_in_ret, h * 16 + 16)
                for q in range(2):
                    dve.wait_ge(p56_full, h * 6 + (4 + q))
                    stt(S_ret[:, 4 * q:4 * q + 4, :].rearrange("p b e -> p (b e)"),
                        S_ret[:, 4 * q:4 * q + 4, :].rearrange("p b e -> p (b e)"),
                        cst[:, bass.ds(h + K_GAMMA, 1)], p56[:].rearrange("p k n -> p (k n)"),
                        ALU.mult, ALU.add).then_inc(p56_free, 1)
                dve.wait_ge(p56_free, h * 7 + 8)
                nc.vector.reciprocal(o_inv[:], o_std[:]).then_inc(o_inv_done, 1)

            for i in range(2):
                dve.wait_ge(o_hi_done, i + 1)
                tt(ro_lo[:, 8 * i:8 * i + 8, :], ret_o[:, 8 * i:8 * i + 8, :],
                   ro_hi[:, 8 * i:8 * i + 8, :].bitcast(F32), ALU.subtract).then_inc(o_split, 1)
            dve.wait_ge(o_hi_done, 3)
            tt(ho_lo[:], hg_o[:], ho_hi[:].bitcast(F32), ALU.subtract).then_inc(o_split, 1)

            with dve.Fori(0, 4) as it:
                for u in range(2):
                    c = it * (2 * MERGE_CHUNKS) + (C_MERGE + u * MERGE_CHUNKS + 4)
                    k = u * MERGE_CHUNKS + 4
                    split_lo(k, c, 12)
                    dve.wait_ge(chunk_used, c + (8 + RING))
                    dve.wait_ge(a_free, it * 2 + (U_MERGE + u + 2))
                    tt(m_a[:], p56[:, :, 0:T], ga_sig[:], ALU.mult).then_inc(c_free, 1)
                    split_lo(k + 12, c + 12, 2)
                    dve.wait_ge(chunk_used, c + (10 + RING))
                    dve.wait_ge(b_free, it * 2 + (U_MERGE + u + 2))
                    tt(m_b[:, 0, :], pD[0], gb_sig[:, 0, :], ALU.mult).then_inc(m_step, 1)
                    tt(m_b[:, 1, :], pD[1], gb_sig[:, 1, :], ALU.mult).then_inc(d_free, 1)
                    dve.wait_ge(d_free, it * 2 + (u + 2))
                    tt(m_a[:], m_a[:], m_b[:], ALU.add).then_inc(m_step, 1)
                    dve.wait_ge(m_hi_done, it * 2 + (u + 1))
                    tt(m_lo[:, bass.ds(it * 4 + 2 * u, 2), :], m_a[:],
                       m_hi[:, bass.ds(it * 4 + 2 * u, 2), :].bitcast(F32), ALU.subtract).then_inc(m_done, 1)

            nc.vector.memset(sq_sum[:], 0.0).then_inc(res_step, 1)

            def residual(x_pair, product, base, freed):
                tt(x_pair, product, x_pair, ALU.add).then_inc(freed, 1)

            def squares(x_pair, base):
                tt(sq[:], x_pair, x_pair, ALU.mult).then_inc(res_step, 1)
                dve.wait_ge(res_step, base + 1)
                tt(sq_sum[:], sq_sum[:], sq[:], ALU.add).then_inc(res_step, 1)

            with dve.Fori(0, 4) as it:
                for u in range(2):
                    split_lo(4 + 4 * u, it * 8 + (C_WOUT + 4 + 4 * u), 4)
                    dve.wait_ge(chunk_used, it * 8 + (C_WOUT + 4 * u + 4 + RING))
                    dve.wait_ge(x_again, it * 16 + 16)
                    x_pair = x2[:, bass.ds(it * 4 + 2 * u, 2), :]
                    psum_pair, free = ((pA, a_free), (pB, b_free))[u]
                    tt(x_pair, psum_pair[:, :, 0:T], x_pair, ALU.add).then_inc(free, 1)
                    dve.wait_ge(free, it + (U_WOUT + 2))
                    dve.wait_ge(res_step, it * 4 + (2 * u + 1))
                    squares(x_pair, it * 4 + (2 * u + 1))

            def rms_reciprocal(n):
                dve.wait_ge(std_done, n)
                nc.vector.reciprocal(rms_inv[:], rms_std[:]).then_inc(inv_done, 1)
                dve.wait_ge(inv_done, n)

            rms_reciprocal(2)
            for k in range(KT + 1):
                if k < KT:
                    stt(h2_f[:, k % 4, :], x2[:, k, :], vec[:, V_FFN + k:V_FFN + k + 1], rms_inv[:],
                        ALU.mult, ALU.mult).then_inc(h2_scaled, 1)
                if k:
                    dve.wait_ge(h2_hi_done, k)
                    tt(h2_lo[:, k - 1, :], h2_f[:, (k - 1) % 4, :], h2_hi[:, k - 1, :].bitcast(F32),
                       ALU.subtract).then_inc(h2_done, 1)
            nc.vector.memset(sq_sum[:], 0.0).then_inc(res_step, 1)

            with dve.Fori(0, FT // 2) as j:
                split_lo(4, j * 8 + (C_FIN + 4), 4)
                dve.wait_ge(gate_sig_done, j + 1)
                tt(gate_sig[:], pA[:, :, 0:T], gate_sig[:], ALU.mult).then_inc(a_free, 1)
                dve.wait_ge(a_free, j + (U_FIN + 2))
                split_lo(8, j * 8 + (C_FIN + 8), 4)
                dve.wait_ge(chunk_used, j * 8 + (C_FIN + 8 + RING))
                tt(gate_up[:], pB[:, :, 0:T], gate_sig[:], ALU.mult).then_inc(b_free, 1)
                dve.wait_ge(hid_hi_done, j + 1)
                tt(hid_lo[:, bass.ds(j * 2, 2), :], gate_up[:],
                   hid_hi[:, bass.ds(j * 2, 2), :].bitcast(F32), ALU.subtract).then_inc(hid_done, 1)

            for g in range(8):
                c0 = C_FOUT + g * OUT_CHUNKS + RING
                for c in range(c0, min(c0 + OUT_CHUNKS, C_END)):
                    split_lo(c, c, 1)
                dve.wait_ge(chunk_used, C_FOUT + (g + 1) * OUT_CHUNKS + RING)
                x_pair = x2[:, 2 * g:2 * g + 2, :]
                psum_pair, free = ((pA, a_free), (pB, b_free))[g % 2]
                tt(x_pair, psum_pair[:, :, 0:T], x_pair, ALU.add).then_inc(free, 1)
                dve.wait_ge(free, U_FOUT + g // 2 + 2)
                dve.wait_ge(res_step, 18 + 2 * g)
                squares(x_pair, 18 + 2 * g)
            rms_reciprocal(3)
            for k in range(KT):
                stt(x2[:, k, :], x2[:, k, :], vec[:, V_FINAL + k:V_FINAL + k + 1], rms_inv[:],
                    ALU.mult, ALU.mult).then_inc(y_scaled, 1)

        @block.tensor
        def _(pe):
            mm, transpose = nc.tensor.matmul, nc.tensor.transpose

            def use_chunk(k, c, i, n, outs, a_hi, a_lo, tall):
                s = k % RING
                pe.wait_ge(split_done, c + (RING + 1))
                for q in range(2 * CK):
                    t, kt = (i % 2, 2 * CK * (i // 2) + q) if tall else (q % 2, CK * i + q // 2)
                    w_hi, w_lo = hi[s][:, q * P:q * P + P], lo[s][:, q * P:q * P + P]
                    mm(outs[t], w_hi, a_hi[:, kt, :], start=(kt == 0), stop=False)
                    mm(outs[t], w_hi, a_lo[:, kt, :], start=False, stop=False)
                    last = mm(outs[t], w_lo, a_hi[:, kt, :], start=False, stop=(kt == CK * n - 1))
                last.then_inc(chunk_used, 1)

            def group(k, c, n, outs, a_hi, a_lo, tall=False, ready=None):
                for i in range(n):
                    if ready:
                        pe.wait_ge(ready, 2 * CK * (i // 2 + 1) if tall else CK * (i + 1))
                    use_chunk(k + i, c + i, i, n, outs, a_hi, a_lo, tall)

            pe.sem_inc(chunk_used, RING)
            for free in (a_free, b_free, p4_free, p56_free, p7_free, c_free, d_free):
                pe.sem_inc(free, 1)

            pe.wait_ge(setup_done, 2)
            for i in range(4):
                pe.wait_ge(x_squared, i + 1)
                for k in range(4 * i, 4 * i + 4):
                    last = mm(pA[:, 0, 0:T], ones[:], x_sq[:, k, :], start=(k == 0), stop=(k == KT - 1))
            last.then_inc(sumsq_done, 1)

            steps = 2 + 4 * NLEV + 5
            with pe.Fori(0, H) as h:
                c = h * HEAD_CHUNKS
                pe.wait_ge(a_free, h * 2 + 1)
                group(0, c, 4, pair_a, h_hi, h_lo, True, h_done)
                pe.wait_ge(b_free, h * 2 + 1)
                group(4, c + 4, 4, pair_b, h_hi, h_lo, True)
                pe.wait_ge(a_free, h * 2 + 2)
                group(8, c + 8, 4, pair_a, h_hi, h_lo, True)

                pe.wait_ge(p4_free, h * 4 + 1)
                pe.wait_ge(products, h * steps + (NLEV + steps))
                mm(p4[:, 0, 0:NP], ones[:], qk_prod[:], start=True, stop=True)
                mm(p4[:, 0, 256:384], k_top[:], q_lev[NLEV][:], start=True, stop=True).then_inc(p4_full, 1)
                pe.wait_ge(p56_free, h * 7 + 1)
                for i in range(NLEV):
                    for b in range(2):
                        last = mm(p56[:, b, 64 * i:64 * i + 64], k_lev[i][:, b * P:b * P + P],
                                  q_lev[i][:, 64 * b:64 * b + 64], start=True, stop=True)
                last.then_inc(p56_full, 1)
                pe.wait_ge(p7_free, h * 5 + 1)
                pe.wait_ge(hig_copied, h * 2 + 1)
                for b in range(2):
                    transpose(p7[:, 0, b * 128:b * 128 + 128], hval[:, b * P:b * P + P], c_ident)
                transpose(p7[0:NS, 0, 256:384], hval[:, NP:T], c_ident).then_inc(p7_full, 1)
                pe.wait_ge(p4_free, h * 4 + 2)
                for b in range(2):
                    transpose(p4[:, 0, b * 128:b * 128 + 128], kbar[:, b * P:b * P + P], c_ident)
                transpose(p4[0:NS, 0, 256:384], hkey[:, NP:T], c_ident).then_inc(p4_full, 1)

                pe.wait_ge(b_free, h * 2 + 2)
                group(12, c + 12, 4, pair_b, h_hi, h_lo)

                pe.wait_ge(p56_free, h * 7 + 2)
                pe.wait_ge(rotated, h * 3 + 3)
                pe.wait_ge(b_free, h * 2 + 3)
                for b in range(2):
                    transpose(p56[:, 1, b * 128:b * 128 + 128], qk[:, 1, b * P:b * P + P], c_ident)
                    for e in range(2):
                        transpose(p56[:, 0, b * 256 + e * 128:b * 256 + e * 128 + 128], vT[:, e, b * P:b * P + P], c_ident)
                transpose(p56[0:NS, 1, 256:384], qk[:, 1, NP:T], c_ident).then_inc(p56_full, 1)
                pe.wait_ge(p7_free, h * 5 + 2)
                transpose(p7[0:NS, 0, 0:128], vT[:, 0, NP:T], c_ident)
                transpose(p7[0:NS, 0, 128:256], vT[:, 1, NP:T], c_ident).then_inc(p7_full, 1)
                pe.wait_ge(p4_free, h * 4 + 3)
                mm(p4[:, 0, 0:NP], qk[:, 1, 0:P], qk[:, 0, 0:NP], start=True, stop=True)
                mm(p4[:, 0, NP:384], qk[:, 1, P:NP], qk[:, 0, P:NP], start=True, stop=True).then_inc(p4_full, 1)
                pe.wait_ge(p7_free, h * 5 + 3)
                mm(p7[:, 0, 0:NP], hval_nat[:, 0, :], hg_scores[:, 0:2, :], start=True, stop=False)
                mm(p7[:, 0, P:NP], hval_nat[:, 1, :], hg_scores[:, 2, :], start=False, stop=True)
                for b in range(2):
                    last = mm(p7[:, 0, 256:384], kbar_nat[:, b, :], hval_nat[:, b, :], start=(b == 0), stop=(b == 1))
                last.then_inc(p7_full, 1)
                pe.wait_ge(p56_free, h * 7 + 3)
                pe.wait_ge(masked, h * 2 + 1)
                for b in range(NS):
                    last = mm(p56[:, b // 4, (b % 4) * 128:(b % 4) * 128 + 128], hkey_masked[:, b, :], hval8[:],
                              start=True, stop=True)
                last.then_inc(p56_full, 1)

                pe.wait_ge(p56_free, h * 7 + 4)
                group(16, c + 16, 4, pC, h_hi, h_lo)

                pe.wait_ge(p4_free, h * 4 + 4)
                for e in range(2):
                    mm(p4[:, 0, e * 256:e * 256 + 256], v_nat[:, 0, e * 128:e * 128 + 128], ret_scores[:, 0:NP],
                       start=True, stop=False)
                    last = mm(p4[:, 0, e * 256 + P:e * 256 + NP], v_nat[:, 1, e * 128:e * 128 + 128],
                              ret_scores[:, NP:384], start=False, stop=True)
                last.then_inc(p4_full, 1)
                pe.wait_ge(p7_free, h * 5 + 4)
                for b in range(2):
                    last = mm(p7[:, 0, 0:RV], kd_nat[:, b, :], v_nat[:, b, :], start=(b == 0), stop=(b == 1))
                last.then_inc(p7_full, 1)
                pe.wait_ge(masked, h * 2 + 2)
                for q in range(2):
                    pe.wait_ge(p56_free, h * 7 + (5 + q))
                    for b in range(4):
                        last = mm(p56[:, b // 2, (b % 2) * 256:(b % 2) * 256 + 256], k_masked[:, 4 * q + b, :], v8[:],
                                  start=True, stop=True)
                    last.then_inc(p56_full, 1)
                pe.wait_ge(p56_free, h * 7 + 7)
                pe.wait_ge(p7_free, h * 5 + 5)
                for b in range(NS):
                    for e in range(2):
                        mm(p7[:, 0, e * 8 + b:e * 8 + b + 1], S_ret[:, b, e * 128:e * 128 + 128],
                           qk[:, 0, NP + b:NP + b + 1], start=True, stop=True)
                    last = mm(p7[:, 0, 16 + b:17 + b], S_hg[:, b, :], hquery[:, NP + b:NP + b + 1],
                              start=True, stop=True)
                last.then_inc(p7_full, 1)
                pe.wait_ge(outputs_squared, h * 2 + 2)
                for e in range(2):
                    mm(p56[:, 0, 0:T], ones[:], o_sq[:, e, :], start=(e == 0), stop=(e == 1))
                mm(p56[:, 1, 0:T], ones[:], o_sq[:, 2, :], start=True, stop=True).then_inc(p56_full, 1)

            pe.wait_ge(p4_free, 4 * H + 1)
            pe.wait_ge(p56_free, 7 * H + 1)
            pe.wait_ge(p7_free, 5 * H + 1)
            with pe.Fori(0, 4) as it:
                for u in range(2):
                    c = it * (2 * MERGE_CHUNKS) + (C_MERGE + u * MERGE_CHUNKS)
                    k = u * MERGE_CHUNKS
                    use = it * 2 + u
                    pe.wait_ge(a_free, use + (U_MERGE + 1))
                    group(k, c, 4, pair_a, h_hi, h_lo)
                    pe.wait_ge(b_free, use + (U_MERGE + 1))
                    group(k + 4, c + 4, 4, pair_b, h_hi, h_lo)
                    pe.wait_ge(o_split, 3)
                    pe.wait_ge(c_free, use + 1)
                    group(k + 8, c + 8, 4, pC, ro_hi, ro_lo)
                    pe.wait_ge(d_free, use + 1)
                    group(k + 12, c + 12, 2, pD, ho_hi, ho_lo)
            pe.wait_ge(m_done, 8)
            with pe.Fori(0, 4) as it:
                pe.wait_ge(a_free, it + (U_WOUT + 1))
                group(0, it * 8 + C_WOUT, 4, pair_a, m_hi, m_lo)
                pe.wait_ge(b_free, it + (U_WOUT + 1))
                group(4, it * 8 + (C_WOUT + 4), 4, pair_b, m_hi, m_lo)

            def total_squares():
                mm(p4[:, 0, 0:T], ones[:], sq_sum[:, 0, :], start=True, stop=False)
                mm(p4[:, 0, 0:T], ones[:], sq_sum[:, 1, :], start=False, stop=True).then_inc(sumsq_done, 1)

            pe.wait_ge(res_step, 1 + 16)
            total_squares()
            with pe.Fori(0, FT // 2) as j:
                pe.wait_ge(a_free, j + (U_FIN + 1))
                group(0, j * 8 + C_FIN, 4, pair_a, h2_hi, h2_lo, False, h2_done)
                pe.wait_ge(b_free, j + (U_FIN + 1))
                group(4, j * 8 + (C_FIN + 4), 4, pair_b, h2_hi, h2_lo)
            pe.wait_ge(hid_done, FT // 2)
            with pe.Fori(0, 2) as it:
                for g in range(4):
                    pair, free = ((pair_a, a_free), (pair_b, b_free))[g % 2]
                    pe.wait_ge(free, it * 2 + (U_FOUT + g // 2 + 1))
                    group(g * OUT_CHUNKS, it * (4 * OUT_CHUNKS) + (C_FOUT + g * OUT_CHUNKS), OUT_CHUNKS, pair,
                          hid_hi, hid_lo)
            pe.wait_ge(res_step, 18 + 16)
            total_squares()


def constants(np):
    half = DK // 2
    inv_freq = (np.float32(10000.0) ** (-np.arange(half, dtype=np.float32) / np.float32(half))).astype(np.float32)
    pos = np.concatenate([np.arange(NP), np.full(NS, 2048)]).astype(np.float32)
    ang = (pos[None, :] * inv_freq[:, None]).astype(np.float32).astype(np.float64)
    cos = np.concatenate([np.cos(ang), np.cos(ang)])
    sin = np.concatenate([-np.sin(ang), np.sin(ang)])
    scale = DK ** -0.5
    rope = np.stack([cos, sin, cos * scale, sin * scale], axis=1).reshape(P, 4 * T)
    gamma = 1.0 - 2.0 ** (-5.0 - np.arange(H, dtype=np.float64))
    m, n = np.arange(P)[:, None], np.arange(NP)[None, :]
    mask = np.where(n >= m, gamma[:, None, None] ** np.maximum(n - m, 0), 0.0)
    j = np.arange(64)[None, :]
    level = []
    for i in range(NLEV):
        s = 1 << i
        n_of = (j // s) * 2 * s + s + j % s
        level.append((m // (2 * s) == n_of // (2 * s)) & (m % (2 * s) < s))
    kdec = gamma[None, None, :] ** (NP - 1 - (np.arange(2)[None, :, None] * P + np.arange(P)[:, None, None]))
    c = np.zeros((P, K_SIZE), np.float32)
    c[:, K_ROPE:K_ROPE + 4 * T] = rope
    c[:, K_MASK:K_MASK + H * NP] = mask.transpose(1, 0, 2).reshape(P, H * NP)
    c[:, K_LEVEL:K_LEVEL + NLEV * 64] = np.concatenate(level, axis=1)
    c[:, K_IDENT:K_IDENT + P] = np.eye(P)
    c[:, K_ONES:K_ONES + P] = 1.0
    c[:, K_KDEC:K_KDEC + 2 * H] = kdec.reshape(P, 2 * H)
    c[:, K_GAMMA:K_GAMMA + H] = gamma[None, :]
    c[0:NS, K_EYE8:K_EYE8 + 8] = np.eye(NS)
    return c


def kernel(**inputs):
    import numpy as np
    import concourse.bacc as bacc
    from concourse.bass_utils import run_bass_kernel_spmd

    a = {k: np.asarray(v) for k, v in inputs.items()}

    def tiled(v):
        return v.reshape(-1, P).T

    tokens = np.concatenate([a["x_prompt"][0], a["x_sample"][:, 0]], axis=0)
    arrays = {
        "consts": constants(np),
        "vectors": np.ascontiguousarray(np.concatenate(
            [tiled(a["norm_mix"][0]), tiled(a["norm_ffn"][0]), tiled(a["norm_final"]), tiled(a["hgrn_norm"][0]),
             tiled(a["hgrn_lb_logits"].reshape(-1))], axis=1)),
        "xT": np.ascontiguousarray(tokens.T.reshape(KT, P, T).transpose(1, 0, 2)),
        "w_in": a["w_in"][0], "w_ret": a["w_ret_out"][0], "w_hg": a["w_hgrn_out"][0], "w_out": a["w_out"][0],
        "w_fin": a["w_ffn_in"][0], "w_fout": a["w_ffn_out"][0],
        "s_ret": a["state_ret"][0], "s_hg": a["state_hgrn"][0],
    }
    outs = {"yT": (P, KT, T), "ret_p": (H, DK, RV), "hg_p": (H, DK, HV),
            "ret_s": (NS, H, DK, RV), "hg_s": (NS, H, DK, HV)}
    nc = bacc.Bacc("TRN2", target_bir_lowering=False, num_devices=1)
    aps = [nc.dram_tensor(f"in_{n}", v.shape, F32, kind="ExternalInput").ap() for n, v in arrays.items()]
    aps += [nc.dram_tensor(f"out_{n}", s, F32, kind="ExternalOutput").ap() for n, s in outs.items()]
    build(nc, *aps)
    r = run_bass_kernel_spmd(nc, [{f"in_{n}": np.ascontiguousarray(v) for n, v in arrays.items()}], core_ids=[0])
    got = {n: r.results[0][f"out_{n}"] for n in outs}
    y = got["yT"].transpose(1, 0, 2).reshape(D, T).T
    return (np.ascontiguousarray(y[:NP])[None], np.ascontiguousarray(y[NP:])[:, None],
            got["ret_p"][None, None], got["hg_p"][None, None], got["ret_s"][None], got["hg_s"][None])
```

```python
from contextlib import ExitStack

import concourse.bass as bass
from concourse import mybir

ALU = mybir.AluOpType
ACT = mybir.ActivationFunctionType
F32 = mybir.dt.float32
F32R = mybir.dt.float32r
I32 = mybir.dt.int32

P = 128
D = 2048
KT = D // P
NP = 256
NS = 8
T = NP + NS
H = 8
DK = 128
RV = 256
HV = 128
FF = 5632
FT = FF // P
EPS = 1e-6
NLEV = 7

RQ, RK, RVO, RG = 0, 1024, 2048, 4096
HQ, HF, HI, HG = 6144, 7168, 8192, 9216
GA, GB = 10240, 12288

RING = 4
CK = 4
CHUNK = CK * 256

HEAD_CHUNKS, MERGE_CHUNKS, PAIR_CHUNKS, IN_CHUNKS, OUT_CHUNKS = 20, 14, 4, 8, 11
C_MERGE = H * HEAD_CHUNKS
C_WOUT = C_MERGE + 8 * MERGE_CHUNKS
C_FIN = C_WOUT + 8 * PAIR_CHUNKS
C_FOUT = C_FIN + (FT // 2) * IN_CHUNKS
C_END = C_FOUT + 8 * OUT_CHUNKS
A_MERGE, B_MERGE = 3 * H, 2 * H
A_WOUT, B_WOUT = A_MERGE + 8, B_MERGE + 8
A_FIN, B_FIN = A_WOUT + 4, B_WOUT + 4
A_FOUT, B_FOUT = A_FIN + FT // 2, B_FIN + FT // 2

R0, SC1, OR2, OH3, TO4, N4 = 0, 1, 2, 3, 4, 5
L0, TV1, OUT2, OUTH4, SS5, N56 = 0, 1, 2, 4, 5, 6
TK0, SF1, TI2, RD3, N7 = 0, 1, 2, 3, 4

K_ROPE = 0
K_MASK = K_ROPE + 4 * T
K_LEVEL = K_MASK + H * NP
K_IDENT = K_LEVEL + NLEV * 64
K_KDEC = K_IDENT + P
K_GAMMA = K_KDEC + 2 * H
K_EYE8 = K_GAMMA + H
K_ROW8 = K_EYE8 + NS * NS
K_SIZE = K_ROW8 + NS
V_MIX, V_FFN, V_FINAL, V_HG, V_LB = 0, KT, 2 * KT, 3 * KT, 3 * KT + 1
V_SIZE = V_LB + 2 * H


def halves(ap, s):
    v = ap.rearrange("p (b two s) -> p b two s", two=2, s=s)
    return v[:, :, 0, :], v[:, :, 1, :]


def build(nc, consts, vectors, xT, w_in, w_ret, w_hg, w_out, w_fin, w_fout, s_ret, s_hg,
          yT, ret_p, hg_p, ret_s, hg_s):
    with ExitStack() as ctx:
        def sem(name):
            return ctx.enter_context(nc.semaphore(name))

        def alloc(stack, name, shape, dt=F32):
            return stack.enter_context(nc.sbuf_tensor(name, shape, dt))

        raw = [alloc(ctx, f"raw{i}", [P, CHUNK]) for i in range(RING)]
        hi = [alloc(ctx, f"hi{i}", [P, CHUNK], F32R) for i in range(RING)]
        lo = [alloc(ctx, f"lo{i}", [P, CHUNK], F32R) for i in range(RING)]
        ones = alloc(ctx, "ones", [P, P])
        vec = alloc(ctx, "vec", [P, V_SIZE])
        rms_std = alloc(ctx, "rms_std", [P, T])
        rms_inv = alloc(ctx, "rms_inv", [P, T])
        epsilon = alloc(ctx, "epsilon", [P, 1])
        table_load = alloc(ctx, "table_load", [P, 1])

        early = ExitStack()
        h_hi = alloc(early, "h_hi", [P, KT, T], F32R)
        h_lo = alloc(early, "h_lo", [P, KT, T], F32R)
        ret_o = alloc(early, "ret_o", [P, 2 * H, T])
        hg_o = alloc(early, "hg_o", [P, H, T])

        heads = ExitStack()
        cst = alloc(heads, "cst", [P, K_SIZE])
        lb = alloc(heads, "lb", [P, H])
        omlb = alloc(heads, "omlb", [P, H])
        lb_tmp = alloc(heads, "lb_tmp", [P, 4, H])
        norm_tmp = ExitStack()
        x_in = alloc(norm_tmp, "x_in", [P, KT, T])
        x_sq = alloc(norm_tmp, "x_sq", [P, KT, T])
        norm_tmp.close()
        hq_sig = alloc(heads, "hq_sig", [P, T])
        z_sig = alloc(heads, "z_sig", [P, T])
        z_nsig = alloc(heads, "z_nsig", [P, T])
        forget = alloc(heads, "forget", [P, T])
        hkey = alloc(heads, "hkey", [P, T])
        hquery = alloc(heads, "hquery", [P, T])
        hval = alloc(heads, "hval", [P, T])
        hg_sig = alloc(heads, "hg_sig", [P, T])
        hg_gate = alloc(heads, "hg_gate", [P, T])
        qk_raw = alloc(heads, "qk_raw", [P, 2, T])
        qk_swap = alloc(heads, "qk_swap", [P, 2, T])
        qk = alloc(heads, "qk", [P, 2, T])
        vT = alloc(heads, "vT", [P, 2, T])
        rg_sig = alloc(heads, "rg_sig", [P, 2, T])
        rg_gate = alloc(heads, "rg_gate", [P, 2, T])
        hval_nat = alloc(heads, "hval_nat", [P, 2, HV])
        hv_rows = alloc(heads, "hv_rows", [4 * NS, HV], F32R)
        kbar_nat = alloc(heads, "kbar_nat", [P, 2, DK])
        v_nat = alloc(heads, "v_nat", [P, 2, RV])
        v_rows = alloc(heads, "v_rows", [4 * NS, RV], F32R)
        kd_nat = alloc(heads, "kd_nat", [P, 2, DK])
        k_parts = alloc(heads, "k_parts", [P, 4, NS], F32R)
        hk_parts = alloc(heads, "hk_parts", [P, 4, NS], F32R)
        v_parts = alloc(heads, "v_parts", [P, 2, 4, NS], F32R)
        hv_parts = alloc(heads, "hv_parts", [P, 4, NS], F32R)
        k_only = alloc(heads, "k_only", [4 * NS, NS, DK], F32R)
        hk_only = alloc(heads, "hk_only", [4 * NS, NS, DK], F32R)
        q_only = alloc(heads, "q_only", [P, NS, NS])
        hq_only = alloc(heads, "hq_only", [P, NS, NS])
        o8 = alloc(heads, "o8", [NS, 384])
        hg_scores = alloc(heads, "hg_scores", [P, 3, P])
        ret_scores = alloc(heads, "ret_scores", [P, 384])
        oT = alloc(heads, "oT", [P, 2, T])
        ohT = alloc(heads, "ohT", [P, T])
        o_sq = alloc(heads, "o_sq", [P, 3, T])
        o_std = alloc(heads, "o_std", [P, 2, T])
        o_inv = alloc(heads, "o_inv", [P, 2, T])
        ret_stage = alloc(heads, "ret_stage", [P, RV])
        hg_stage = alloc(heads, "hg_stage", [P, HV])
        S_ret = alloc(heads, "S_ret", [P, NS, RV])
        S_hg = alloc(heads, "S_hg", [P, NS, HV])
        run_f = alloc(heads, "run_f", [P, NP])
        run_g = alloc(heads, "run_g", [P, NP])
        q_lev = [alloc(heads, f"q_lev{i}", [P, P]) for i in range(NLEV + 1)]
        k_lev = [alloc(heads, f"k_lev{i}", [P, NP]) for i in range(NLEV)]
        k_top = alloc(heads, "k_top", [P, P])
        kbar = alloc(heads, "kbar", [P, NP])
        qk_prod = alloc(heads, "qk_prod", [P, NP])
        heads.close()

        merge = ExitStack()
        ro_hi = alloc(merge, "ro_hi", [P, 2 * H, T], F32R)
        ro_lo = alloc(merge, "ro_lo", [P, 2 * H, T], F32R)
        ho_hi = alloc(merge, "ho_hi", [P, H, T], F32R)
        ho_lo = alloc(merge, "ho_lo", [P, H, T], F32R)
        m_hi = alloc(merge, "m_hi", [P, KT, T], F32R)
        m_lo = alloc(merge, "m_lo", [P, KT, T], F32R)
        ga_sig = alloc(merge, "ga_sig", [P, 2, T])
        gb_sig = alloc(merge, "gb_sig", [P, 2, T])
        m_a = alloc(merge, "m_a", [P, 2, T])
        m_b = alloc(merge, "m_b", [P, 2, T])
        merge.close()
        early.close()

        late = ExitStack()
        x2 = alloc(late, "x2", [P, KT, T])
        sq = alloc(late, "sq", [P, 2, T])
        sq_sum = alloc(late, "sq_sum", [P, 2, T])
        gate_sig = alloc(late, "gate_sig", [P, 2, T])
        gate = alloc(late, "gate", [P, 2, T])
        gate_up = alloc(late, "gate_up", [P, 2, T])
        h2_f = alloc(late, "h2_f", [P, 2, T])
        h2_hi = alloc(late, "h2_hi", [P, KT, T], F32R)
        h2_lo = alloc(late, "h2_lo", [P, KT, T], F32R)
        hid_hi = alloc(late, "hid_hi", [P, FT, T], F32R)
        hid_lo = alloc(late, "hid_lo", [P, FT, T], F32R)
        late.close()

        c_rope = cst[:, K_ROPE:K_ROPE + 4 * T].rearrange("p (a c t) -> p a c t", a=2, c=2)
        c_ident = cst[:, K_IDENT:K_IDENT + P]
        c_level = cst[:, K_LEVEL:K_LEVEL + NLEV * 64].bitcast(I32).rearrange("p (l j) -> p l j", l=NLEV)
        c_kdec = cst[:, K_KDEC:K_KDEC + 2 * H].rearrange("p (b h) -> p b h", b=2)
        c_eye8 = cst[:, K_EYE8:K_EYE8 + NS * NS].rearrange("p (b j) -> p b j", b=NS)
        c_row8 = cst[0:4 * NS, K_ROW8:K_ROW8 + NS]

        def psum(name, banks):
            return ctx.enter_context(nc.psum_tensor(name, [P, banks, 512], F32))

        pA = psum("pA", 2)
        pB = psum("pB", 2)
        p4 = psum("p4", 1)
        p56 = psum("p56", 2)
        p7 = psum("p7", 1)
        pC = [p56[:, 0, 0:T], p56[:, 1, 0:T]]
        pD = [p4[:, 0, 0:T], p7[:, 0, 0:T]]
        pair_a = [pA[:, 0, 0:T], pA[:, 1, 0:T]]
        pair_b = [pB[:, 0, 0:T], pB[:, 1, 0:T]]

        raw_full = [sem(f"raw_full{i}") for i in range(RING)]
        hi_done = sem("hi_done")
        split_done = sem("split_done")
        chunk_used = sem("chunk_used")
        a_free, b_free = sem("a_free"), sem("b_free")
        p4_full, p4_free = sem("p4_full"), sem("p4_free")
        p56_full, p56_free = sem("p56_full"), sem("p56_free")
        p7_full, p7_free = sem("p7_full"), sem("p7_free")
        vec_in, x_in_full, cst_in = sem("vec_in"), [sem(f"x_in_full{i}") for i in range(4)], sem("cst_in")
        setup_done = sem("setup_done")
        x_squared = sem("x_squared")
        sumsq_done = sem("sumsq_done")
        std_done = sem("std_done")
        inv_done = sem("inv_done")
        h_hi_done, h_done = sem("h_hi_done"), sem("h_done")
        x_gain = sem("x_gain")
        squares_added = sem("squares_added")
        x_scaled = [sem("x_scaled_even"), sem("x_scaled_odd")]
        lb_max, lb_exp, lb_step = sem("lb_max"), sem("lb_exp"), sem("lb_step")
        hqf_sig = sem("hqf_sig")
        forget_done = sem("forget_done")
        qk_copied = sem("qk_copied")
        rotated = sem("rotated")
        hig_copied = sem("hig_copied")
        products = sem("products")
        parts_done = sem("parts_done")
        masked = sem("masked")
        keys_copied = sem("keys_copied")
        score_step = sem("score_step")
        rg_sig_done = sem("rg_sig_done")
        outputs_squared = sem("outputs_squared")
        squares_summed = sem("squares_summed")
        o_inv_done = sem("o_inv_done")
        normed = sem("normed")
        state_in_ret, state_in_hg = sem("state_in_ret"), sem("state_in_hg")
        state_out = sem("state_out")
        prompt_out_ret, prompt_out_hg = sem("prompt_out_ret"), sem("prompt_out_hg")
        o_hi_done, o_split = sem("o_hi_done"), sem("o_split")
        ga_done, gb_done = sem("ga_done"), sem("gb_done")
        m_step = sem("m_step")
        m_hi_done, m_done = sem("m_hi_done"), sem("m_done")
        c_free, d_free = sem("c_free"), sem("d_free")
        x_again = sem("x_again")
        res_step = sem("res_step")
        h2_scaled, h2_hi_done, h2_done = sem("h2_scaled"), sem("h2_hi_done"), sem("h2_done")
        gate_sig_done = sem("gate_sig_done")
        gate_step = sem("gate_step")
        hid_hi_done, hid_done = sem("hid_hi_done"), sem("hid_done")
        y_gain = sem("y_gain")
        y_scaled, y_out = [sem("y_scaled_dve"), sem("y_scaled_pool")], sem("y_out")

        def rows(w):
            return w.rearrange("(c k p) n -> c p k n", k=CK, p=P)

        v_in, v_ret, v_hg, v_out = rows(w_in), rows(w_ret), rows(w_hg), rows(w_out)
        v_fin, v_fout = rows(w_fin), rows(w_fout)

        v_tall = w_in.rearrange("(c k p) n -> c p k n", k=2 * CK, p=P)

        def tall(i, first, col):
            return v_tall[i // 2][:, :, first + 1024 * (i % 2):][:, :, bass.ds(col, 128)]

        block = ctx.enter_context(nc.Block())

        @block.sync
        def _(sp):
            sp.sem_inc(prompt_out_ret, 16)
            sp.sem_inc(prompt_out_hg, 16)
            sp.sem_inc(state_out, 32)
            sp.dma_start(vec[:], vectors).then_inc(vec_in, 16)
            for i in range(4):
                sp.dma_start(x_in[:, 4 * i:4 * i + 4, :], xT[:, 4 * i:4 * i + 4, :]).then_inc(x_in_full[i], 16)

            def load(k, c, src):
                sp.wait_ge(split_done, c + 1)
                dst = raw[k % RING][:].rearrange("p (k n) -> p k n", n=src.shape[-1])
                sp.dma_start(dst, src).then_inc(raw_full[k % RING], 16)

            def columns(k, c, view, n, col, first=0):
                for i in range(n):
                    load(k + i, c + i, view[i][:, :, first:][:, :, bass.ds(col, 256)])

            def head(h, first=False):
                c = h * HEAD_CHUNKS
                for i in range(4):
                    load(i, c + i, tall(i, HQ, h * 128))
                if first:
                    sp.dma_start(cst[:], consts).then_inc(cst_in, 16)
                for i in range(4):
                    load(4 + i, c + 4 + i, tall(i, RQ, h * 128 if first else sp.snap(h + 1) * 128 - 128))
                columns(8, c + 8, v_in, 4, h * 256, RVO)
                for i in range(4):
                    load(12 + i, c + 12 + i, tall(i, HI, h * 128))
                    if i == 1:
                        sp.wait_ge(state_out, h * 32 + 32)
                        sp.dma_start(S_ret[:], s_ret[:, bass.ds(h, 1), :, :].rearrange("b h d e -> d (b h) e")
                                     ).then_inc(state_in_ret, 16)
                        sp.dma_start(S_hg[:], s_hg[:, bass.ds(h, 1), :, :].rearrange("b h d e -> d (b h) e")
                                     ).then_inc(state_in_hg, 16)
                columns(16, c + 16, v_in, 4, h * 256, RG)

            head(0, first=True)
            with sp.Fori(1, H) as h:
                head(h)
            with sp.Fori(0, 4) as it:
                for u in range(2):
                    c = it * (2 * MERGE_CHUNKS) + (C_MERGE + u * MERGE_CHUNKS)
                    k, col, first = u * MERGE_CHUNKS, sp.snap(it + 1) * 512 - 512, u * 256
                    columns(k, c, v_in, 4, col, first + GA)
                    columns(k + 4, c + 4, v_in, 4, col, first + GB)
                    columns(k + 8, c + 8, v_ret, 4, col, first)
                    columns(k + 12, c + 12, v_hg, 2, col, first)
            with sp.Fori(0, 4) as it:
                for u in range(2):
                    columns(4 * u, it * 8 + (C_WOUT + 4 * u), v_out, 4, it * 512, 256 * u)
                    if u == 0:
                        sp.wait_ge(chunk_used, C_WOUT + RING)
                        sp.dma_start(x2[:, bass.ds(it * 4, 4), :], xT[:, bass.ds(it * 4, 4), :]).then_inc(x_again, 16)
            with sp.Fori(0, FT // 2) as j:
                columns(0, j * 8 + C_FIN, v_fin, 4, j * 256)
                columns(4, j * 8 + (C_FIN + 4), v_fin, 4, j * 256, FF)
            with sp.Fori(0, 2) as it:
                for g in range(4):
                    columns(g * OUT_CHUNKS, it * (4 * OUT_CHUNKS) + (C_FOUT + g * OUT_CHUNKS), v_fout,
                            OUT_CHUNKS, it * 1024, g * 256)
            for engine, n, k in ((0, 2, 0), (1, 1, 10), (0, 4, 4), (1, 2, 12), (0, 5, 8), (1, 3, 14)):
                sp.wait_ge(y_scaled[engine], n)
                size = 4 if engine == 0 and n < 5 else 2
                sp.dma_start(yT[:, k:k + size, :], x2[:, k:k + size, :]).then_inc(y_out, 16)
            sp.wait_ge(y_out, 96)

        @block.scalar
        def _(act):
            copy = nc.scalar.copy
            fn = nc.scalar.activation

            def split_hi(k, c, n):
                for i in range(n):
                    s = (k + i) % RING
                    act.wait_ge(raw_full[s], 16 * ((c + i) // RING + 1) if isinstance(c, int)
                                else (c + i - s) * 4 + 16)
                    act.wait_ge(chunk_used, c + (i + 1))
                    copy(hi[s][:], raw[s][:]).then_inc(hi_done, 1)

            act.wait_ge(lb_max, 3)
            fn(lb_tmp[:, 1:3, :], lb_tmp[:, 1:3, :], ACT.Exp).then_inc(lb_exp, 1)
            act.wait_ge(setup_done, 2)
            fn(table_load[:], epsilon[:], ACT.Sqrt)
            for i in range(4):
                act.wait_ge(x_in_full[i], 16)
                fn(x_sq[:, 4 * i:4 * i + 4, :], x_in[:, 4 * i:4 * i + 4, :], ACT.Square).then_inc(x_squared, 1)
            split_hi(0, 0, 1)
            act.wait_ge(sumsq_done, 1)
            fn(rms_std[:], pA[:, 0, 0:T], ACT.Sqrt, bias=epsilon[:], scale=1.0 / D).then_inc(std_done, 1)
            split_hi(1, 1, 2)
            for k in range(KT):
                act.wait_ge(x_scaled[k % 2], k // 2 + 1)
                copy(h_hi[:, k, :], x_in[:, k, :]).then_inc(h_hi_done, 1)
                if k == 8:
                    split_hi(3, 3, 1)

            def tail(i, h):
                if i == 0:
                    act.wait_ge(p4_full, h * N4 + (TO4 + 1 - N4))
                    copy(oT[:, :, NP:T], p4[:, 0, 0:16].rearrange("p (e b) -> p e b", e=2))
                    copy(ohT[:, NP:T], p4[:, 0, 16:24]).then_inc(p4_free, 1)
                    act.wait_ge(p4_free, h * N4 + (TO4 + 2 - N4))
                    fn(o_sq[:, 0:2, :], oT[:], ACT.Square).then_inc(outputs_squared, 1)
                    fn(o_sq[:, 2, :], ohT[:], ACT.Square).then_inc(outputs_squared, 1)
                elif i == 1:
                    act.wait_ge(p56_full, h * N56 + (SS5 + 1 - N56))
                    fn(o_std[:, 0, :], p56[:, 0, 0:T], ACT.Sqrt, bias=epsilon[:], scale=1.0 / RV)
                    fn(o_std[:, 1, :], p56[:, 1, 0:T], ACT.Sqrt, bias=epsilon[:], scale=1.0 / HV
                       ).then_inc(p56_free, 1)

            def head(h, first=False):
                c = h * HEAD_CHUNKS
                for i in range(HEAD_CHUNKS):
                    split_hi(4 + i, c + (4 + i), 1)
                    if not first:
                        tail(i, h)
                    if i == 3:
                        act.wait_ge(chunk_used, c + (4 + RING))
                        fn(hq_sig[:], pair_a[0], ACT.Sigmoid).then_inc(hqf_sig, 1)
                        fn(z_sig[:], pair_a[1], ACT.Sigmoid).then_inc(hqf_sig, 1)
                        fn(z_nsig[:], pair_a[1], ACT.Sigmoid, scale=-1.0).then_inc(hqf_sig, 1)
                    elif i == 7:
                        act.wait_ge(chunk_used, c + (8 + RING))
                        copy(qk_raw[:], pB[:, :, 0:T]).then_inc(qk_copied, 1)
                        copy(qk_swap[0:64], pB[64:128, :, 0:T]).then_inc(qk_copied, 1)
                        copy(qk_swap[64:128], pB[0:64, :, 0:T]).then_inc(b_free, 1)
                    elif i == 11:
                        act.wait_ge(chunk_used, c + (12 + RING))
                        copy(vT[:], pA[:, :, 0:T]).then_inc(a_free, 1)
                        act.wait_ge(p7_full, h * N7 + (TK0 + 1))
                        for b in range(2):
                            last = fn(kd_nat[:, b, :], p7[:, 0, b * 128:b * 128 + 128], ACT.Copy,
                                      scale=c_kdec[:, b, bass.ds(h, 1)])
                        last.then_inc(keys_copied, 1)
                    elif i == 14:
                        act.wait_ge(p56_full, h * N56 + (TV1 + 1))
                        copy(v_nat[:], p56[:, 0, :].rearrange("p (b e) -> p b e", b=2))
                        copy(kbar_nat[:], p56[:, 1, 0:256].rearrange("p (b e) -> p b e", b=2))
                        copy(v_rows[:], p56[0:4 * NS, 1, 256:512]).then_inc(p56_free, 1)
                    elif i == 15:
                        act.wait_ge(chunk_used, c + (16 + RING))
                        copy(hval[:], pair_b[0]).then_inc(hig_copied, 1)
                        fn(hg_sig[:], pair_b[1], ACT.Sigmoid).then_inc(hig_copied, 1)
                        act.wait_ge(p7_full, h * N7 + (SF1 + 1))
                        act.wait_ge(prompt_out_ret, h * 16 + 16)
                        copy(ret_stage[:], p7[:, 0, 0:RV]).then_inc(p7_free, 1)
                        act.wait_ge(p7_free, h * N7 + (SF1 + 2))
                        act.dma_start(ret_p[bass.ds(h, 1)].rearrange("h d e -> (h d) e"), ret_stage[:]
                                      ).then_inc(prompt_out_ret, 16)
                    elif i == 16:
                        act.wait_ge(p4_full, h * N4 + (OR2 + 1))
                        copy(oT[:, :, 0:NP], p4[:, 0, :].rearrange("p (e n) -> p e n", e=2)).then_inc(p4_free, 1)
                        act.wait_ge(p7_full, h * N7 + (TI2 + 1))
                        copy(hval_nat[:], p7[:, 0, 0:256].rearrange("p (b e) -> p b e", b=2))
                        copy(hv_rows[:], p7[0:4 * NS, 0, 256:384]).then_inc(p7_free, 1)
                    elif i == 17:
                        act.wait_ge(p4_full, h * N4 + (OH3 + 1))
                        act.wait_ge(prompt_out_hg, h * 16 + 16)
                        copy(ohT[:, 0:NP], p4[:, 0, 0:NP])
                        copy(hg_stage[:], p4[:, 0, 256:384]).then_inc(p4_free, 1)
                        act.wait_ge(p4_free, h * N4 + (OH3 + 2))
                        act.dma_start(hg_p[bass.ds(h, 1)].rearrange("h d e -> (h d) e"), hg_stage[:]
                                      ).then_inc(prompt_out_hg, 16)
                    elif i == 19:
                        act.wait_ge(chunk_used, c + (20 + RING))
                        fn(rg_sig[:], pA[:, :, 0:T], ACT.Sigmoid).then_inc(rg_sig_done, 1)
                        act.wait_ge(p7_full, h * N7 + (RD3 + 1))
                        copy(o8[:], p7[0:NS, 0, 0:384]).then_inc(p7_free, 1)
                        act.dma_start(hg_s[:, bass.ds(h, 1), :, :].rearrange("b h d e -> d (b h) e"), S_hg[:]
                                      ).then_inc(state_out, 16)
                        act.dma_start(ret_s[:, bass.ds(h, 1), :, :].rearrange("b h d e -> d (b h) e"), S_ret[:]
                                      ).then_inc(state_out, 16)

            head(0, first=True)
            with act.Fori(1, H) as h:
                head(h)

            def merge_two(it, first=False):
                for u in range(2):
                    c = it * (2 * MERGE_CHUNKS) + (C_MERGE + u * MERGE_CHUNKS)
                    for i in range(MERGE_CHUNKS):
                        split_hi(u * MERGE_CHUNKS + 4 + i, c + (4 + i), 1)
                        if first and u == 0:
                            tail(i, H)
                            if i == 5:
                                act.wait_ge(state_out, 32 * (H + 1))
                                act.wait_ge(prompt_out_ret, 16 * (H + 1))
                                act.wait_ge(prompt_out_hg, 16 * (H + 1))
                                act.wait_ge(normed, 4 * H + 4)
                            if 5 <= i < 9:
                                k = 4 * (i - 5)
                                copy(ro_hi[:, k:k + 4, :], ret_o[:, k:k + 4, :]).then_inc(o_hi_done, 1)
                            elif 9 <= i < 11:
                                k = 4 * (i - 9)
                                copy(ho_hi[:, k:k + 4, :], hg_o[:, k:k + 4, :]).then_inc(o_hi_done, 1)
                        if i == 3:
                            act.wait_ge(chunk_used, c + (4 + RING))
                            fn(ga_sig[:], pA[:, :, 0:T], ACT.Sigmoid).then_inc(a_free, 1)
                        elif i == 7:
                            act.wait_ge(chunk_used, c + (8 + RING))
                            fn(gb_sig[:], pB[:, :, 0:T], ACT.Sigmoid).then_inc(b_free, 1)
                    act.wait_ge(m_step, it * 4 + (2 * u + 2))
                    copy(m_hi[:, bass.ds(it * 4 + 2 * u, 2), :], m_a[:]).then_inc(m_hi_done, 1)

            merge_two(0, first=True)
            with act.Fori(1, 4) as it:
                merge_two(it)

            with act.Fori(0, 4) as it:
                for u in range(2):
                    split_hi(4 + 4 * u, it * 8 + (C_WOUT + 4 + 4 * u), 4)
                    act.wait_ge(h2_scaled, it * 2 + (u + 1))
                    copy(h2_hi[:, bass.ds(it * 4 + 2 * u, 2), :], h2_f[:]).then_inc(h2_hi_done, 1)

            def rms_root(n):
                act.wait_ge(sumsq_done, n)
                fn(rms_std[:], p4[:, 0, 0:T], ACT.Sqrt, bias=epsilon[:], scale=1.0 / D).then_inc(std_done, 1)

            def gate_pair(j, first=False):
                split_hi(4, j * 8 + (C_FIN + 4), 4)
                if first:
                    rms_root(2)
                act.wait_ge(a_free, j + (A_FIN + 2))
                fn(gate_sig[:], gate[:], ACT.Sigmoid).then_inc(gate_sig_done, 1)
                split_hi(8, j * 8 + (C_FIN + 8), 4)
                act.wait_ge(gate_step, j * 2 + 2)
                copy(hid_hi[:, bass.ds(j * 2, 2), :], gate_up[:]).then_inc(hid_hi_done, 1)

            gate_pair(0, first=True)
            with act.Fori(1, FT // 2) as j:
                gate_pair(j)

            for c in range(C_FOUT + RING, C_END):
                split_hi(c, c, 1)
            fn(table_load[:], epsilon[:], ACT.Sqrt)
            rms_root(3)

        @block.gpsimd
        def _(pool):
            tt = nc.gpsimd.tensor_tensor
            pool.sem_inc(normed, 4)
            pool.wait_ge(vec_in, 16)
            for i in range(4):
                pool.wait_ge(x_squared, i + 1)
                tt(x_in[:, 4 * i:4 * i + 4, :], x_in[:, 4 * i:4 * i + 4, :],
                   vec[:, V_MIX + 4 * i:V_MIX + 4 * i + 4].rearrange("p (k a) -> p k a", a=1
                   ).broadcast_to([P, 4, T]), ALU.mult).then_inc(x_gain, 1)
            pool.wait_ge(inv_done, 1)
            pool.wait_ge(x_gain, 4)
            for k in range(1, KT, 2):
                tt(x_in[:, k, :], x_in[:, k, :], rms_inv[:], ALU.mult).then_inc(x_scaled[1], 1)
            pool.wait_ge(h_done, KT)
            for i in range(NLEV):
                nc.gpsimd.memset(k_lev[i][:], 0.0).then_inc(products, 1)

            steps = 2 + 4 * NLEV + 5
            def last_outputs(h):
                pool.wait_ge(o_inv_done, h)
                tt(oT[:], oT[:], o_inv[:, 0:1, :].broadcast_to([P, 2, T]), ALU.mult).then_inc(normed, 1)
                tt(ohT[:], ohT[:], o_inv[:, 1, :], ALU.mult).then_inc(normed, 1)
                pool.wait_ge(normed, h * 4 + 2)
                tt(ret_o[:, bass.ds(h * 2 - 2, 2), :], oT[:], rg_gate[:], ALU.mult).then_inc(normed, 1)
                tt(hg_o[:, bass.ds(h - 1, 1), :].rearrange("p h t -> p (h t)"), ohT[:], hg_gate[:], ALU.mult
                   ).then_inc(normed, 1)

            def levels(h):
                count = [NLEV]

                def step(ins):
                    count[0] += 1
                    ins.then_inc(products, 1)
                    pool.wait_ge(products, h * steps + count[0])

                pool.wait_ge(forget_done, h * 2 + 2)
                pool.wait_ge(a_free, h * 3 + 2)
                tt(qk_prod[:], hquery[:, 0:NP], hkey[:, 0:NP], ALU.mult).then_inc(products, 1)
                nc.gpsimd.memset(run_g[:], 1.0).then_inc(products, 1)
                count[0] += 2
                step(nc.gpsimd.tensor_copy(run_f[:], forget[:, 0:NP]))
                for i in range(NLEV):
                    s = 1 << i
                    f0, f1 = halves(run_f[:], s)
                    g0, g1 = halves(run_g[:], s)
                    k0, _ = halves(hkey[:, 0:NP], s)
                    _, q1 = halves(hquery[:, 0:NP], s)
                    kl0, _ = halves(k_lev[i][:], s)
                    shape = [P, NP // (2 * s), s]
                    tt(q_lev[i][:].rearrange("p (b s) -> p b s", s=s), q1, f1, ALU.mult).then_inc(products, 1)
                    count[0] += 1
                    step(tt(kl0, k0, g0, ALU.mult))
                    step(tt(g0, g0, f1[:, :, s - 1:s].broadcast_to(shape), ALU.mult))
                    step(tt(f1, f1, f0[:, :, s - 1:s].broadcast_to(shape), ALU.mult))
                tt(q_lev[NLEV][:], hquery[:, P:NP], run_f[:, P:NP], ALU.mult).then_inc(products, 1)
                tt(k_top[:], hkey[:, 0:P], run_g[:, 0:P], ALU.mult).then_inc(products, 1)
                count[0] += 2
                step(tt(run_g[:, 0:P], run_g[:, 0:P], run_f[:, NP - 1:NP].broadcast_to([P, P]), ALU.mult))
                step(tt(kbar[:], hkey[:, 0:NP], run_g[:], ALU.mult))
                assert count[0] == NLEV + steps

            levels(0)
            with pool.Fori(1, H) as h:
                last_outputs(h)
                levels(h)
            last_outputs(H)

            for g in range(8):
                pool.wait_ge(res_step, 18 + 2 * g + 1)
                tt(x2[:, 2 * g:2 * g + 2, :], x2[:, 2 * g:2 * g + 2, :],
                   vec[:, V_FINAL + 2 * g:V_FINAL + 2 * g + 2].rearrange("p (k a) -> p k a", a=1
                   ).broadcast_to([P, 2, T]), ALU.mult).then_inc(y_gain, 1)
            pool.wait_ge(inv_done, 3)
            pool.wait_ge(y_gain, 8)
            for i in range(3):
                k = 10 + 2 * i
                tt(x2[:, k:k + 2, :], x2[:, k:k + 2, :], rms_inv[:].rearrange("p (a t) -> p a t", a=1
                   ).broadcast_to([P, 2, T]), ALU.mult).then_inc(y_scaled[1], 1)

        @block.vector
        def _(dve):
            tt, ts = nc.vector.tensor_tensor, nc.vector.tensor_scalar
            stt = nc.vector.scalar_tensor_tensor

            def split_lo(k, c, n):
                for i in range(n):
                    s = (k + i) % RING
                    dve.wait_ge(hi_done, c + (i + 1))
                    tt(lo[s][:], raw[s][:], hi[s][:].bitcast(F32), ALU.subtract).then_inc(split_done, 1)

            dve.sem_inc(split_done, RING)
            nc.vector.memset(epsilon[:], EPS).then_inc(setup_done, 1)
            nc.vector.memset(ones[:], 1.0).then_inc(setup_done, 1)
            dve.wait_ge(vec_in, 16)
            logits = vec[:, V_LB:V_LB + 2 * H].rearrange("p (r h) -> p r h", r=2)
            tt(lb_tmp[:, 0, :], logits[:, 0, :], logits[:, 1, :], ALU.max).then_inc(lb_max, 1)
            dve.wait_ge(lb_max, 1)
            for r in range(2):
                tt(lb_tmp[:, 1 + r, :], logits[:, r, :], lb_tmp[:, 0, :], ALU.subtract).then_inc(lb_max, 1)
            dve.wait_ge(lb_exp, 1)
            tt(lb_tmp[:, 3, :], lb_tmp[:, 1, :], lb_tmp[:, 2, :], ALU.add).then_inc(lb_step, 1)
            dve.wait_ge(lb_step, 1)
            nc.vector.reciprocal(lb_tmp[:, 0, :], lb_tmp[:, 3, :]).then_inc(lb_step, 1)
            dve.wait_ge(lb_step, 2)
            tt(lb[:], lb_tmp[:, 1, :], lb_tmp[:, 0, :], ALU.mult).then_inc(lb_step, 1)
            dve.wait_ge(lb_step, 3)
            ts(omlb[:], lb[:], -1.0, 1.0, ALU.mult, ALU.add).then_inc(lb_step, 1)
            for i in range(2, 4):
                dve.wait_ge(x_squared, i + 1)
                tt(x_sq[:, 4:8, :], x_sq[:, 4:8, :], x_sq[:, 4 * i:4 * i + 4, :], ALU.add).then_inc(squares_added, 1)
                dve.wait_ge(squares_added, i - 1)
            tt(x_sq[:, 4:6, :], x_sq[:, 4:6, :], x_sq[:, 6:8, :], ALU.add).then_inc(squares_added, 1)
            split_lo(0, 0, 1)
            dve.wait_ge(std_done, 1)
            nc.vector.reciprocal(rms_inv[:], rms_std[:]).then_inc(inv_done, 1)
            dve.wait_ge(inv_done, 1)
            dve.wait_ge(x_gain, 4)
            for k in range(KT + 2):
                if k < KT and k % 2 == 0:
                    tt(x_in[:, k, :], x_in[:, k, :], rms_inv[:], ALU.mult).then_inc(x_scaled[0], 1)
                if k >= 2:
                    dve.wait_ge(h_hi_done, k - 1)
                    tt(h_lo[:, k - 2, :], x_in[:, k - 2, :], h_hi[:, k - 2, :].bitcast(F32),
                       ALU.subtract).then_inc(h_done, 1)
                if k in (7, 11, 15):
                    split_lo((k - 3) // 4, (k - 3) // 4, 1)
            dve.wait_ge(cst_in, 16)
            dve.wait_ge(lb_step, 4)

            def parts(out, x, hi_at, lo_at, h, n):
                x = x.rearrange("p (a b) -> p a b", a=1).broadcast_to([P, 2, NS])
                nc.vector.tensor_copy(out[:, hi_at, :], x).then_inc(parts_done, 1)
                dve.wait_ge(parts_done, h * 10 + (2 * n + 1))
                tt(out[:, lo_at, :], x, out[:, hi_at, :].bitcast(F32), ALU.subtract).then_inc(parts_done, 1)

            key_hi, key_lo, value_hi, value_lo = slice(0, 2), slice(2, 4), slice(0, 4, 2), slice(1, 4, 2)

            def masked_query(out, q):
                tt(out, q.rearrange("p (b a) -> p b a", a=1).broadcast_to([P, NS, NS]), c_eye8, ALU.mult
                   ).then_inc(masked, 1)

            def masked_keys(out, rows32):
                shape = [4 * NS, NS, DK]
                return tt(out, rows32.rearrange("p (a d) -> p a d", a=1).broadcast_to(shape),
                          c_row8.rearrange("p (b a) -> p b a", a=1).broadcast_to(shape), ALU.mult
                          ).then_inc(masked, 1)

            def tail(i, h):
                if i == 0:
                    dve.wait_ge(outputs_squared, h * 2)
                    tt(o_sq[:, 0, :], o_sq[:, 0, :], o_sq[:, 1, :], ALU.add).then_inc(squares_summed, 1)
                elif i == 1:
                    dve.wait_ge(p56_free, h * N56 + (SS5 + 2 - N56))
                    nc.vector.reciprocal(o_inv[:], o_std[:]).then_inc(o_inv_done, 1)

            def head(h, first=False):
                c = h * HEAD_CHUNKS
                for i in range(HEAD_CHUNKS):
                    split_lo(4 + i, c + (4 + i), 1)
                    if not first:
                        tail(i, h)
                    if i == 3:
                        dve.wait_ge(hqf_sig, h * 3 + 3)
                        ts(forget[:], z_sig[:], omlb[:, bass.ds(h, 1)], lb[:, bass.ds(h, 1)], ALU.mult, ALU.add
                           ).then_inc(forget_done, 1)
                        ts(hkey[:], z_nsig[:], omlb[:, bass.ds(h, 1)], None, ALU.mult).then_inc(forget_done, 1)
                        tt(hquery[:], pair_a[0], hq_sig[:], ALU.mult).then_inc(a_free, 1)
                        dve.wait_ge(forget_done, h * 2 + 2)
                        parts(hk_parts, hkey[:, NP:T], key_hi, key_lo, h, 0)
                        dve.wait_ge(a_free, h * 3 + 2)
                        masked_query(hq_only[:], hquery[:, NP:T])
                    elif i == 7:
                        dve.wait_ge(qk_copied, h * 2 + 2)
                        dve.wait_ge(b_free, h * 2 + 2)
                        tt(qk[:], qk_raw[:], c_rope[:, :, 0, :], ALU.mult).then_inc(rotated, 1)
                        tt(qk_swap[:], qk_swap[:], c_rope[:, :, 1, :], ALU.mult).then_inc(rotated, 1)
                        dve.wait_ge(rotated, h * 3 + 2)
                        tt(qk[:], qk[:], qk_swap[:], ALU.add).then_inc(rotated, 1)
                        dve.wait_ge(rotated, h * 3 + 3)
                        parts(k_parts, qk[:, 1, NP:T], key_hi, key_lo, h, 1)
                        masked_query(q_only[:], qk[:, 0, NP:T])
                    elif i == 11:
                        dve.wait_ge(a_free, h * 3 + 3)
                        for e in range(2):
                            parts(v_parts[:, e], vT[:, e, NP:T], value_hi, value_lo, h, 2 + e)
                        dve.wait_ge(keys_copied, h + 1)
                        masked_keys(k_only[:], p7[0:4 * NS, 0, 256:384])
                        masked_keys(hk_only[:], p7[0:4 * NS, 0, 384:512])
                        dve.wait_ge(masked, h * 4 + 4)
                        dve.sem_inc(p7_free, 1)
                    elif i == 12:
                        dve.wait_ge(p4_full, h * N4 + (R0 + 1))
                        tt(hg_scores[:, 0:3:2, :], p4[:, 0, 0:256].rearrange("p (b n) -> p b n", b=2),
                           c_ident.rearrange("p (a n) -> p a n", a=1).broadcast_to([P, 2, P]), ALU.mult
                           ).then_inc(score_step, 1)
                        dve.wait_ge(p56_full, h * N56 + (L0 + 1))
                        dve.wait_ge(score_step, h + 1)
                        nc.vector.tensor_copy(hg_scores[:, 1, :], p4[:, 0, 256:384]).then_inc(p4_free, 1)
                        for n in range(NLEV):
                            s = 1 << n
                            dst = hg_scores[:, 0:3:2, :].rearrange("p k (b two s) -> p k b two s", two=2, s=s
                                                                   )[:, :, :, 1, :]
                            src = p56[:, :, 64 * n:64 * n + 64].rearrange("p k (b s) -> p k b s", s=s)
                            msk = c_level[:, n:n + 1, :].rearrange("p a (b s) -> p a b s", s=s
                                                                   ).broadcast_to([P, 2, 64 // s, s])
                            if n:
                                nc.vector.drain()
                            last = nc.vector.copy_predicated(dst, msk, src)
                        last.then_inc(p56_free, 1)
                    elif i == 13:
                        dve.wait_ge(p4_full, h * N4 + (SC1 + 1))
                        tt(ret_scores[:, 0:NP], p4[:, 0, 0:NP], cst[:, bass.ds(h * NP + K_MASK, NP)], ALU.mult)
                        tt(ret_scores[:, NP:384], p4[:, 0, NP:384], cst[:, bass.ds(h * NP + K_MASK, P)], ALU.mult
                           ).then_inc(p4_free, 1)
                    elif i in (15, 16):
                        if i == 15:
                            dve.wait_ge(hig_copied, h * 2 + 1)
                            parts(hv_parts, hval[:, NP:T], value_hi, value_lo, h, 4)
                            dve.wait_ge(state_in_ret, h * 16 + 16)
                        q = i - 15
                        dve.wait_ge(p56_full, h * N56 + (OUT2 + q + 1))
                        stt(S_ret[:, 4 * q:4 * q + 4, :].rearrange("p b e -> p (b e)"),
                            S_ret[:, 4 * q:4 * q + 4, :].rearrange("p b e -> p (b e)"),
                            cst[:, bass.ds(h + K_GAMMA, 1)], p56[:].rearrange("p k n -> p (k n)"),
                            ALU.mult, ALU.add).then_inc(p56_free, 1)
                    elif i == 17:
                        dve.wait_ge(state_in_hg, h * 16 + 16)
                        dve.wait_ge(p56_full, h * N56 + (OUTH4 + 1))
                        for b in range(NS):
                            last = stt(S_hg[:, b, :], S_hg[:, b, :], forget[:, NP + b:NP + b + 1],
                                       p56[:, b // 4, (b % 4) * 128:(b % 4) * 128 + 128], ALU.mult, ALU.add)
                        last.then_inc(p56_free, 1)
                    elif i == 18:
                        dve.wait_ge(normed, h * 4 + 4)
                        dve.wait_ge(hig_copied, h * 2 + 2)
                        stt(hg_gate[:], pair_b[1], vec[:, V_HG:V_HG + 1], hg_sig[:], ALU.mult, ALU.mult
                            ).then_inc(b_free, 1)
                    elif i == 19:
                        dve.wait_ge(rg_sig_done, h + 1)
                        tt(rg_gate[:], pA[:, :, 0:T], rg_sig[:], ALU.mult).then_inc(a_free, 1)

            head(0, first=True)
            with dve.Fori(1, H) as h:
                head(h)

            def merge_two(it, first=False):
                for u in range(2):
                    c = it * (2 * MERGE_CHUNKS) + (C_MERGE + u * MERGE_CHUNKS)
                    for i in range(MERGE_CHUNKS):
                        split_lo(u * MERGE_CHUNKS + 4 + i, c + (4 + i), 1)
                        if first and u == 0:
                            tail(i, H)
                            if 5 <= i < 11:
                                dve.wait_ge(o_hi_done, i - 4)
                                k = 4 * (i - 5 if i < 9 else i - 9)
                                o_lo, o, o_hi = (ro_lo, ret_o, ro_hi) if i < 9 else (ho_lo, hg_o, ho_hi)
                                tt(o_lo[:, k:k + 4, :], o[:, k:k + 4, :], o_hi[:, k:k + 4, :].bitcast(F32),
                                   ALU.subtract).then_inc(o_split, 1)
                        if i == 11:
                            dve.wait_ge(chunk_used, c + (12 + RING))
                            dve.wait_ge(a_free, it * 2 + (A_MERGE + u + 2))
                            tt(m_a[:], p56[:, :, 0:T], ga_sig[:], ALU.mult).then_inc(c_free, 1)
                        elif i == 13:
                            dve.wait_ge(chunk_used, c + (14 + RING))
                            dve.wait_ge(b_free, it * 2 + (B_MERGE + u + 2))
                            tt(m_b[:, 0, :], pD[0], gb_sig[:, 0, :], ALU.mult).then_inc(m_step, 1)
                            tt(m_b[:, 1, :], pD[1], gb_sig[:, 1, :], ALU.mult).then_inc(d_free, 1)
                            dve.wait_ge(d_free, it * 2 + (u + 2))
                            tt(m_a[:], m_a[:], m_b[:], ALU.add).then_inc(m_step, 1)
                            dve.wait_ge(m_hi_done, it * 2 + (u + 1))
                            tt(m_lo[:, bass.ds(it * 4 + 2 * u, 2), :], m_a[:],
                               m_hi[:, bass.ds(it * 4 + 2 * u, 2), :].bitcast(F32), ALU.subtract).then_inc(m_done, 1)

            merge_two(0, first=True)
            with dve.Fori(1, 4) as it:
                merge_two(it)

            nc.vector.memset(sq_sum[:], 0.0).then_inc(res_step, 1)

            def squares(x_pair, base):
                tt(sq[:], x_pair, x_pair, ALU.mult).then_inc(res_step, 1)
                dve.wait_ge(res_step, base + 1)
                tt(sq_sum[:], sq_sum[:], sq[:], ALU.add).then_inc(res_step, 1)

            with dve.Fori(0, 4) as it:
                for u in range(2):
                    split_lo(4 + 4 * u, it * 8 + (C_WOUT + 4 + 4 * u), 4)
                    dve.wait_ge(chunk_used, it * 8 + (C_WOUT + 4 * u + 4 + RING))
                    dve.wait_ge(x_again, it * 16 + 16)
                    x_pair = x2[:, bass.ds(it * 4 + 2 * u, 2), :]
                    psum_pair, free, used = ((pA, a_free, A_WOUT), (pB, b_free, B_WOUT))[u]
                    tt(x_pair, psum_pair[:, :, 0:T], x_pair, ALU.add).then_inc(free, 1)
                    dve.wait_ge(free, it + (used + 2))
                    tt(h2_f[:], x_pair, vec[:, bass.ds(it * 4 + (V_FFN + 2 * u), 2)].rearrange("p (k a) -> p k a", a=1
                       ).broadcast_to([P, 2, T]), ALU.mult).then_inc(h2_scaled, 1)
                    dve.wait_ge(res_step, it * 4 + (2 * u + 1))
                    squares(x_pair, it * 4 + (2 * u + 1))
                    dve.wait_ge(h2_hi_done, it * 2 + (u + 1))
                    tt(h2_lo[:, bass.ds(it * 4 + 2 * u, 2), :], h2_f[:],
                       h2_hi[:, bass.ds(it * 4 + 2 * u, 2), :].bitcast(F32), ALU.subtract).then_inc(h2_done, 1)

            def rms_reciprocal(n):
                dve.wait_ge(std_done, n)
                nc.vector.reciprocal(rms_inv[:], rms_std[:]).then_inc(inv_done, 1)
                dve.wait_ge(inv_done, n)

            def gate_pair(j, first=False):
                split_lo(4, j * 8 + (C_FIN + 4), 4)
                if first:
                    rms_reciprocal(2)
                    nc.vector.memset(sq_sum[:], 0.0).then_inc(res_step, 1)
                inv_pair = rms_inv[:].rearrange("p (a t) -> p a t", a=1).broadcast_to([P, 2, T])
                dve.wait_ge(chunk_used, j * 8 + (C_FIN + 4 + RING))
                tt(gate[:], pA[:, :, 0:T], inv_pair, ALU.mult).then_inc(a_free, 1)
                dve.wait_ge(gate_sig_done, j + 1)
                tt(gate[:], gate[:], gate_sig[:], ALU.mult).then_inc(gate_step, 1)
                split_lo(8, j * 8 + (C_FIN + 8), 4)
                dve.wait_ge(chunk_used, j * 8 + (C_FIN + 8 + RING))
                tt(gate_up[:], pB[:, :, 0:T], inv_pair, ALU.mult).then_inc(b_free, 1)
                dve.wait_ge(b_free, j + (B_FIN + 2))
                dve.wait_ge(gate_step, j * 2 + 1)
                tt(gate_up[:], gate_up[:], gate[:], ALU.mult).then_inc(gate_step, 1)
                dve.wait_ge(hid_hi_done, j + 1)
                tt(hid_lo[:, bass.ds(j * 2, 2), :], gate_up[:],
                   hid_hi[:, bass.ds(j * 2, 2), :].bitcast(F32), ALU.subtract).then_inc(hid_done, 1)

            gate_pair(0, first=True)
            with dve.Fori(1, FT // 2) as j:
                gate_pair(j)

            for g in range(8):
                c0 = C_FOUT + g * OUT_CHUNKS + RING
                for c in range(c0, min(c0 + OUT_CHUNKS, C_END)):
                    split_lo(c, c, 1)
                dve.wait_ge(chunk_used, C_FOUT + (g + 1) * OUT_CHUNKS + RING)
                x_pair = x2[:, 2 * g:2 * g + 2, :]
                psum_pair, free, used = ((pA, a_free, A_FOUT), (pB, b_free, B_FOUT))[g % 2]
                tt(x_pair, psum_pair[:, :, 0:T], x_pair, ALU.add).then_inc(free, 1)
                dve.wait_ge(free, used + g // 2 + 2)
                tt(sq[:], x_pair, x_pair, ALU.mult).then_inc(res_step, 1)
                if g < 7:
                    dve.wait_ge(res_step, 18 + 2 * g + 1)
                    tt(sq_sum[:], sq_sum[:], sq[:], ALU.add).then_inc(res_step, 1)
            rms_reciprocal(3)
            dve.wait_ge(y_gain, 8)
            for i in range(5):
                k = 2 * i
                tt(x2[:, k:k + 2, :], x2[:, k:k + 2, :], rms_inv[:].rearrange("p (a t) -> p a t", a=1
                   ).broadcast_to([P, 2, T]), ALU.mult).then_inc(y_scaled[0], 1)

        @block.tensor
        def _(pe):
            mm, transpose = nc.tensor.matmul, nc.tensor.transpose

            def use_chunk(k, c, i, n, outs, a_hi, a_lo, tall):
                s = k % RING
                pe.wait_ge(split_done, c + (RING + 1))
                for q in range(2 * CK):
                    t, kt = (i % 2, 2 * CK * (i // 2) + q) if tall else (q % 2, CK * i + q // 2)
                    w_hi, w_lo = hi[s][:, q * P:q * P + P], lo[s][:, q * P:q * P + P]
                    mm(outs[t], w_hi, a_hi[:, kt, :], start=(kt == 0), stop=False)
                    mm(outs[t], w_hi, a_lo[:, kt, :], start=False, stop=False)
                    last = mm(outs[t], w_lo, a_hi[:, kt, :], start=False, stop=(kt == CK * n - 1))
                last.then_inc(chunk_used, 1)

            def group(k, c, n, outs, a_hi, a_lo, tall=False, ready=None):
                for i in range(n):
                    if ready:
                        kt = 2 * CK * (i // 2 + 1) if tall else CK * (i + 1)
                        pe.wait_ge(ready[0], kt // ready[1])
                    use_chunk(k + i, c + i, i, n, outs, a_hi, a_lo, tall)

            pe.sem_inc(chunk_used, RING)
            for free in (a_free, b_free, p4_free, p56_free, p7_free, c_free, d_free):
                pe.sem_inc(free, 1)

            pe.wait_ge(setup_done, 2)
            pe.wait_ge(x_squared, 1)
            for k in range(4):
                mm(pA[:, 0, 0:T], ones[:], x_sq[:, k, :], start=(k == 0), stop=False)
            pe.wait_ge(squares_added, 3)
            mm(pA[:, 0, 0:T], ones[:], x_sq[:, 4, :], start=False, stop=False)
            mm(pA[:, 0, 0:T], ones[:], x_sq[:, 5, :], start=False, stop=True).then_inc(sumsq_done, 1)

            steps = 2 + 4 * NLEV + 5

            def natural(out, src, width):
                for b in range(2):
                    last = transpose(out[:, b * width:b * width + 128], src[:, b * P:b * P + P], c_ident)
                return last

            def parts_rows(out, parts):
                return transpose(out, parts.rearrange("p q b -> p (q b)").bitcast(F32), c_ident)

            def tail(i, h):
                if i == 0:
                    pe.wait_ge(p7_free, h * N7 + (RD3 + 2 - N7))
                    pe.wait_ge(p4_free, h * N4 + (TO4 + 1 - N4))
                    mm(p4[:, 0, 0:8], o8[:, 0:128], c_ident[0:NS, 0:NS], start=True, stop=True)
                    for e in range(1, 3):
                        last = transpose(p4[:, 0, 8 * e:8 * e + 8], o8[:, e * 128:e * 128 + 128], c_ident[0:NS, 0:NS])
                    last.then_inc(p4_full, 1)
                elif i == 1:
                    pe.wait_ge(p56_free, h * N56 + (SS5 + 1 - N56))
                    pe.wait_ge(squares_summed, h)
                    mm(p56[:, 0, 0:T], ones[:], o_sq[:, 0, :], start=True, stop=True)
                    mm(p56[:, 1, 0:T], ones[:], o_sq[:, 2, :], start=True, stop=True).then_inc(p56_full, 1)

            def attend(i, h):
                if i == 11:
                    pe.wait_ge(p7_free, h * N7 + (TK0 + 1))
                    pe.wait_ge(parts_done, h * 10 + 4)
                    natural(p7[:, 0, 0:256], qk[:, 1, :], 128)
                    parts_rows(p7[0:4 * NS, 0, 256:384], k_parts[:])
                    parts_rows(p7[0:4 * NS, 0, 384:512], hk_parts[:]).then_inc(p7_full, 1)
                elif i == 12:
                    pe.wait_ge(p4_free, h * N4 + (R0 + 1))
                    pe.wait_ge(products, h * steps + (NLEV + steps))
                    mm(p4[:, 0, 0:NP], ones[:], qk_prod[:], start=True, stop=True)
                    mm(p4[:, 0, 256:384], k_top[:], q_lev[NLEV][:], start=True, stop=True).then_inc(p4_full, 1)
                    pe.wait_ge(p56_free, h * N56 + (L0 + 1))
                    for n in range(NLEV):
                        for b in range(2):
                            last = mm(p56[:, b, 64 * n:64 * n + 64], k_lev[n][:, b * P:b * P + P],
                                      q_lev[n][:, 64 * b:64 * b + 64], start=True, stop=True)
                    last.then_inc(p56_full, 1)
                elif i == 13:
                    pe.wait_ge(p4_free, h * N4 + (SC1 + 1))
                    mm(p4[:, 0, 0:NP], qk[:, 1, 0:P], qk[:, 0, 0:NP], start=True, stop=True)
                    mm(p4[:, 0, NP:384], qk[:, 1, P:NP], qk[:, 0, P:NP], start=True, stop=True).then_inc(p4_full, 1)
                elif i == 14:
                    pe.wait_ge(p56_free, h * N56 + (TV1 + 1))
                    pe.wait_ge(parts_done, h * 10 + 8)
                    for e in range(2):
                        natural(p56[:, 0, e * 128:], vT[:, e, :], 256)
                        parts_rows(p56[0:4 * NS, 1, 256 + e * 128:384 + e * 128], v_parts[:, e])
                    natural(p56[:, 1, 0:256], kbar[:], 128).then_inc(p56_full, 1)
                elif i in (15, 16):
                    q = i - 15
                    pe.wait_ge(masked, h * 4 + 4)
                    pe.wait_ge(p56_free, h * N56 + (OUT2 + q + 1))
                    for b in range(4):
                        last = mm(p56[:, b // 2, (b % 2) * 256:(b % 2) * 256 + 256], k_only[:, 4 * q + b, :],
                                  v_rows[:], start=True, stop=True)
                    last.then_inc(p56_full, 1)
                    if i == 15:
                        pe.wait_ge(p7_free, h * N7 + (SF1 + 1))
                        for b in range(2):
                            last = mm(p7[:, 0, 0:RV], kd_nat[:, b, :], v_nat[:, b, :], start=(b == 0), stop=(b == 1))
                        last.then_inc(p7_full, 1)
                    else:
                        pe.wait_ge(p4_free, h * N4 + (OR2 + 1))
                        for e in range(2):
                            mm(p4[:, 0, e * 256:e * 256 + 256], v_nat[:, 0, e * 128:e * 128 + 128],
                               ret_scores[:, 0:NP], start=True, stop=False)
                            last = mm(p4[:, 0, e * 256 + P:e * 256 + NP], v_nat[:, 1, e * 128:e * 128 + 128],
                                      ret_scores[:, NP:384], start=False, stop=True)
                        last.then_inc(p4_full, 1)
                        pe.wait_ge(p7_free, h * N7 + (TI2 + 1))
                        pe.wait_ge(parts_done, h * 10 + 10)
                        natural(p7[:, 0, 0:256], hval[:], 128)
                        parts_rows(p7[0:4 * NS, 0, 256:384], hv_parts[:]).then_inc(p7_full, 1)
                elif i == 17:
                    pe.wait_ge(p4_free, h * N4 + (OH3 + 1))
                    pe.wait_ge(p7_free, h * N7 + (TI2 + 2))
                    mm(p4[:, 0, 0:NP], hval_nat[:, 0, :], hg_scores[:, 0:2, :], start=True, stop=False)
                    mm(p4[:, 0, P:NP], hval_nat[:, 1, :], hg_scores[:, 2, :], start=False, stop=True)
                    for b in range(2):
                        last = mm(p4[:, 0, 256:384], kbar_nat[:, b, :], hval_nat[:, b, :], start=(b == 0), stop=(b == 1))
                    last.then_inc(p4_full, 1)
                    pe.wait_ge(p56_free, h * N56 + (OUTH4 + 1))
                    for b in range(NS):
                        last = mm(p56[:, b // 4, (b % 4) * 128:(b % 4) * 128 + 128], hk_only[:, b, :], hv_rows[:],
                                  start=True, stop=True)
                    last.then_inc(p56_full, 1)
                elif i == 19:
                    pe.wait_ge(p56_free, h * N56 + (OUTH4 + 2))
                    pe.wait_ge(p7_free, h * N7 + (RD3 + 1))
                    for b in range(NS):
                        mm(p7[0:NS, 0, 0:RV], q_only[:, b, :], S_ret[:, b, :], start=(b == 0), stop=(b == NS - 1))
                    for b in range(NS):
                        last = mm(p7[0:NS, 0, RV:384], hq_only[:, b, :], S_hg[:, b, :], start=(b == 0),
                                  stop=(b == NS - 1))
                    last.then_inc(p7_full, 1)

            def head(h, first=False):
                c = h * HEAD_CHUNKS
                for g, (pair, free, used, tall) in enumerate((
                        (pair_a, a_free, h * 3 + 1, True), (pair_b, b_free, h * 2 + 1, True),
                        (pair_a, a_free, h * 3 + 2, False), (pair_b, b_free, h * 2 + 2, True),
                        (pair_a, a_free, h * 3 + 3, False))):
                    pe.wait_ge(free, used)
                    for i in range(4):
                        if first and g == 0:
                            pe.wait_ge(h_done, 2 * CK * (i // 2 + 1))
                        use_chunk(4 * g + i, c + (4 * g + i), i, 4, pair, h_hi, h_lo, tall)
                        if not first:
                            tail(4 * g + i, h)
                        attend(4 * g + i, h)

            head(0, first=True)
            with pe.Fori(1, H) as h:
                head(h)

            def merge_two(it, first=False):
                for u in range(2):
                    c = it * (2 * MERGE_CHUNKS) + (C_MERGE + u * MERGE_CHUNKS)
                    k = u * MERGE_CHUNKS
                    use = it * 2 + u
                    pe.wait_ge(a_free, use + (A_MERGE + 1))
                    for i in range(4):
                        use_chunk(k + i, c + i, i, 4, pair_a, h_hi, h_lo, False)
                        if first and u == 0:
                            tail(i, H)
                    pe.wait_ge(b_free, use + (B_MERGE + 1))
                    group(k + 4, c + 4, 4, pair_b, h_hi, h_lo)
                    if first and u == 0:
                        pe.wait_ge(p4_free, N4 * H + 1)
                        pe.wait_ge(p56_free, N56 * H + 1)
                        pe.wait_ge(p7_free, N7 * H + 1)
                    pe.wait_ge(c_free, use + 1)
                    group(k + 8, c + 8, 4, pC, ro_hi, ro_lo, ready=(o_split, 4) if first and u == 0 else None)
                    pe.wait_ge(d_free, use + 1)
                    if first and u == 0:
                        pe.wait_ge(o_split, 6)
                    group(k + 12, c + 12, 2, pD, ho_hi, ho_lo)

            merge_two(0, first=True)
            with pe.Fori(1, 4) as it:
                merge_two(it)
            with pe.Fori(0, 4) as it:
                pe.wait_ge(a_free, it + (A_WOUT + 1))
                group(0, it * 8 + C_WOUT, 4, pair_a, m_hi, m_lo, ready=(m_done, 2))
                pe.wait_ge(b_free, it + (B_WOUT + 1))
                group(4, it * 8 + (C_WOUT + 4), 4, pair_b, m_hi, m_lo)

            def total_squares():
                mm(p4[:, 0, 0:T], ones[:], sq_sum[:, 0, :], start=True, stop=False)
                mm(p4[:, 0, 0:T], ones[:], sq_sum[:, 1, :], start=False, stop=True).then_inc(sumsq_done, 1)

            def gate_pair(j, first=False):
                pe.wait_ge(a_free, j + (A_FIN + 1))
                group(0, j * 8 + C_FIN, 4, pair_a, h2_hi, h2_lo, ready=(h2_done, 2) if first else None)
                if first:
                    pe.wait_ge(res_step, 1 + 16)
                    total_squares()
                pe.wait_ge(b_free, j + (B_FIN + 1))
                group(4, j * 8 + (C_FIN + 4), 4, pair_b, h2_hi, h2_lo)

            gate_pair(0, first=True)
            with pe.Fori(1, FT // 2) as j:
                gate_pair(j)
            with pe.Fori(0, 2) as it:
                for g in range(4):
                    pair, free, used = ((pair_a, a_free, A_FOUT), (pair_b, b_free, B_FOUT))[g % 2]
                    pe.wait_ge(free, it * 2 + (used + g // 2 + 1))
                    group(g * OUT_CHUNKS, it * (4 * OUT_CHUNKS) + (C_FOUT + g * OUT_CHUNKS), OUT_CHUNKS, pair,
                          hid_hi, hid_lo, ready=(hid_done, 2) if g == 0 else None)
            pe.wait_ge(res_step, 18 + 14)
            mm(p4[:, 0, 0:T], ones[:], sq_sum[:, 0, :], start=True, stop=False)
            mm(p4[:, 0, 0:T], ones[:], sq_sum[:, 1, :], start=False, stop=False)
            pe.wait_ge(res_step, 18 + 15)
            mm(p4[:, 0, 0:T], ones[:], sq[:, 0, :], start=False, stop=False)
            mm(p4[:, 0, 0:T], ones[:], sq[:, 1, :], start=False, stop=True).then_inc(sumsq_done, 1)


def constants(np):
    half = DK // 2
    inv_freq = (np.float32(10000.0) ** (-np.arange(half, dtype=np.float32) / np.float32(half))).astype(np.float32)
    pos = np.concatenate([np.arange(NP), np.full(NS, 2048)]).astype(np.float32)
    ang = (pos[None, :] * inv_freq[:, None]).astype(np.float32).astype(np.float64)
    cos = np.concatenate([np.cos(ang), np.cos(ang)])
    sin = np.concatenate([-np.sin(ang), np.sin(ang)])
    scale = DK ** -0.5
    rope = np.stack([cos, sin, cos * scale, sin * scale], axis=1).reshape(P, 4 * T)
    gamma = 1.0 - 2.0 ** (-5.0 - np.arange(H, dtype=np.float64))
    m, n = np.arange(P)[:, None], np.arange(NP)[None, :]
    mask = np.where(n >= m, gamma[:, None, None] ** np.maximum(n - m, 0), 0.0)
    j = np.arange(64)[None, :]
    level = []
    for i in range(NLEV):
        s = 1 << i
        n_of = (j // s) * 2 * s + s + j % s
        level.append((m // (2 * s) == n_of // (2 * s)) & (m % (2 * s) < s))
    kdec = gamma[None, None, :] ** (NP - 1 - (np.arange(2)[None, :, None] * P + np.arange(P)[:, None, None]))
    c = np.zeros((P, K_SIZE), np.float32)
    c[:, K_ROPE:K_ROPE + 4 * T] = rope
    c[:, K_MASK:K_MASK + H * NP] = mask.transpose(1, 0, 2).reshape(P, H * NP)
    c[:, K_LEVEL:K_LEVEL + NLEV * 64] = np.concatenate(level, axis=1)
    c[:, K_IDENT:K_IDENT + P] = np.eye(P)
    c[:, K_KDEC:K_KDEC + 2 * H] = kdec.reshape(P, 2 * H)
    c[:, K_GAMMA:K_GAMMA + H] = gamma[None, :]
    c[:, K_EYE8:K_EYE8 + NS * NS] = np.eye(NS).reshape(1, NS * NS)
    c[:, K_ROW8:K_ROW8 + NS] = np.tile(np.eye(NS), (P // NS, 1))
    return c


def kernel(**inputs):
    import numpy as np
    import concourse.bacc as bacc
    from concourse.bass_utils import run_bass_kernel_spmd

    a = {k: np.asarray(v) for k, v in inputs.items()}

    def tiled(v):
        return v.reshape(-1, P).T

    tokens = np.concatenate([a["x_prompt"][0], a["x_sample"][:, 0]], axis=0)
    arrays = {
        "consts": constants(np),
        "vectors": np.ascontiguousarray(np.concatenate(
            [tiled(a["norm_mix"][0]), tiled(a["norm_ffn"][0]), tiled(a["norm_final"]), tiled(a["hgrn_norm"][0]),
             tiled(a["hgrn_lb_logits"].reshape(-1))], axis=1)),
        "xT": np.ascontiguousarray(tokens.T.reshape(KT, P, T).transpose(1, 0, 2)),
        "w_in": a["w_in"][0], "w_ret": a["w_ret_out"][0], "w_hg": a["w_hgrn_out"][0], "w_out": a["w_out"][0],
        "w_fin": a["w_ffn_in"][0], "w_fout": a["w_ffn_out"][0],
        "s_ret": a["state_ret"][0], "s_hg": a["state_hgrn"][0],
    }
    outs = {"yT": (P, KT, T), "ret_p": (H, DK, RV), "hg_p": (H, DK, HV),
            "ret_s": (NS, H, DK, RV), "hg_s": (NS, H, DK, HV)}
    nc = bacc.Bacc("TRN2", target_bir_lowering=False, num_devices=1)
    aps = [nc.dram_tensor(f"in_{n}", v.shape, F32, kind="ExternalInput").ap() for n, v in arrays.items()]
    aps += [nc.dram_tensor(f"out_{n}", s, F32, kind="ExternalOutput").ap() for n, s in outs.items()]
    build(nc, *aps)
    r = run_bass_kernel_spmd(nc, [{f"in_{n}": np.ascontiguousarray(v) for n, v in arrays.items()}], core_ids=[0])
    got = {n: r.results[0][f"out_{n}"] for n in outs}
    y = got["yT"].transpose(1, 0, 2).reshape(D, T).T
    return (np.ascontiguousarray(y[:NP])[None], np.ascontiguousarray(y[NP:])[:, None],
            got["ret_p"][None, None], got["hg_p"][None, None], got["ret_s"][None], got["hg_s"][None])
```

```python
from contextlib import ExitStack

import concourse.bass as bass
from concourse import mybir

ALU = mybir.AluOpType
ACT = mybir.ActivationFunctionType
F32 = mybir.dt.float32
F32R = mybir.dt.float32r
I32 = mybir.dt.int32
AX = mybir.AxisListType

P = 128
D = 2048
KT = D // P
NP = 256
NS = 8
T = NP + NS
H = 8
DK = 128
RV = 256
HV = 128
FF = 5632
FT = FF // P
EPS = 1e-6
NLEV = 7

RQ, RK, RVO, RG = 0, 1024, 2048, 4096
HQ, HF, HI, HG = 6144, 7168, 8192, 9216
GA, GB = 10240, 12288

RING = 4
CK = 4
CHUNK = CK * 256

HEAD_CHUNKS, MERGE_CHUNKS, PAIR_CHUNKS, IN_CHUNKS, OUT_CHUNKS = 20, 14, 4, 8, 11
C_MERGE = H * HEAD_CHUNKS
C_WOUT = C_MERGE + 8 * MERGE_CHUNKS
C_FIN = C_WOUT + 8 * PAIR_CHUNKS
C_FOUT = C_FIN + (FT // 2) * IN_CHUNKS
C_END = C_FOUT + 8 * OUT_CHUNKS
A_MERGE, B_MERGE = 3 * H, 2 * H
A_WOUT, B_WOUT = A_MERGE + 8, B_MERGE + 8
A_FIN, B_FIN = A_WOUT + 4, B_WOUT + 4
A_FOUT, B_FOUT = A_FIN + FT // 2, B_FIN + FT // 2

R0, SC1, OR2, OH3, TO4, N4 = 0, 1, 2, 3, 4, 5
L0, TV1, OUT2, OUTH4, SS5, N56 = 0, 1, 2, 4, 5, 6
TK0, SF1, TI2, RD3, N7 = 0, 1, 2, 3, 4

K_ROPE = 0
K_MASK = K_ROPE + 4 * T
K_LEVEL = K_MASK + H * NP
K_IDENT = K_LEVEL + NLEV * 64
K_KDEC = K_IDENT + P
K_GAMMA = K_KDEC + 2 * H
K_EYE8 = K_GAMMA + H
K_ROW8 = K_EYE8 + NS * NS
K_SIZE = K_ROW8 + NS
V_MIX, V_FFN, V_FINAL, V_HG, V_LB = 0, KT, 2 * KT, 3 * KT, 3 * KT + 1
V_SIZE = V_LB + 2 * H


def halves(ap, s):
    v = ap.rearrange("p (b two s) -> p b two s", two=2, s=s)
    return v[:, :, 0, :], v[:, :, 1, :]


def build(nc, consts, vectors, xT, w_in, w_ret, w_hg, w_out, w_fin, w_fout, s_ret, s_hg,
          yT, ret_p, hg_p, ret_s, hg_s):
    with ExitStack() as ctx:
        def sem(name):
            return ctx.enter_context(nc.semaphore(name))

        def alloc(stack, name, shape, dt=F32):
            return stack.enter_context(nc.sbuf_tensor(name, shape, dt))

        raw = [alloc(ctx, f"raw{i}", [P, CHUNK]) for i in range(RING)]
        hi = [alloc(ctx, f"hi{i}", [P, CHUNK], F32R) for i in range(RING)]
        lo = [alloc(ctx, f"lo{i}", [P, CHUNK], F32R) for i in range(RING)]
        ones = alloc(ctx, "ones", [P, P])
        vec = alloc(ctx, "vec", [P, V_SIZE])
        rms_std = alloc(ctx, "rms_std", [P, T])
        rms_inv = alloc(ctx, "rms_inv", [P, T])
        epsilon = alloc(ctx, "epsilon", [P, 1])
        table_load = alloc(ctx, "table_load", [P, 1])

        early = ExitStack()
        h_hi = alloc(early, "h_hi", [P, KT, T], F32R)
        h_lo = alloc(early, "h_lo", [P, KT, T], F32R)
        ret_o = alloc(early, "ret_o", [P, 2 * H, T])
        hg_o = alloc(early, "hg_o", [P, H, T])

        heads = ExitStack()
        cst = alloc(heads, "cst", [P, K_SIZE])
        lb = alloc(heads, "lb", [P, H])
        omlb = alloc(heads, "omlb", [P, H])
        lb_tmp = alloc(heads, "lb_tmp", [P, 4, H])
        norm_tmp = ExitStack()
        x_in = alloc(norm_tmp, "x_in", [P, KT, T])
        x_gained = alloc(norm_tmp, "x_gained", [P, KT, T])
        x_sq = alloc(norm_tmp, "x_sq", [P, KT, T])
        norm_tmp.close()
        forget = alloc(heads, "forget", [P, T])
        hkey = alloc(heads, "hkey", [P, T])
        hquery = alloc(heads, "hquery", [P, T])
        hig = alloc(heads, "hig", [P, 2, T])
        hg_sig = alloc(heads, "hg_sig", [P, T])
        hg_gate = alloc(heads, "hg_gate", [P, T])
        qk = alloc(heads, "qk", [P, 2, T])
        rg_sig = alloc(heads, "rg_sig", [P, 2, T])
        rg_gate = alloc(heads, "rg_gate", [P, 2, T])
        hval_nat = alloc(heads, "hval_nat", [P, 2, HV])
        hv_rows = alloc(heads, "hv_rows", [4 * NS, HV], F32R)
        kbar_nat = alloc(heads, "kbar_nat", [P, 2, DK])
        v_nat = alloc(heads, "v_nat", [P, 2, RV])
        v_rows = alloc(heads, "v_rows", [4 * NS, RV], F32R)
        kd_nat = alloc(heads, "kd_nat", [P, 2, DK])
        k_parts = alloc(heads, "k_parts", [P, 4, NS], F32R)
        hk_parts = alloc(heads, "hk_parts", [P, 4, NS], F32R)
        v_parts = alloc(heads, "v_parts", [P, 2, 4, NS], F32R)
        hv_parts = alloc(heads, "hv_parts", [P, 4, NS], F32R)
        k_only = alloc(heads, "k_only", [4 * NS, NS, DK], F32R)
        hk_only = alloc(heads, "hk_only", [4 * NS, NS, DK], F32R)
        q_parts = alloc(heads, "q_parts", [P, NS, 2], F32R)
        hq_parts = alloc(heads, "hq_parts", [P, NS, 2], F32R)
        q_only = alloc(heads, "q_only", [P, NS, 2, NS], F32R)
        hq_only = alloc(heads, "hq_only", [P, NS, 2, NS], F32R)
        o16 = alloc(heads, "o16", [2 * NS, 384])
        hg_scores = alloc(heads, "hg_scores", [P, 3, P])
        ret_scores = alloc(heads, "ret_scores", [P, 384])
        oT = alloc(heads, "oT", [P, 2, T])
        ohT = alloc(heads, "ohT", [P, T])
        ret_stage = alloc(heads, "ret_stage", [P, RV])
        hg_stage = alloc(heads, "hg_stage", [P, HV])
        S_ret = alloc(heads, "S_ret", [P, NS, RV])
        S_hg = alloc(heads, "S_hg", [P, NS, HV])
        k_lev = [alloc(heads, f"k_lev{i}", [P, NP]) for i in range(NLEV)]
        passing = ExitStack()
        hq_sig = alloc(passing, "hq_sig", [P, T])
        z_sig = alloc(passing, "z_sig", [P, T])
        z_nsig = alloc(passing, "z_nsig", [P, T])
        qk_raw = alloc(passing, "qk_raw", [P, 2, T])
        qk_swap = alloc(passing, "qk_swap", [P, 2, T])
        hqf = alloc(passing, "hqf", [P, 2, T])
        vT = alloc(passing, "vT", [P, 2, T])
        o_sq = alloc(passing, "o_sq", [P, 3, T])
        o_inv = alloc(passing, "o_inv", [P, 2, T])
        run_f = alloc(passing, "run_f", [P, NP])
        run_g = alloc(passing, "run_g", [P, NP])
        q_lev = [alloc(passing, f"q_lev{i}", [P, P]) for i in range(NLEV + 1)]
        k_top = alloc(passing, "k_top", [P, P])
        kbar = alloc(passing, "kbar", [P, NP])
        qk_prod = alloc(passing, "qk_prod", [P, NP])
        passing.close()
        S_ret_hi = alloc(heads, "S_ret_hi", [P, NS, RV], F32R)
        S_ret_lo = alloc(heads, "S_ret_lo", [P, NS, RV], F32R)
        S_hg_hi = alloc(heads, "S_hg_hi", [P, NS, HV], F32R)
        S_hg_lo = alloc(heads, "S_hg_lo", [P, NS, HV], F32R)
        heads.close()

        merge = ExitStack()
        ga_sig = alloc(merge, "ga_sig", [P, 2, T])
        gb_sig = alloc(merge, "gb_sig", [P, 2, T])
        m_a = alloc(merge, "m_a", [P, 2, T])
        m_b = alloc(merge, "m_b", [P, 2, T])
        ro_hi = alloc(merge, "ro_hi", [P, 2 * H, T], F32R)
        ro_lo = alloc(merge, "ro_lo", [P, 2 * H, T], F32R)
        ho_hi = alloc(merge, "ho_hi", [P, H, T], F32R)
        ho_lo = alloc(merge, "ho_lo", [P, H, T], F32R)
        m_hi = alloc(merge, "m_hi", [P, KT, T], F32R)
        m_lo = alloc(merge, "m_lo", [P, KT, T], F32R)
        merge.close()
        early.close()

        late = ExitStack()
        x2 = alloc(late, "x2", [P, KT, T])
        sq = alloc(late, "sq", [P, 2, T])
        sq_sum = alloc(late, "sq_sum", [P, 2, T])
        gate_sig = alloc(late, "gate_sig", [P, 2, T])
        gate = alloc(late, "gate", [P, 2, T])
        gate_up = alloc(late, "gate_up", [P, 2, T])
        h2_f = alloc(late, "h2_f", [P, 2, T])
        h2_hi = alloc(late, "h2_hi", [P, KT, T], F32R)
        h2_lo = alloc(late, "h2_lo", [P, KT, T], F32R)
        hid_hi = alloc(late, "hid_hi", [P, FT, T], F32R)
        hid_lo = alloc(late, "hid_lo", [P, FT, T], F32R)
        late.close()

        c_rope = cst[:, K_ROPE:K_ROPE + 4 * T].rearrange("p (a c t) -> p a c t", a=2, c=2)
        c_ident = cst[:, K_IDENT:K_IDENT + P]
        c_level = cst[:, K_LEVEL:K_LEVEL + NLEV * 64].bitcast(I32).rearrange("p (l j) -> p l j", l=NLEV)
        c_kdec = cst[:, K_KDEC:K_KDEC + 2 * H].rearrange("p (b h) -> p b h", b=2)
        c_eye8 = cst[:, K_EYE8:K_EYE8 + NS * NS].rearrange("p (b j) -> p b j", b=NS)
        c_row8 = cst[0:4 * NS, K_ROW8:K_ROW8 + NS]

        def psum(name, banks):
            return ctx.enter_context(nc.psum_tensor(name, [P, banks, 512], F32))

        pA = psum("pA", 2)
        pB = psum("pB", 2)
        p4 = psum("p4", 1)
        p56 = psum("p56", 2)
        p7 = psum("p7", 1)
        pC = [p56[:, 0, 0:T], p56[:, 1, 0:T]]
        pD = [p4[:, 0, 0:T], p7[:, 0, 0:T]]
        pair_a = [pA[:, 0, 0:T], pA[:, 1, 0:T]]
        pair_b = [pB[:, 0, 0:T], pB[:, 1, 0:T]]

        raw_full = [sem(f"raw_full{i}") for i in range(RING)]
        hi_done = sem("hi_done")
        split_done = sem("split_done")
        chunk_used = sem("chunk_used")
        a_free, b_free = sem("a_free"), sem("b_free")
        p4_full, p4_free = sem("p4_full"), sem("p4_free")
        p56_full, p56_free = sem("p56_full"), sem("p56_free")
        p7_full, p7_free = sem("p7_full"), sem("p7_free")
        vec_in, x_in_full, cst_in = sem("vec_in"), [sem(f"x_in_full{i}") for i in range(4)], sem("cst_in")
        setup_done = sem("setup_done")
        x_squared = sem("x_squared")
        sumsq_done = sem("sumsq_done")
        std_done = sem("std_done")
        inv_done = sem("inv_done")
        h_hi_done, h_done = sem("h_hi_done"), sem("h_done")
        x_gain = [sem("x_gain_dve"), sem("x_gain_pool")]
        squares_added = sem("squares_added")
        rope_scaled = sem("rope_scaled")
        lb_max, lb_exp, lb_step = sem("lb_max"), sem("lb_exp"), sem("lb_step")
        hqf_sig = sem("hqf_sig")
        forget_done = sem("forget_done")
        qk_copied = sem("qk_copied")
        rotated = sem("rotated")
        hg_sig_done = sem("hg_sig_done")
        products = sem("products")
        parts_done = sem("parts_done")
        masked = sem("masked")
        keys_copied = sem("keys_copied")
        score_step = sem("score_step")
        rg_sig_done = sem("rg_sig_done")
        state_hi = sem("state_hi")
        state_split = sem("state_split")
        sample_outputs = sem("sample_outputs")
        outputs_squared = sem("outputs_squared")
        squares_summed = sem("squares_summed")
        o_inv_done = sem("o_inv_done")
        normed = sem("normed")
        state_in_ret, state_in_hg = sem("state_in_ret"), sem("state_in_hg")
        state_out = sem("state_out")
        prompt_out_ret, prompt_out_hg = sem("prompt_out_ret"), sem("prompt_out_hg")
        o_hi_done, o_split = sem("o_hi_done"), sem("o_split")
        ga_done, gb_done = sem("ga_done"), sem("gb_done")
        m_step = sem("m_step")
        m_hi_done, m_done = sem("m_hi_done"), sem("m_done")
        c_free, d_free = sem("c_free"), sem("d_free")
        x_again = sem("x_again")
        res_step = sem("res_step")
        h2_scaled, h2_hi_done, h2_done = sem("h2_scaled"), sem("h2_hi_done"), sem("h2_done")
        gate_sig_done = sem("gate_sig_done")
        gate_step = sem("gate_step")
        hid_hi_done, hid_done = sem("hid_hi_done"), sem("hid_done")
        y_gain = sem("y_gain")
        y_scaled, y_out = [sem("y_scaled_dve"), sem("y_scaled_pool")], sem("y_out")

        def rows(w):
            return w.rearrange("(c k p) n -> c p k n", k=CK, p=P)

        v_in, v_ret, v_hg, v_out = rows(w_in), rows(w_ret), rows(w_hg), rows(w_out)
        v_fin, v_fout = rows(w_fin), rows(w_fout)

        v_tall = w_in.rearrange("(c k p) n -> c p k n", k=2 * CK, p=P)

        def tall(i, first, col):
            return v_tall[i // 2][:, :, first + 1024 * (i % 2):][:, :, bass.ds(col, 128)]

        block = ctx.enter_context(nc.Block())

        @block.sync
        def _(sp):
            sp.sem_inc(prompt_out_ret, 16)
            sp.sem_inc(prompt_out_hg, 16)
            sp.sem_inc(state_out, 32)
            sp.dma_start(vec[:], vectors).then_inc(vec_in, 16)

            def load_x(i):
                sp.dma_start(x_in[:, 4 * i:4 * i + 4, :], xT[:, 4 * i:4 * i + 4, :]).then_inc(x_in_full[i], 16)

            def load(k, c, src):
                sp.wait_ge(split_done, c + 1)
                dst = raw[k % RING][:].rearrange("p (k n) -> p k n", n=src.shape[-1])
                sp.dma_start(dst, src).then_inc(raw_full[k % RING], 16)

            def columns(k, c, view, n, col, first=0):
                for i in range(n):
                    load(k + i, c + i, view[i][:, :, first:][:, :, bass.ds(col, 256)])

            def head(h, first=False):
                c = h * HEAD_CHUNKS
                for i in range(4):
                    if first and i < 2:
                        load_x(2 * i)
                        load_x(2 * i + 1)
                    load(i, c + i, tall(i, HQ, h * 128))
                if first:
                    sp.dma_start(cst[:], consts).then_inc(cst_in, 16)
                for i in range(4):
                    load(4 + i, c + 4 + i, tall(i, RQ, h * 128 if first else sp.snap(h + 1) * 128 - 128))
                columns(8, c + 8, v_in, 4, h * 256, RVO)
                for i in range(4):
                    load(12 + i, c + 12 + i, tall(i, HI, h * 128))
                    if i == 1:
                        sp.wait_ge(state_out, h * 32 + 32)
                        sp.dma_start(S_ret[:], s_ret[:, bass.ds(h, 1), :, :].rearrange("b h d e -> d (b h) e")
                                     ).then_inc(state_in_ret, 16)
                        sp.dma_start(S_hg[:], s_hg[:, bass.ds(h, 1), :, :].rearrange("b h d e -> d (b h) e")
                                     ).then_inc(state_in_hg, 16)
                columns(16, c + 16, v_in, 4, h * 256, RG)

            head(0, first=True)
            with sp.Fori(1, H) as h:
                head(h)
            with sp.Fori(0, 4) as it:
                for u in range(2):
                    c = it * (2 * MERGE_CHUNKS) + (C_MERGE + u * MERGE_CHUNKS)
                    k, col, first = u * MERGE_CHUNKS, sp.snap(it + 1) * 512 - 512, u * 256
                    columns(k, c, v_in, 4, col, first + GA)
                    columns(k + 4, c + 4, v_in, 4, col, first + GB)
                    columns(k + 8, c + 8, v_ret, 4, col, first)
                    columns(k + 12, c + 12, v_hg, 2, col, first)
            with sp.Fori(0, 4) as it:
                for u in range(2):
                    columns(4 * u, it * 8 + (C_WOUT + 4 * u), v_out, 4, it * 512, 256 * u)
                    if u == 0:
                        sp.wait_ge(chunk_used, C_WOUT + RING)
                        sp.dma_start(x2[:, bass.ds(it * 4, 4), :], xT[:, bass.ds(it * 4, 4), :]).then_inc(x_again, 16)
            with sp.Fori(0, FT // 2) as j:
                columns(0, j * 8 + C_FIN, v_fin, 4, j * 256)
                columns(4, j * 8 + (C_FIN + 4), v_fin, 4, j * 256, FF)
            with sp.Fori(0, 2) as it:
                for g in range(4):
                    columns(g * OUT_CHUNKS, it * (4 * OUT_CHUNKS) + (C_FOUT + g * OUT_CHUNKS), v_fout,
                            OUT_CHUNKS, it * 1024, g * 256)
            for engine, n, k, size in ((0, 1, 0, 2), (1, 1, 10, 2), (0, 3, 2, 4), (1, 2, 12, 2), (0, 5, 6, 4),
                                       (1, 3, 14, 2)):
                sp.wait_ge(y_scaled[engine], n)
                sp.dma_start(yT[:, k:k + size, :], x2[:, k:k + size, :]).then_inc(y_out, 16)
            sp.wait_ge(y_out, 96)

        @block.scalar
        def _(act):
            copy = nc.scalar.copy
            fn = nc.scalar.activation

            def split_hi(k, c, n):
                for i in range(n):
                    s = (k + i) % RING
                    act.wait_ge(raw_full[s], 16 * ((c + i) // RING + 1) if isinstance(c, int)
                                else (c + i - s) * 4 + 16)
                    act.wait_ge(chunk_used, c + (i + 1))
                    copy(hi[s][:], raw[s][:]).then_inc(hi_done, 1)

            act.wait_ge(lb_max, 3)
            fn(lb_tmp[:, 1:3, :], lb_tmp[:, 1:3, :], ACT.Exp).then_inc(lb_exp, 1)
            act.wait_ge(setup_done, 2)
            fn(table_load[:], epsilon[:], ACT.Sqrt)
            def square(i):
                act.wait_ge(x_in_full[i], 16)
                fn(x_sq[:, 4 * i:4 * i + 4, :], x_in[:, 4 * i:4 * i + 4, :], ACT.Square).then_inc(x_squared, 1)

            def gained_hi(i):
                act.wait_ge(x_gain[i // 2], i % 2 + 1)
                copy(h_hi[:, 4 * i:4 * i + 4, :], x_gained[:, 4 * i:4 * i + 4, :]).then_inc(h_hi_done, 1)

            gained_hi(0)
            gained_hi(1)
            split_hi(0, 0, 1)
            square(0)
            square(1)
            gained_hi(2)
            split_hi(1, 1, 1)
            square(2)
            gained_hi(3)
            split_hi(2, 2, 1)
            square(3)
            split_hi(3, 3, 1)

            def rms_root(n):
                act.wait_ge(sumsq_done, n)
                fn(rms_std[:], p4[:, 0, 0:T], ACT.Sqrt, bias=epsilon[:], scale=1.0 / D).then_inc(std_done, 1)

            def tail(i, h):
                if i == 0:
                    act.wait_ge(sample_outputs, h * 2)
                    fn(o_sq[:, 0:2, :], oT[:], ACT.Square).then_inc(outputs_squared, 1)
                    fn(o_sq[:, 2, :], ohT[:], ACT.Square).then_inc(outputs_squared, 1)
                elif i == 2:
                    act.wait_ge(p56_full, h * N56 + (SS5 + 1 - N56))
                    fn(o_inv[:, 0, :], p56[:, 0, 0:T], ACT.Sqrt, bias=epsilon[:], scale=1.0 / RV)
                    fn(o_inv[:, 1, :], p56[:, 1, 0:T], ACT.Sqrt, bias=epsilon[:], scale=1.0 / HV
                       ).then_inc(p56_free, 1)

            def head(h, first=False):
                c = h * HEAD_CHUNKS
                for i in range(HEAD_CHUNKS):
                    split_hi(4 + i, c + (4 + i), 1)
                    if first and i == 2:
                        rms_root(1)
                    if not first:
                        tail(i, h)
                    if i == 3:
                        act.wait_ge(a_free, h * 3 + 2)
                        fn(hq_sig[:], hqf[:, 0, :], ACT.Sigmoid).then_inc(hqf_sig, 1)
                        fn(z_sig[:], hqf[:, 1, :], ACT.Sigmoid).then_inc(hqf_sig, 1)
                        fn(z_nsig[:], hqf[:, 1, :], ACT.Sigmoid, scale=-1.0).then_inc(hqf_sig, 1)
                    elif i == 7:
                        act.wait_ge(chunk_used, c + (8 + RING))
                        copy(qk_raw[:], pB[:, :, 0:T]).then_inc(qk_copied, 1)
                        copy(qk_swap[0:64], pB[64:128, :, 0:T]).then_inc(qk_copied, 1)
                        copy(qk_swap[64:128], pB[0:64, :, 0:T]).then_inc(b_free, 1)
                    elif i == 11:
                        act.wait_ge(p7_full, h * N7 + (TK0 + 1))
                        for b in range(2):
                            last = fn(kd_nat[:, b, :], p7[:, 0, b * 128:b * 128 + 128], ACT.Copy,
                                      scale=c_kdec[:, b, bass.ds(h, 1)])
                        last.then_inc(keys_copied, 1)
                    elif i == 14:
                        act.wait_ge(p56_full, h * N56 + (TV1 + 1))
                        copy(v_nat[:], p56[:, 0, :].rearrange("p (b e) -> p b e", b=2))
                        copy(kbar_nat[:], p56[:, 1, 0:256].rearrange("p (b e) -> p b e", b=2))
                        copy(v_rows[:], p56[0:4 * NS, 1, 256:512]).then_inc(p56_free, 1)
                    elif i == 15:
                        act.wait_ge(b_free, h * 2 + 3)
                        fn(hg_sig[:], hig[:, 1, :], ACT.Sigmoid).then_inc(hg_sig_done, 1)
                        act.wait_ge(p7_full, h * N7 + (SF1 + 1))
                        act.wait_ge(prompt_out_ret, h * 16 + 16)
                        copy(ret_stage[:], p7[:, 0, 0:RV]).then_inc(p7_free, 1)
                        act.wait_ge(p7_free, h * N7 + (SF1 + 2))
                        act.dma_start(ret_p[bass.ds(h, 1)].rearrange("h d e -> (h d) e"), ret_stage[:]
                                      ).then_inc(prompt_out_ret, 16)
                    elif i == 16:
                        act.wait_ge(p4_full, h * N4 + (OR2 + 1))
                        copy(oT[:, :, 0:NP], p4[:, 0, :].rearrange("p (e n) -> p e n", e=2)).then_inc(p4_free, 1)
                        act.wait_ge(p7_full, h * N7 + (TI2 + 1))
                        copy(hval_nat[:], p7[:, 0, 0:256].rearrange("p (b e) -> p b e", b=2))
                        copy(hv_rows[:], p7[0:4 * NS, 0, 256:384]).then_inc(p7_free, 1)
                        act.wait_ge(p56_free, h * N56 + (OUT2 + 2))
                        copy(S_ret_hi[:, 0:4, :], S_ret[:, 0:4, :]).then_inc(state_hi, 1)
                    elif i == 17:
                        act.wait_ge(p4_full, h * N4 + (OH3 + 1))
                        act.wait_ge(prompt_out_hg, h * 16 + 16)
                        copy(ohT[:, 0:NP], p4[:, 0, 0:NP])
                        copy(hg_stage[:], p4[:, 0, 256:384]).then_inc(p4_free, 1)
                        act.wait_ge(p4_free, h * N4 + (OH3 + 2))
                        act.dma_start(hg_p[bass.ds(h, 1)].rearrange("h d e -> (h d) e"), hg_stage[:]
                                      ).then_inc(prompt_out_hg, 16)
                        act.wait_ge(p56_free, h * N56 + (OUT2 + 3))
                        copy(S_ret_hi[:, 4:8, :], S_ret[:, 4:8, :]).then_inc(state_hi, 1)
                    elif i == 18:
                        act.wait_ge(p56_free, h * N56 + (OUTH4 + 2))
                        copy(S_hg_hi[:], S_hg[:]).then_inc(state_hi, 1)
                    elif i == 19:
                        act.wait_ge(a_free, h * 3 + 4)
                        fn(rg_sig[:], rg_gate[:], ACT.Sigmoid).then_inc(rg_sig_done, 1)
                        act.wait_ge(state_split, h * 3 + 3)
                        act.dma_start(hg_s[:, bass.ds(h, 1), :, :].rearrange("b h d e -> d (b h) e"), S_hg[:]
                                      ).then_inc(state_out, 16)
                        act.dma_start(ret_s[:, bass.ds(h, 1), :, :].rearrange("b h d e -> d (b h) e"), S_ret[:]
                                      ).then_inc(state_out, 16)
                        act.wait_ge(p7_full, h * N7 + (RD3 + 1))
                        copy(o16[:], p7[0:2 * NS, 0, 0:384]).then_inc(p7_free, 1)

            head(0, first=True)
            with act.Fori(1, H) as h:
                head(h)

            def merge_two(it, first=False):
                for u in range(2):
                    c = it * (2 * MERGE_CHUNKS) + (C_MERGE + u * MERGE_CHUNKS)
                    for i in range(MERGE_CHUNKS):
                        split_hi(u * MERGE_CHUNKS + 4 + i, c + (4 + i), 1)
                        if first and u == 0:
                            tail(i, H)
                            if i == 5:
                                act.wait_ge(state_out, 32 * (H + 1))
                                act.wait_ge(prompt_out_ret, 16 * (H + 1))
                                act.wait_ge(prompt_out_hg, 16 * (H + 1))
                                act.wait_ge(normed, 4 * H + 4)
                            if 5 <= i < 9:
                                k = 4 * (i - 5)
                                copy(ro_hi[:, k:k + 4, :], ret_o[:, k:k + 4, :]).then_inc(o_hi_done, 1)
                            elif 9 <= i < 11:
                                k = 4 * (i - 9)
                                copy(ho_hi[:, k:k + 4, :], hg_o[:, k:k + 4, :]).then_inc(o_hi_done, 1)
                        if i == 3:
                            act.wait_ge(a_free, it * 2 + (A_MERGE + u + 2))
                            fn(ga_sig[:], ga_sig[:], ACT.Sigmoid).then_inc(ga_done, 1)
                        elif i == 7:
                            act.wait_ge(b_free, it * 2 + (B_MERGE + u + 2))
                            fn(gb_sig[:], gb_sig[:], ACT.Sigmoid).then_inc(gb_done, 1)
                    act.wait_ge(m_step, it * 4 + (2 * u + 2))
                    copy(m_hi[:, bass.ds(it * 4 + 2 * u, 2), :], m_a[:]).then_inc(m_hi_done, 1)

            merge_two(0, first=True)
            with act.Fori(1, 4) as it:
                merge_two(it)

            with act.Fori(0, 4) as it:
                for u in range(2):
                    split_hi(4 + 4 * u, it * 8 + (C_WOUT + 4 + 4 * u), 4)
                    act.wait_ge(h2_scaled, it * 2 + (u + 1))
                    copy(h2_hi[:, bass.ds(it * 4 + 2 * u, 2), :], h2_f[:]).then_inc(h2_hi_done, 1)

            def gate_pair(j, first=False):
                split_hi(4, j * 8 + (C_FIN + 4), 4)
                if first:
                    rms_root(2)
                act.wait_ge(a_free, j + (A_FIN + 2))
                fn(gate_sig[:], gate[:], ACT.Sigmoid).then_inc(gate_sig_done, 1)
                split_hi(8, j * 8 + (C_FIN + 8), 4)
                act.wait_ge(gate_step, j * 2 + 2)
                copy(hid_hi[:, bass.ds(j * 2, 2), :], gate_up[:]).then_inc(hid_hi_done, 1)

            gate_pair(0, first=True)
            with act.Fori(1, FT // 2) as j:
                gate_pair(j)

            for c in range(C_FOUT + RING, C_END):
                split_hi(c, c, 1)
            fn(table_load[:], epsilon[:], ACT.Sqrt)
            rms_root(3)

        @block.gpsimd
        def _(pool):
            tt = nc.gpsimd.tensor_tensor
            pool.sem_inc(normed, 4)
            pool.wait_ge(vec_in, 16)
            for i in range(2, 4):
                pool.wait_ge(x_in_full[i], 16)
                tt(x_gained[:, 4 * i:4 * i + 4, :], x_in[:, 4 * i:4 * i + 4, :],
                   vec[:, V_MIX + 4 * i:V_MIX + 4 * i + 4].rearrange("p (k a) -> p k a", a=1
                   ).broadcast_to([P, 4, T]), ALU.mult).then_inc(x_gain[1], 1)
            for i in range(1, 4):
                pool.wait_ge(x_squared, i + 1)
                tt(x_sq[:, 0:4, :], x_sq[:, 0:4, :], x_sq[:, 4 * i:4 * i + 4, :], ALU.add).then_inc(squares_added, 1)
                pool.wait_ge(squares_added, i)
            tt(x_sq[:, 0:2, :], x_sq[:, 0:2, :], x_sq[:, 2:4, :], ALU.add).then_inc(squares_added, 1)
            pool.wait_ge(sumsq_done, 1)
            pool.wait_ge(h_done, 4)
            for i in range(NLEV):
                nc.gpsimd.memset(k_lev[i][:], 0.0).then_inc(products, 1)

            steps = 2 + 4 * NLEV + 5
            def last_outputs(h):
                pool.wait_ge(o_inv_done, h)
                tt(oT[:], oT[:], o_inv[:, 0:1, :].broadcast_to([P, 2, T]), ALU.mult).then_inc(normed, 1)
                tt(ohT[:], ohT[:], o_inv[:, 1, :], ALU.mult).then_inc(normed, 1)
                pool.wait_ge(normed, h * 4 + 2)
                tt(ret_o[:, bass.ds(h * 2 - 2, 2), :], oT[:], rg_gate[:], ALU.mult).then_inc(normed, 1)
                tt(hg_o[:, bass.ds(h - 1, 1), :].rearrange("p h t -> p (h t)"), ohT[:], hg_gate[:], ALU.mult
                   ).then_inc(normed, 1)

            def levels(h):
                count = [NLEV]

                def step(ins):
                    count[0] += 1
                    ins.then_inc(products, 1)
                    pool.wait_ge(products, h * steps + count[0])

                pool.wait_ge(forget_done, h * 3 + 3)
                tt(qk_prod[:], hquery[:, 0:NP], hkey[:, 0:NP], ALU.mult).then_inc(products, 1)
                nc.gpsimd.memset(run_g[:], 1.0).then_inc(products, 1)
                count[0] += 2
                step(nc.gpsimd.tensor_copy(run_f[:], forget[:, 0:NP]))
                for i in range(NLEV):
                    s = 1 << i
                    f0, f1 = halves(run_f[:], s)
                    g0, g1 = halves(run_g[:], s)
                    k0, _ = halves(hkey[:, 0:NP], s)
                    _, q1 = halves(hquery[:, 0:NP], s)
                    kl0, _ = halves(k_lev[i][:], s)
                    shape = [P, NP // (2 * s), s]
                    tt(q_lev[i][:].rearrange("p (b s) -> p b s", s=s), q1, f1, ALU.mult).then_inc(products, 1)
                    count[0] += 1
                    step(tt(kl0, k0, g0, ALU.mult))
                    step(tt(g0, g0, f1[:, :, s - 1:s].broadcast_to(shape), ALU.mult))
                    step(tt(f1, f1, f0[:, :, s - 1:s].broadcast_to(shape), ALU.mult))
                tt(q_lev[NLEV][:], hquery[:, P:NP], run_f[:, P:NP], ALU.mult).then_inc(products, 1)
                tt(k_top[:], hkey[:, 0:P], run_g[:, 0:P], ALU.mult).then_inc(products, 1)
                count[0] += 2
                step(tt(run_g[:, 0:P], run_g[:, 0:P], run_f[:, NP - 1:NP].broadcast_to([P, P]), ALU.mult))
                step(tt(kbar[:], hkey[:, 0:NP], run_g[:], ALU.mult))
                assert count[0] == NLEV + steps

            levels(0)
            with pool.Fori(1, H) as h:
                last_outputs(h)
                levels(h)
            last_outputs(H)

            for g in range(8):
                pool.wait_ge(res_step, 18 + 2 * g + 1)
                tt(x2[:, 2 * g:2 * g + 2, :], x2[:, 2 * g:2 * g + 2, :],
                   vec[:, V_FINAL + 2 * g:V_FINAL + 2 * g + 2].rearrange("p (k a) -> p k a", a=1
                   ).broadcast_to([P, 2, T]), ALU.mult).then_inc(y_gain, 1)
            pool.wait_ge(inv_done, 3)
            pool.wait_ge(y_gain, 8)
            for i in range(3):
                k = 10 + 2 * i
                tt(x2[:, k:k + 2, :], x2[:, k:k + 2, :], rms_inv[:].rearrange("p (a t) -> p a t", a=1
                   ).broadcast_to([P, 2, T]), ALU.mult).then_inc(y_scaled[1], 1)

        @block.vector
        def _(dve):
            tt, ts = nc.vector.tensor_tensor, nc.vector.tensor_scalar
            stt = nc.vector.scalar_tensor_tensor

            def split_lo(k, c, n):
                for i in range(n):
                    s = (k + i) % RING
                    dve.wait_ge(hi_done, c + (i + 1))
                    tt(lo[s][:], raw[s][:], hi[s][:].bitcast(F32), ALU.subtract).then_inc(split_done, 1)

            dve.sem_inc(split_done, RING)
            nc.vector.memset(epsilon[:], EPS).then_inc(setup_done, 1)
            nc.vector.memset(ones[:], 1.0).then_inc(setup_done, 1)
            dve.wait_ge(vec_in, 16)
            logits = vec[:, V_LB:V_LB + 2 * H].rearrange("p (r h) -> p r h", r=2)
            tt(lb_tmp[:, 0, :], logits[:, 0, :], logits[:, 1, :], ALU.max).then_inc(lb_max, 1)
            dve.wait_ge(lb_max, 1)
            for r in range(2):
                tt(lb_tmp[:, 1 + r, :], logits[:, r, :], lb_tmp[:, 0, :], ALU.subtract).then_inc(lb_max, 1)
            def gained(i):
                dve.wait_ge(x_in_full[i], 16)
                tt(x_gained[:, 4 * i:4 * i + 4, :], x_in[:, 4 * i:4 * i + 4, :],
                   vec[:, V_MIX + 4 * i:V_MIX + 4 * i + 4].rearrange("p (k a) -> p k a", a=1
                   ).broadcast_to([P, 4, T]), ALU.mult).then_inc(x_gain[0], 1)

            def gained_lo(i):
                dve.wait_ge(h_hi_done, i + 1)
                tt(h_lo[:, 4 * i:4 * i + 4, :], x_gained[:, 4 * i:4 * i + 4, :],
                   h_hi[:, 4 * i:4 * i + 4, :].bitcast(F32), ALU.subtract).then_inc(h_done, 1)

            gained(0)
            gained(1)
            gained_lo(0)
            gained_lo(1)
            split_lo(0, 0, 1)
            dve.wait_ge(lb_exp, 1)
            tt(lb_tmp[:, 3, :], lb_tmp[:, 1, :], lb_tmp[:, 2, :], ALU.add).then_inc(lb_step, 1)
            dve.wait_ge(lb_step, 1)
            nc.vector.reciprocal(lb_tmp[:, 0, :], lb_tmp[:, 3, :]).then_inc(lb_step, 1)
            dve.wait_ge(lb_step, 2)
            tt(lb[:], lb_tmp[:, 1, :], lb_tmp[:, 0, :], ALU.mult).then_inc(lb_step, 1)
            dve.wait_ge(lb_step, 3)
            ts(omlb[:], lb[:], -1.0, 1.0, ALU.mult, ALU.add).then_inc(lb_step, 1)
            gained_lo(2)
            split_lo(1, 1, 1)
            gained_lo(3)
            split_lo(2, 2, 2)

            def rms_reciprocal(n):
                dve.wait_ge(std_done, n)
                nc.vector.reciprocal(rms_inv[:], rms_std[:]).then_inc(inv_done, 1)
                dve.wait_ge(inv_done, n)

            inv_pair = rms_inv[:].rearrange("p (a t) -> p a t", a=1).broadcast_to([P, 2, T])

            def parts(hi_out, lo_out, x, h, n):
                nc.vector.tensor_copy(hi_out, x).then_inc(parts_done, 1)
                dve.wait_ge(parts_done, h * 14 + (2 * n + 1))
                tt(lo_out, x, hi_out.bitcast(F32), ALU.subtract).then_inc(parts_done, 1)

            def twice(x):
                return x.rearrange("p (a b) -> p a b", a=1).broadcast_to([P, 2, NS])

            def key_parts(out, x, h, n):
                parts(out[:, 0:2, :], out[:, 2:4, :], twice(x), h, n)

            def value_parts(out, x, h, n):
                parts(out[:, 0:4:2, :], out[:, 1:4:2, :], twice(x), h, n)

            def query_parts(out, x, h, n):
                parts(out[:, :, 0], out[:, :, 1], x, h, n)

            def masked_query(out, q):
                shape = [P, NS, 2, NS]
                tt(out, q.bitcast(F32).rearrange("p b (c a) -> p b c a", a=1).broadcast_to(shape),
                   c_eye8.rearrange("p b (a j) -> p b a j", a=1).broadcast_to(shape), ALU.mult).then_inc(masked, 1)

            def masked_keys(out, rows32):
                shape = [4 * NS, NS, DK]
                return tt(out, rows32.rearrange("p (a d) -> p a d", a=1).broadcast_to(shape),
                          c_row8.rearrange("p (b a) -> p b a", a=1).broadcast_to(shape), ALU.mult
                          ).then_inc(masked, 1)

            def state_lo(out, state, state_hi_part, h, n):
                dve.wait_ge(state_hi, h * 3 + (n + 1))
                tt(out, state, state_hi_part.bitcast(F32), ALU.subtract).then_inc(state_split, 1)

            def tail(i, h):
                if i == 0:
                    dve.wait_ge(p4_full, h * N4 + (TO4 + 1 - N4))
                    by_part = p4[:, 0, 0:48].rearrange("p (e two b) -> p e b two", e=3, two=2)
                    nc.vector.tensor_reduce(oT[:, :, NP:T], by_part[:, 0:2], AX.X, ALU.add).then_inc(sample_outputs, 1)
                    nc.vector.tensor_reduce(ohT[:, NP:T], by_part[:, 2], AX.X, ALU.add).then_inc(sample_outputs, 1)
                    dve.wait_ge(sample_outputs, h * 2)
                    dve.sem_inc(p4_free, 1)
                    dve.wait_ge(outputs_squared, h * 2 - 1)
                    tt(o_sq[:, 0, :], o_sq[:, 0, :], o_sq[:, 1, :], ALU.add).then_inc(squares_summed, 1)
                elif i == 2:
                    dve.wait_ge(p56_free, h * N56 + (SS5 + 2 - N56))
                    nc.vector.reciprocal(o_inv[:], o_inv[:]).then_inc(o_inv_done, 1)

            def head(h, first=False):
                c = h * HEAD_CHUNKS
                for i in range(HEAD_CHUNKS):
                    if i == 3:
                        dve.wait_ge(chunk_used, c + (4 + RING))
                        tt(hqf[:], pA[:, :, 0:T], inv_pair, ALU.mult).then_inc(a_free, 1)
                    elif i == 11:
                        dve.wait_ge(chunk_used, c + (12 + RING))
                        tt(vT[:], pA[:, :, 0:T], inv_pair, ALU.mult).then_inc(a_free, 1)
                    elif i == 15:
                        dve.wait_ge(chunk_used, c + (16 + RING))
                        tt(hig[:], pB[:, :, 0:T], inv_pair, ALU.mult).then_inc(b_free, 1)
                    elif i == 19:
                        dve.wait_ge(chunk_used, c + (20 + RING))
                        tt(rg_gate[:], pA[:, :, 0:T], inv_pair, ALU.mult).then_inc(a_free, 1)
                    split_lo(4 + i, c + (4 + i), 1)
                    if first and i == 2:
                        rms_reciprocal(1)
                        dve.wait_ge(lb_step, 4)
                    elif first and i == 5:
                        dve.wait_ge(cst_in, 16)
                        rope = cst[:, K_ROPE:K_ROPE + 4 * T].rearrange("p (c t) -> p c t", c=4)
                        tt(rope, rope, rms_inv[:].rearrange("p (a t) -> p a t", a=1).broadcast_to([P, 4, T]),
                           ALU.mult).then_inc(rope_scaled, 1)
                        dve.wait_ge(rope_scaled, 1)
                    if not first:
                        tail(i, h)
                    if i == 3:
                        dve.wait_ge(hqf_sig, h * 3 + 3)
                        ts(forget[:], z_sig[:], omlb[:, bass.ds(h, 1)], lb[:, bass.ds(h, 1)], ALU.mult, ALU.add
                           ).then_inc(forget_done, 1)
                        ts(hkey[:], z_nsig[:], omlb[:, bass.ds(h, 1)], None, ALU.mult).then_inc(forget_done, 1)
                        dve.wait_ge(a_free, h * 3 + 2)
                        tt(hquery[:], hqf[:, 0, :], hq_sig[:], ALU.mult).then_inc(forget_done, 1)
                        dve.wait_ge(forget_done, h * 3 + 3)
                        key_parts(hk_parts, hkey[:, NP:T], h, 0)
                        query_parts(hq_parts, hquery[:, NP:T], h, 1)
                        dve.wait_ge(parts_done, h * 14 + 4)
                        masked_query(hq_only[:], hq_parts[:])
                    elif i == 7:
                        dve.wait_ge(qk_copied, h * 2 + 2)
                        dve.wait_ge(b_free, h * 2 + 2)
                        tt(qk[:], qk_raw[:], c_rope[:, :, 0, :], ALU.mult).then_inc(rotated, 1)
                        tt(qk_swap[:], qk_swap[:], c_rope[:, :, 1, :], ALU.mult).then_inc(rotated, 1)
                        dve.wait_ge(rotated, h * 3 + 2)
                        tt(qk[:], qk[:], qk_swap[:], ALU.add).then_inc(rotated, 1)
                        dve.wait_ge(rotated, h * 3 + 3)
                        key_parts(k_parts, qk[:, 1, NP:T], h, 2)
                        query_parts(q_parts, qk[:, 0, NP:T], h, 3)
                        dve.wait_ge(parts_done, h * 14 + 8)
                        masked_query(q_only[:], q_parts[:])
                    elif i == 11:
                        dve.wait_ge(a_free, h * 3 + 3)
                        for e in range(2):
                            value_parts(v_parts[:, e], vT[:, e, NP:T], h, 4 + e)
                        dve.wait_ge(keys_copied, h + 1)
                        masked_keys(k_only[:], p7[0:4 * NS, 0, 256:384])
                        masked_keys(hk_only[:], p7[0:4 * NS, 0, 384:512])
                        dve.wait_ge(masked, h * 4 + 4)
                        dve.sem_inc(p7_free, 1)
                    elif i == 12:
                        dve.wait_ge(p4_full, h * N4 + (R0 + 1))
                        tt(hg_scores[:, 0:3:2, :], p4[:, 0, 0:256].rearrange("p (b n) -> p b n", b=2),
                           c_ident.rearrange("p (a n) -> p a n", a=1).broadcast_to([P, 2, P]), ALU.mult
                           ).then_inc(score_step, 1)
                        dve.wait_ge(p56_full, h * N56 + (L0 + 1))
                        dve.wait_ge(score_step, h + 1)
                        nc.vector.tensor_copy(hg_scores[:, 1, :], p4[:, 0, 256:384]).then_inc(p4_free, 1)
                        for n in range(NLEV):
                            s = 1 << n
                            dst = hg_scores[:, 0:3:2, :].rearrange("p k (b two s) -> p k b two s", two=2, s=s
                                                                   )[:, :, :, 1, :]
                            src = p56[:, :, 64 * n:64 * n + 64].rearrange("p k (b s) -> p k b s", s=s)
                            msk = c_level[:, n:n + 1, :].rearrange("p a (b s) -> p a b s", s=s
                                                                   ).broadcast_to([P, 2, 64 // s, s])
                            if n:
                                nc.vector.drain()
                            last = nc.vector.copy_predicated(dst, msk, src)
                        last.then_inc(p56_free, 1)
                    elif i == 13:
                        dve.wait_ge(p4_full, h * N4 + (SC1 + 1))
                        tt(ret_scores[:, 0:NP], p4[:, 0, 0:NP], cst[:, bass.ds(h * NP + K_MASK, NP)], ALU.mult)
                        tt(ret_scores[:, NP:384], p4[:, 0, NP:384], cst[:, bass.ds(h * NP + K_MASK, P)], ALU.mult
                           ).then_inc(p4_free, 1)
                    elif i in (15, 16):
                        if i == 15:
                            dve.wait_ge(state_in_ret, h * 16 + 16)
                        q = i - 15
                        dve.wait_ge(p56_full, h * N56 + (OUT2 + q + 1))
                        stt(S_ret[:, 4 * q:4 * q + 4, :].rearrange("p b e -> p (b e)"),
                            S_ret[:, 4 * q:4 * q + 4, :].rearrange("p b e -> p (b e)"),
                            cst[:, bass.ds(h + K_GAMMA, 1)], p56[:].rearrange("p k n -> p (k n)"),
                            ALU.mult, ALU.add).then_inc(p56_free, 1)
                        if i == 15:
                            dve.wait_ge(b_free, h * 2 + 3)
                            value_parts(hv_parts, hig[:, 0, NP:T], h, 6)
                        else:
                            state_lo(S_ret_lo[:, 0:4, :], S_ret[:, 0:4, :], S_ret_hi[:, 0:4, :], h, 0)
                    elif i == 17:
                        dve.wait_ge(state_in_hg, h * 16 + 16)
                        dve.wait_ge(p56_full, h * N56 + (OUTH4 + 1))
                        for b in range(NS):
                            last = stt(S_hg[:, b, :], S_hg[:, b, :], forget[:, NP + b:NP + b + 1],
                                       p56[:, b // 4, (b % 4) * 128:(b % 4) * 128 + 128], ALU.mult, ALU.add)
                        last.then_inc(p56_free, 1)
                        state_lo(S_ret_lo[:, 4:8, :], S_ret[:, 4:8, :], S_ret_hi[:, 4:8, :], h, 1)
                    elif i == 18:
                        state_lo(S_hg_lo[:], S_hg[:], S_hg_hi[:], h, 2)
                        dve.wait_ge(normed, h * 4 + 4)
                        dve.wait_ge(hg_sig_done, h + 1)
                        stt(hg_gate[:], hig[:, 1, :], vec[:, V_HG:V_HG + 1], hg_sig[:], ALU.mult, ALU.mult)
                    elif i == 19:
                        dve.wait_ge(a_free, h * 3 + 4)
                        dve.wait_ge(rg_sig_done, h + 1)
                        tt(rg_gate[:], rg_gate[:], rg_sig[:], ALU.mult)

            head(0, first=True)
            with dve.Fori(1, H) as h:
                head(h)

            def merge_two(it, first=False):
                for u in range(2):
                    c = it * (2 * MERGE_CHUNKS) + (C_MERGE + u * MERGE_CHUNKS)
                    for i in range(MERGE_CHUNKS):
                        if i == 3:
                            dve.wait_ge(chunk_used, c + (4 + RING))
                            tt(ga_sig[:], pA[:, :, 0:T], inv_pair, ALU.mult).then_inc(a_free, 1)
                        elif i == 7:
                            dve.wait_ge(chunk_used, c + (8 + RING))
                            tt(gb_sig[:], pB[:, :, 0:T], inv_pair, ALU.mult).then_inc(b_free, 1)
                        split_lo(u * MERGE_CHUNKS + 4 + i, c + (4 + i), 1)
                        if first and u == 0:
                            tail(i, H)
                            if 5 <= i < 11:
                                dve.wait_ge(o_hi_done, i - 4)
                                k = 4 * (i - 5 if i < 9 else i - 9)
                                o_lo, o, o_hi = (ro_lo, ret_o, ro_hi) if i < 9 else (ho_lo, hg_o, ho_hi)
                                tt(o_lo[:, k:k + 4, :], o[:, k:k + 4, :], o_hi[:, k:k + 4, :].bitcast(F32),
                                   ALU.subtract).then_inc(o_split, 1)
                        if i == 11:
                            dve.wait_ge(chunk_used, c + (12 + RING))
                            dve.wait_ge(ga_done, it * 2 + (u + 1))
                            tt(m_a[:], p56[:, :, 0:T], ga_sig[:], ALU.mult).then_inc(c_free, 1)
                        elif i == 13:
                            dve.wait_ge(chunk_used, c + (14 + RING))
                            dve.wait_ge(gb_done, it * 2 + (u + 1))
                            tt(m_b[:, 0, :], pD[0], gb_sig[:, 0, :], ALU.mult).then_inc(m_step, 1)
                            tt(m_b[:, 1, :], pD[1], gb_sig[:, 1, :], ALU.mult).then_inc(d_free, 1)
                            dve.wait_ge(d_free, it * 2 + (u + 2))
                            tt(m_a[:], m_a[:], m_b[:], ALU.add).then_inc(m_step, 1)
                            dve.wait_ge(m_hi_done, it * 2 + (u + 1))
                            tt(m_lo[:, bass.ds(it * 4 + 2 * u, 2), :], m_a[:],
                               m_hi[:, bass.ds(it * 4 + 2 * u, 2), :].bitcast(F32), ALU.subtract).then_inc(m_done, 1)

            merge_two(0, first=True)
            with dve.Fori(1, 4) as it:
                merge_two(it)

            nc.vector.memset(sq_sum[:], 0.0).then_inc(res_step, 1)

            def squares(x_pair, base):
                tt(sq[:], x_pair, x_pair, ALU.mult).then_inc(res_step, 1)
                dve.wait_ge(res_step, base + 1)
                tt(sq_sum[:], sq_sum[:], sq[:], ALU.add).then_inc(res_step, 1)

            with dve.Fori(0, 4) as it:
                for u in range(2):
                    split_lo(4 + 4 * u, it * 8 + (C_WOUT + 4 + 4 * u), 4)
                    dve.wait_ge(chunk_used, it * 8 + (C_WOUT + 4 * u + 4 + RING))
                    dve.wait_ge(x_again, it * 16 + 16)
                    x_pair = x2[:, bass.ds(it * 4 + 2 * u, 2), :]
                    psum_pair, free, used = ((pA, a_free, A_WOUT), (pB, b_free, B_WOUT))[u]
                    tt(x_pair, psum_pair[:, :, 0:T], x_pair, ALU.add).then_inc(free, 1)
                    dve.wait_ge(free, it + (used + 2))
                    tt(h2_f[:], x_pair, vec[:, bass.ds(it * 4 + (V_FFN + 2 * u), 2)].rearrange("p (k a) -> p k a", a=1
                       ).broadcast_to([P, 2, T]), ALU.mult).then_inc(h2_scaled, 1)
                    dve.wait_ge(res_step, it * 4 + (2 * u + 1))
                    squares(x_pair, it * 4 + (2 * u + 1))
                    dve.wait_ge(h2_hi_done, it * 2 + (u + 1))
                    tt(h2_lo[:, bass.ds(it * 4 + 2 * u, 2), :], h2_f[:],
                       h2_hi[:, bass.ds(it * 4 + 2 * u, 2), :].bitcast(F32), ALU.subtract).then_inc(h2_done, 1)

            def gate_pair(j, first=False):
                split_lo(4, j * 8 + (C_FIN + 4), 4)
                if first:
                    rms_reciprocal(2)
                    nc.vector.memset(sq_sum[:], 0.0).then_inc(res_step, 1)
                dve.wait_ge(chunk_used, j * 8 + (C_FIN + 4 + RING))
                tt(gate[:], pA[:, :, 0:T], inv_pair, ALU.mult).then_inc(a_free, 1)
                dve.wait_ge(gate_sig_done, j + 1)
                tt(gate[:], gate[:], gate_sig[:], ALU.mult).then_inc(gate_step, 1)
                split_lo(8, j * 8 + (C_FIN + 8), 4)
                dve.wait_ge(chunk_used, j * 8 + (C_FIN + 8 + RING))
                tt(gate_up[:], pB[:, :, 0:T], inv_pair, ALU.mult).then_inc(b_free, 1)
                dve.wait_ge(b_free, j + (B_FIN + 2))
                dve.wait_ge(gate_step, j * 2 + 1)
                tt(gate_up[:], gate_up[:], gate[:], ALU.mult).then_inc(gate_step, 1)
                dve.wait_ge(hid_hi_done, j + 1)
                tt(hid_lo[:, bass.ds(j * 2, 2), :], gate_up[:],
                   hid_hi[:, bass.ds(j * 2, 2), :].bitcast(F32), ALU.subtract).then_inc(hid_done, 1)

            gate_pair(0, first=True)
            with dve.Fori(1, FT // 2) as j:
                gate_pair(j)

            for g in range(8):
                c0 = C_FOUT + g * OUT_CHUNKS + RING
                for c in range(c0, min(c0 + OUT_CHUNKS, C_END)):
                    split_lo(c, c, 1)
                dve.wait_ge(chunk_used, C_FOUT + (g + 1) * OUT_CHUNKS + RING)
                x_pair = x2[:, 2 * g:2 * g + 2, :]
                psum_pair, free, used = ((pA, a_free, A_FOUT), (pB, b_free, B_FOUT))[g % 2]
                tt(x_pair, psum_pair[:, :, 0:T], x_pair, ALU.add).then_inc(free, 1)
                dve.wait_ge(free, used + g // 2 + 2)
                tt(sq[:], x_pair, x_pair, ALU.mult).then_inc(res_step, 1)
                if g < 7:
                    dve.wait_ge(res_step, 18 + 2 * g + 1)
                    tt(sq_sum[:], sq_sum[:], sq[:], ALU.add).then_inc(res_step, 1)
            rms_reciprocal(3)
            dve.wait_ge(y_gain, 8)
            for i in range(5):
                k = 2 * i
                tt(x2[:, k:k + 2, :], x2[:, k:k + 2, :], rms_inv[:].rearrange("p (a t) -> p a t", a=1
                   ).broadcast_to([P, 2, T]), ALU.mult).then_inc(y_scaled[0], 1)

        @block.tensor
        def _(pe):
            mm, transpose = nc.tensor.matmul, nc.tensor.transpose

            def use_chunk(k, c, i, n, outs, a_hi, a_lo, tall):
                s = k % RING
                pe.wait_ge(split_done, c + (RING + 1))
                for q in range(2 * CK):
                    t, kt = (i % 2, 2 * CK * (i // 2) + q) if tall else (q % 2, CK * i + q // 2)
                    w_hi, w_lo = hi[s][:, q * P:q * P + P], lo[s][:, q * P:q * P + P]
                    mm(outs[t], w_hi, a_hi[:, kt, :], start=(kt == 0), stop=False)
                    mm(outs[t], w_hi, a_lo[:, kt, :], start=False, stop=False)
                    last = mm(outs[t], w_lo, a_hi[:, kt, :], start=False, stop=(kt == CK * n - 1))
                last.then_inc(chunk_used, 1)

            def group(k, c, n, outs, a_hi, a_lo, tall=False, ready=None):
                for i in range(n):
                    if ready:
                        kt = 2 * CK * (i // 2 + 1) if tall else CK * (i + 1)
                        pe.wait_ge(ready[0], kt // ready[1])
                    use_chunk(k + i, c + i, i, n, outs, a_hi, a_lo, tall)

            pe.sem_inc(chunk_used, RING)
            for free in (a_free, b_free, p4_free, p56_free, p7_free, c_free, d_free):
                pe.sem_inc(free, 1)

            steps = 2 + 4 * NLEV + 5

            def natural(out, src, width):
                for b in range(2):
                    last = transpose(out[:, b * width:b * width + 128], src[:, b * P:b * P + P], c_ident)
                return last

            def parts_rows(out, parts):
                return transpose(out, parts.rearrange("p q b -> p (q b)").bitcast(F32), c_ident)

            def tail(i, h):
                if i == 0:
                    pe.wait_ge(p7_free, h * N7 + (RD3 + 2 - N7))
                    pe.wait_ge(p4_free, h * N4 + (TO4 + 1 - N4))
                    one16 = c_ident[0:2 * NS, 0:2 * NS]
                    mm(p4[:, 0, 0:16], o16[:, 0:128], one16, start=True, stop=True)
                    for e in range(1, 3):
                        last = transpose(p4[:, 0, 16 * e:16 * e + 16], o16[:, e * 128:e * 128 + 128], one16)
                    last.then_inc(p4_full, 1)
                elif i == 2:
                    pe.wait_ge(p56_free, h * N56 + (SS5 + 1 - N56))
                    pe.wait_ge(squares_summed, h)
                    pe.wait_ge(outputs_squared, h * 2)
                    mm(p56[:, 0, 0:T], ones[:], o_sq[:, 0, :], start=True, stop=True)
                    mm(p56[:, 1, 0:T], ones[:], o_sq[:, 2, :], start=True, stop=True).then_inc(p56_full, 1)

            def attend(i, h):
                if i == 11:
                    pe.wait_ge(p7_free, h * N7 + (TK0 + 1))
                    pe.wait_ge(parts_done, h * 14 + 6)
                    natural(p7[:, 0, 0:256], qk[:, 1, :], 128)
                    parts_rows(p7[0:4 * NS, 0, 256:384], k_parts[:])
                    parts_rows(p7[0:4 * NS, 0, 384:512], hk_parts[:]).then_inc(p7_full, 1)
                elif i == 12:
                    pe.wait_ge(p4_free, h * N4 + (R0 + 1))
                    pe.wait_ge(products, h * steps + (NLEV + steps))
                    mm(p4[:, 0, 0:NP], ones[:], qk_prod[:], start=True, stop=True)
                    mm(p4[:, 0, 256:384], k_top[:], q_lev[NLEV][:], start=True, stop=True).then_inc(p4_full, 1)
                    pe.wait_ge(p56_free, h * N56 + (L0 + 1))
                    for n in range(NLEV):
                        for b in range(2):
                            last = mm(p56[:, b, 64 * n:64 * n + 64], k_lev[n][:, b * P:b * P + P],
                                      q_lev[n][:, 64 * b:64 * b + 64], start=True, stop=True)
                    last.then_inc(p56_full, 1)
                elif i == 13:
                    pe.wait_ge(p4_free, h * N4 + (SC1 + 1))
                    mm(p4[:, 0, 0:NP], qk[:, 1, 0:P], qk[:, 0, 0:NP], start=True, stop=True)
                    mm(p4[:, 0, NP:384], qk[:, 1, P:NP], qk[:, 0, P:NP], start=True, stop=True).then_inc(p4_full, 1)
                elif i == 14:
                    pe.wait_ge(p56_free, h * N56 + (TV1 + 1))
                    pe.wait_ge(parts_done, h * 14 + 12)
                    for e in range(2):
                        natural(p56[:, 0, e * 128:], vT[:, e, :], 256)
                        parts_rows(p56[0:4 * NS, 1, 256 + e * 128:384 + e * 128], v_parts[:, e])
                    natural(p56[:, 1, 0:256], kbar[:], 128).then_inc(p56_full, 1)
                elif i in (15, 16):
                    q = i - 15
                    pe.wait_ge(masked, h * 4 + 4)
                    pe.wait_ge(p56_free, h * N56 + (OUT2 + q + 1))
                    for b in range(4):
                        last = mm(p56[:, b // 2, (b % 2) * 256:(b % 2) * 256 + 256], k_only[:, 4 * q + b, :],
                                  v_rows[:], start=True, stop=True)
                    last.then_inc(p56_full, 1)
                    if i == 15:
                        pe.wait_ge(p7_free, h * N7 + (SF1 + 1))
                        for b in range(2):
                            last = mm(p7[:, 0, 0:RV], kd_nat[:, b, :], v_nat[:, b, :], start=(b == 0), stop=(b == 1))
                        last.then_inc(p7_full, 1)
                    else:
                        pe.wait_ge(p4_free, h * N4 + (OR2 + 1))
                        for e in range(2):
                            mm(p4[:, 0, e * 256:e * 256 + 256], v_nat[:, 0, e * 128:e * 128 + 128],
                               ret_scores[:, 0:NP], start=True, stop=False)
                            last = mm(p4[:, 0, e * 256 + P:e * 256 + NP], v_nat[:, 1, e * 128:e * 128 + 128],
                                      ret_scores[:, NP:384], start=False, stop=True)
                        last.then_inc(p4_full, 1)
                        pe.wait_ge(p7_free, h * N7 + (TI2 + 1))
                        pe.wait_ge(parts_done, h * 14 + 14)
                        natural(p7[:, 0, 0:256], hig[:, 0, :], 128)
                        parts_rows(p7[0:4 * NS, 0, 256:384], hv_parts[:]).then_inc(p7_full, 1)
                elif i == 17:
                    pe.wait_ge(p4_free, h * N4 + (OH3 + 1))
                    pe.wait_ge(p7_free, h * N7 + (TI2 + 2))
                    mm(p4[:, 0, 0:NP], hval_nat[:, 0, :], hg_scores[:, 0:2, :], start=True, stop=False)
                    mm(p4[:, 0, P:NP], hval_nat[:, 1, :], hg_scores[:, 2, :], start=False, stop=True)
                    for b in range(2):
                        last = mm(p4[:, 0, 256:384], kbar_nat[:, b, :], hval_nat[:, b, :], start=(b == 0), stop=(b == 1))
                    last.then_inc(p4_full, 1)
                    pe.wait_ge(p56_free, h * N56 + (OUTH4 + 1))
                    for b in range(NS):
                        last = mm(p56[:, b // 4, (b % 4) * 128:(b % 4) * 128 + 128], hk_only[:, b, :], hv_rows[:],
                                  start=True, stop=True)
                    last.then_inc(p56_full, 1)
                elif i == 19:
                    pe.wait_ge(p7_free, h * N7 + (RD3 + 1))
                    pe.wait_ge(state_split, h * 3 + 2)
                    for query, states, cols in ((q_only, (S_ret_hi, S_ret_lo), slice(0, RV)),
                                                (hq_only, (S_hg_hi, S_hg_lo), slice(RV, 384))):
                        if query is hq_only:
                            pe.wait_ge(state_split, h * 3 + 3)
                        for b in range(NS):
                            for n, part in enumerate(states):
                                last = mm(p7[0:2 * NS, 0, cols], query[:, b].rearrange("p c j -> p (c j)"),
                                          part[:, b, :], start=(b == 0 and n == 0), stop=(b == NS - 1 and n == 1))
                    last.then_inc(p7_full, 1)

            def head(h, first=False):
                c = h * HEAD_CHUNKS
                for g, (pair, free, used, tall) in enumerate((
                        (pair_a, a_free, h * 3 + 1, True), (pair_b, b_free, h * 2 + 1, True),
                        (pair_a, a_free, h * 3 + 2, False), (pair_b, b_free, h * 2 + 2, True),
                        (pair_a, a_free, h * 3 + 3, False))):
                    pe.wait_ge(free, used)
                    for i in range(4):
                        if first and g == 0:
                            pe.wait_ge(h_done, 2 * (i // 2) + 2)
                        use_chunk(4 * g + i, c + (4 * g + i), i, 4, pair, h_hi, h_lo, tall)
                        if not first:
                            tail(4 * g + i, h)
                        elif g == 0 and i == 2:
                            pe.wait_ge(squares_added, 4)
                            for k in range(2):
                                last = mm(p4[:, 0, 0:T], ones[:], x_sq[:, k, :], start=(k == 0), stop=(k == 1))
                            last.then_inc(sumsq_done, 1)
                        attend(4 * g + i, h)

            head(0, first=True)
            with pe.Fori(1, H) as h:
                head(h)

            def merge_two(it, first=False):
                for u in range(2):
                    c = it * (2 * MERGE_CHUNKS) + (C_MERGE + u * MERGE_CHUNKS)
                    k = u * MERGE_CHUNKS
                    use = it * 2 + u
                    pe.wait_ge(a_free, use + (A_MERGE + 1))
                    for i in range(4):
                        use_chunk(k + i, c + i, i, 4, pair_a, h_hi, h_lo, False)
                        if first and u == 0:
                            tail(i, H)
                    pe.wait_ge(b_free, use + (B_MERGE + 1))
                    group(k + 4, c + 4, 4, pair_b, h_hi, h_lo)
                    if first and u == 0:
                        pe.wait_ge(p4_free, N4 * H + 1)
                        pe.wait_ge(p56_free, N56 * H + 1)
                        pe.wait_ge(p7_free, N7 * H + 1)
                    pe.wait_ge(c_free, use + 1)
                    group(k + 8, c + 8, 4, pC, ro_hi, ro_lo, ready=(o_split, 4) if first and u == 0 else None)
                    pe.wait_ge(d_free, use + 1)
                    if first and u == 0:
                        pe.wait_ge(o_split, 6)
                    group(k + 12, c + 12, 2, pD, ho_hi, ho_lo)

            merge_two(0, first=True)
            with pe.Fori(1, 4) as it:
                merge_two(it)
            with pe.Fori(0, 4) as it:
                pe.wait_ge(a_free, it + (A_WOUT + 1))
                group(0, it * 8 + C_WOUT, 4, pair_a, m_hi, m_lo, ready=(m_done, 2))
                pe.wait_ge(b_free, it + (B_WOUT + 1))
                group(4, it * 8 + (C_WOUT + 4), 4, pair_b, m_hi, m_lo)

            def total_squares():
                mm(p4[:, 0, 0:T], ones[:], sq_sum[:, 0, :], start=True, stop=False)
                mm(p4[:, 0, 0:T], ones[:], sq_sum[:, 1, :], start=False, stop=True).then_inc(sumsq_done, 1)

            def gate_pair(j, first=False):
                pe.wait_ge(a_free, j + (A_FIN + 1))
                group(0, j * 8 + C_FIN, 4, pair_a, h2_hi, h2_lo, ready=(h2_done, 2) if first else None)
                if first:
                    pe.wait_ge(res_step, 1 + 16)
                    total_squares()
                pe.wait_ge(b_free, j + (B_FIN + 1))
                group(4, j * 8 + (C_FIN + 4), 4, pair_b, h2_hi, h2_lo)

            gate_pair(0, first=True)
            with pe.Fori(1, FT // 2) as j:
                gate_pair(j)
            with pe.Fori(0, 2) as it:
                for g in range(4):
                    pair, free, used = ((pair_a, a_free, A_FOUT), (pair_b, b_free, B_FOUT))[g % 2]
                    pe.wait_ge(free, it * 2 + (used + g // 2 + 1))
                    group(g * OUT_CHUNKS, it * (4 * OUT_CHUNKS) + (C_FOUT + g * OUT_CHUNKS), OUT_CHUNKS, pair,
                          hid_hi, hid_lo, ready=(hid_done, 2) if g == 0 else None)
            pe.wait_ge(res_step, 18 + 14)
            mm(p4[:, 0, 0:T], ones[:], sq_sum[:, 0, :], start=True, stop=False)
            mm(p4[:, 0, 0:T], ones[:], sq_sum[:, 1, :], start=False, stop=False)
            pe.wait_ge(res_step, 18 + 15)
            mm(p4[:, 0, 0:T], ones[:], sq[:, 0, :], start=False, stop=False)
            mm(p4[:, 0, 0:T], ones[:], sq[:, 1, :], start=False, stop=True).then_inc(sumsq_done, 1)


def constants(np):
    half = DK // 2
    inv_freq = (np.float32(10000.0) ** (-np.arange(half, dtype=np.float32) / np.float32(half))).astype(np.float32)
    pos = np.concatenate([np.arange(NP), np.full(NS, 2048)]).astype(np.float32)
    ang = (pos[None, :] * inv_freq[:, None]).astype(np.float32).astype(np.float64)
    cos = np.concatenate([np.cos(ang), np.cos(ang)])
    sin = np.concatenate([-np.sin(ang), np.sin(ang)])
    scale = DK ** -0.5
    rope = np.stack([cos, sin, cos * scale, sin * scale], axis=1).reshape(P, 4 * T)
    gamma = 1.0 - 2.0 ** (-5.0 - np.arange(H, dtype=np.float64))
    m, n = np.arange(P)[:, None], np.arange(NP)[None, :]
    mask = np.where(n >= m, gamma[:, None, None] ** np.maximum(n - m, 0), 0.0)
    j = np.arange(64)[None, :]
    level = []
    for i in range(NLEV):
        s = 1 << i
        n_of = (j // s) * 2 * s + s + j % s
        level.append((m // (2 * s) == n_of // (2 * s)) & (m % (2 * s) < s))
    kdec = gamma[None, None, :] ** (NP - 1 - (np.arange(2)[None, :, None] * P + np.arange(P)[:, None, None]))
    c = np.zeros((P, K_SIZE), np.float32)
    c[:, K_ROPE:K_ROPE + 4 * T] = rope
    c[:, K_MASK:K_MASK + H * NP] = mask.transpose(1, 0, 2).reshape(P, H * NP)
    c[:, K_LEVEL:K_LEVEL + NLEV * 64] = np.concatenate(level, axis=1)
    c[:, K_IDENT:K_IDENT + P] = np.eye(P)
    c[:, K_KDEC:K_KDEC + 2 * H] = kdec.reshape(P, 2 * H)
    c[:, K_GAMMA:K_GAMMA + H] = gamma[None, :]
    c[:, K_EYE8:K_EYE8 + NS * NS] = np.eye(NS).reshape(1, NS * NS)
    c[:, K_ROW8:K_ROW8 + NS] = np.tile(np.eye(NS), (P // NS, 1))
    return c


def kernel(**inputs):
    import numpy as np
    import concourse.bacc as bacc
    from concourse.bass_utils import run_bass_kernel_spmd

    a = {k: np.asarray(v) for k, v in inputs.items()}

    def tiled(v):
        return v.reshape(-1, P).T

    tokens = np.concatenate([a["x_prompt"][0], a["x_sample"][:, 0]], axis=0)
    arrays = {
        "consts": constants(np),
        "vectors": np.ascontiguousarray(np.concatenate(
            [tiled(a["norm_mix"][0]), tiled(a["norm_ffn"][0]), tiled(a["norm_final"]), tiled(a["hgrn_norm"][0]),
             tiled(a["hgrn_lb_logits"].reshape(-1))], axis=1)),
        "xT": np.ascontiguousarray(tokens.T.reshape(KT, P, T).transpose(1, 0, 2)),
        "w_in": a["w_in"][0], "w_ret": a["w_ret_out"][0], "w_hg": a["w_hgrn_out"][0], "w_out": a["w_out"][0],
        "w_fin": a["w_ffn_in"][0], "w_fout": a["w_ffn_out"][0],
        "s_ret": a["state_ret"][0], "s_hg": a["state_hgrn"][0],
    }
    outs = {"yT": (P, KT, T), "ret_p": (H, DK, RV), "hg_p": (H, DK, HV),
            "ret_s": (NS, H, DK, RV), "hg_s": (NS, H, DK, HV)}
    nc = bacc.Bacc("TRN2", target_bir_lowering=False, num_devices=1)
    aps = [nc.dram_tensor(f"in_{n}", v.shape, F32, kind="ExternalInput").ap() for n, v in arrays.items()]
    aps += [nc.dram_tensor(f"out_{n}", s, F32, kind="ExternalOutput").ap() for n, s in outs.items()]
    build(nc, *aps)
    r = run_bass_kernel_spmd(nc, [{f"in_{n}": np.ascontiguousarray(v) for n, v in arrays.items()}], core_ids=[0])
    got = {n: r.results[0][f"out_{n}"] for n in outs}
    y = got["yT"].transpose(1, 0, 2).reshape(D, T).T
    return (np.ascontiguousarray(y[:NP])[None], np.ascontiguousarray(y[NP:])[:, None],
            got["ret_p"][None, None], got["hg_p"][None, None], got["ret_s"][None], got["hg_s"][None])
```
